# Optimizing a Trainium2 kernel written in Bass

```python
import jax, jax.numpy as jnp
from jax import lax
import numpy as np
import math

D_MODEL = 1024
BATCH = 1
SEQ = 512
DEPTH = 1

SSM_HEADDIM = 64
SSM_HEADS = 16
SSM_INNER = SSM_HEADS * SSM_HEADDIM
SSM_GROUPS = 2
SSM_HPG = SSM_HEADS // SSM_GROUPS
SSM_STATE = 64
CONV_K = 4
CHUNK = 128
CONV_DIM = SSM_INNER + 2 * SSM_GROUPS * SSM_STATE

ATT_HEADS = 8
ATT_HEADDIM = 128
ATT_INNER = ATT_HEADS * ATT_HEADDIM
Q_BLOCK = 128

N_BRANCHES = 2
EPS = 1e-6

IN_SPLITS = (SSM_INNER, CONV_DIM, SSM_HEADS, ATT_INNER, ATT_INNER, ATT_INNER, ATT_INNER, ATT_HEADS, N_BRANCHES * D_MODEL)
IN_COLS = int(sum(IN_SPLITS))


def _rmsnorm(x, w):
    xf = x.astype(jnp.float32)
    y = xf * lax.rsqrt(jnp.mean(xf * xf, axis=-1, keepdims=True) + EPS)
    return (y * w.astype(jnp.float32)).astype(x.dtype)

def _causal_depthwise_conv(u, w, b):
    ch = u.shape[-1]
    out = lax.conv_general_dilated(
        u, w[:, None, :].astype(u.dtype), window_strides=(1,), padding=[(CONV_K - 1, 0)],
        dimension_numbers=("NWC", "WIO", "NWC"), feature_group_count=ch)
    return out + b.astype(u.dtype)

def _ssd_branch(z, xbc, dt_raw, conv_w, conv_b, dt_bias, a_log, d_skip, ssm_norm_w):
    bsz, s, _ = xbc.shape
    g, r, p, n = SSM_GROUPS, SSM_HPG, SSM_HEADDIM, SSM_STATE
    nc = s // CHUNK
    xbc = jax.nn.silu(_causal_depthwise_conv(xbc, conv_w, conv_b))
    xs, bm, cm = jnp.split(xbc, [SSM_INNER, SSM_INNER + g * n], axis=-1)
    xs = xs.reshape(bsz, s, g, r, p)
    dt = jax.nn.softplus(dt_raw.astype(jnp.float32) + dt_bias.astype(jnp.float32)).reshape(bsz, s, g, r)
    a = dt * (-jnp.exp(a_log.astype(jnp.float32))).reshape(g, r)
    xdt = xs.astype(jnp.float32) * dt[..., None]
    xc = xdt.reshape(bsz, nc, CHUNK, g, r, p)
    bc = bm.astype(jnp.float32).reshape(bsz, nc, CHUNK, g, n)
    cc = cm.astype(jnp.float32).reshape(bsz, nc, CHUNK, g, n)
    ac = a.reshape(bsz, nc, CHUNK, g, r).transpose(0, 3, 4, 1, 2)
    a_cs = jnp.cumsum(ac, axis=-1)
    tril = jnp.tril(jnp.ones((CHUNK, CHUNK), dtype=bool))
    seg = a_cs[..., :, None] - a_cs[..., None, :]
    lmat = jnp.exp(jnp.where(tril, seg, -jnp.inf))
    cb = jnp.einsum("bclgn,bcsgn->bgcls", cc, bc)
    y_diag = jnp.einsum("bgrcls,bcsgrp->bclgrp", cb[:, :, None] * lmat, xc)
    decay_states = jnp.exp(a_cs[..., -1:] - a_cs)
    states = jnp.einsum("bclgn,bgrcl,bclgrp->bcgrpn", bc, decay_states, xc)
    states = jnp.concatenate([jnp.zeros_like(states[:, :1]), states], axis=1)
    cs = jnp.cumsum(jnp.pad(a_cs[..., -1], ((0, 0), (0, 0), (0, 0), (1, 0))), axis=-1)
    tril_c = jnp.tril(jnp.ones((nc + 1, nc + 1), dtype=bool))
    decay_chunk = jnp.exp(jnp.where(tril_c, cs[..., :, None] - cs[..., None, :], -jnp.inf))
    new_states = jnp.einsum("bgrzc,bcgrpn->bzgrpn", decay_chunk, states)
    prev_states = new_states[:, :-1]
    y_off = jnp.einsum("bclgn,bcgrpn,bgrcl->bclgrp", cc, prev_states, jnp.exp(a_cs))
    y = (y_diag + y_off).reshape(bsz, s, g, r, p) + d_skip.astype(jnp.float32).reshape(g, r)[..., None] * xs.astype(jnp.float32)
    y = y.reshape(bsz, s, SSM_INNER).astype(z.dtype)
    return _rmsnorm(y * jax.nn.silu(z), ssm_norm_w)

def _fox_branch(q, k, v, z, f_logit, b_f):
    bsz, s, _ = q.shape
    nb = s // Q_BLOCK
    q = q.reshape(bsz, s, ATT_HEADS, ATT_HEADDIM).transpose(0, 2, 1, 3)
    k = k.reshape(bsz, s, ATT_HEADS, ATT_HEADDIM).transpose(0, 2, 1, 3)
    v = v.reshape(bsz, s, ATT_HEADS, ATT_HEADDIM).transpose(0, 2, 1, 3)
    log_f = jax.nn.log_sigmoid(f_logit.astype(jnp.float32) + b_f.astype(jnp.float32))
    f_cum = jnp.cumsum(log_f, axis=1).transpose(0, 2, 1)
    scale = ATT_HEADDIM ** -0.5
    qb = q.reshape(bsz, ATT_HEADS, nb, Q_BLOCK, ATT_HEADDIM).transpose(2, 0, 1, 3, 4)
    fq = f_cum.reshape(bsz, ATT_HEADS, nb, Q_BLOCK).transpose(2, 0, 1, 3)
    qpos = jnp.arange(s, dtype=jnp.int32).reshape(nb, Q_BLOCK)
    kpos = jnp.arange(s, dtype=jnp.int32)

    def one_block(args):
        qi, fi, pi = args
        logits = jnp.einsum("bhqd,bhkd->bhqk", qi, k).astype(jnp.float32) * scale
        logits = logits + fi[..., :, None] - f_cum[..., None, :]
        logits = jnp.where(pi[:, None] >= kpos[None, :], logits, -jnp.inf)
        probs = jax.nn.softmax(logits, axis=-1).astype(v.dtype)
        return jnp.einsum("bhqk,bhkd->bhqd", probs, v)

    o = lax.map(one_block, (qb, fq, qpos))
    o = o.transpose(1, 0, 3, 2, 4).reshape(bsz, s, ATT_INNER)
    return o * jax.nn.silu(z)

def first_inputs(seed: int = 0) -> dict:
    key = jax.random.key(seed)
    ks = jax.random.split(key, 20)
    d = D_MODEL
    x = jax.random.normal(ks[0], (BATCH, SEQ, d), jnp.float32)
    c = jax.random.normal(ks[1], (BATCH, d), jnp.float32)
    w_ada = jax.random.normal(ks[2], (d, 3 * d), jnp.float32) * d ** -0.5 * 0.5
    b_ada = jax.random.normal(ks[3], (3 * d,), jnp.float32) * 0.01
    norm_w = 1.0 + 0.05 * jax.random.normal(ks[4], (d,), jnp.float32)
    w_in = jax.random.normal(ks[5], (d, IN_COLS), jnp.float32) * d ** -0.5
    conv_w = jax.random.normal(ks[6], (CONV_K, CONV_DIM), jnp.float32) * 0.5
    conv_b = jax.random.normal(ks[7], (CONV_DIM,), jnp.float32) * 0.02
    dt0 = jnp.exp(jax.random.uniform(ks[8], (SSM_HEADS,), jnp.float32, np.log(1e-3), np.log(1e-1)))
    dt_bias = dt0 + jnp.log(-jnp.expm1(-dt0))
    a_log = jnp.log(jax.random.uniform(ks[9], (SSM_HEADS,), jnp.float32, 1.0, 16.0))
    d_skip = 1.0 + 0.1 * jax.random.normal(ks[10], (SSM_HEADS,), jnp.float32)
    ssm_norm_w = 1.0 + 0.05 * jax.random.normal(ks[11], (SSM_INNER,), jnp.float32)
    b_f = jnp.linspace(1.0, 6.0, ATT_HEADS, dtype=jnp.float32) + 0.1 * jax.random.normal(ks[12], (ATT_HEADS,), jnp.float32)
    b_gate = jax.random.normal(ks[13], (N_BRANCHES * d,), jnp.float32) * 0.01
    w_proj_ssm = jax.random.normal(ks[14], (SSM_INNER, d), jnp.float32) * SSM_INNER ** -0.5
    w_proj_att = jax.random.normal(ks[15], (ATT_INNER, d), jnp.float32) * ATT_INNER ** -0.5
    w_out = jax.random.normal(ks[16], (d, d), jnp.float32) * d ** -0.5
    final_norm_w = 1.0 + 0.05 * jax.random.normal(ks[17], (d,), jnp.float32)
    return {"x": x, "c": c, "w_ada": w_ada, "b_ada": b_ada, "norm_w": norm_w, "w_in": w_in,
            "conv_w": conv_w, "conv_b": conv_b, "dt_bias": dt_bias, "a_log": a_log, "d_skip": d_skip,
            "ssm_norm_w": ssm_norm_w, "b_f": b_f, "b_gate": b_gate, "w_proj_ssm": w_proj_ssm,
            "w_proj_att": w_proj_att, "w_out": w_out, "final_norm_w": final_norm_w}

def first_block(x, c, w_ada, b_ada, norm_w, w_in, conv_w, conv_b, dt_bias, a_log, d_skip,
              ssm_norm_w, b_f, b_gate, w_proj_ssm, w_proj_att, w_out, final_norm_w):
    ada = jax.nn.silu(c) @ w_ada + b_ada
    shift, scale, gate = jnp.split(ada, 3, axis=-1)
    offsets = [int(o) for o in np.cumsum(IN_SPLITS)[:-1]]
    for _ in range(DEPTH):
        h = _rmsnorm(x, norm_w) * (1.0 + scale[:, None, :]) + shift[:, None, :]
        proj = jnp.einsum("bsd,de->bse", h, w_in)
        z_ssm, xbc, dt_raw, q, k, v, z_att, f_logit, g_logit = jnp.split(proj, offsets, axis=-1)
        y_ssm = _ssd_branch(z_ssm, xbc, dt_raw, conv_w, conv_b, dt_bias, a_log, d_skip, ssm_norm_w)
        y_att = _fox_branch(q, k, v, z_att, f_logit, b_f)
        g_ssm, g_att = jnp.split(jax.nn.sigmoid(g_logit + b_gate), N_BRANCHES, axis=-1)
        merged = g_ssm * jnp.einsum("bse,ed->bsd", y_ssm, w_proj_ssm) + g_att * jnp.einsum("bse,ed->bsd", y_att, w_proj_att)
        x = x + gate[:, None, :] * jnp.einsum("bsd,de->bse", merged, w_out)
    return _rmsnorm(x, final_norm_w)


DEPTH_2 = 2

N_A = DEPTH_2 // 2
N_B = DEPTH_2 - N_A
N_HEADS = 16
HEAD_DIM = D_MODEL // N_HEADS
CONV_W = 31
FFN_DIM = 2816
FFN_CONV_W = 3
PLE_DIM = 256
LN_EPS = 1e-5
DN_ALPHA = (2.0 * DEPTH_2) ** 0.25
DN_BETA = (8.0 * DEPTH_2) ** -0.25


def layer_norm(x, g, b):
    xf = x.astype(jnp.float32)
    mu = jnp.mean(xf, axis=-1, keepdims=True)
    var = jnp.mean(jnp.square(xf - mu), axis=-1, keepdims=True)
    y = (xf - mu) * lax.rsqrt(var + LN_EPS)
    return (y * g.astype(jnp.float32) + b.astype(jnp.float32)).astype(x.dtype)

def causal_dwconv(x, w, b):
    k = w.shape[0]
    y = lax.conv_general_dilated(
        x, w[:, None, :].astype(x.dtype), window_strides=(1,), padding=[(k - 1, 0)],
        dimension_numbers=("NWC", "WIO", "NWC"), feature_group_count=x.shape[-1])
    return y + b

def conformer_conv(x, pw1_w, pw1_b, dw_w, dw_b, ln_g, ln_b, pw2_w, pw2_b):
    h = x @ pw1_w + pw1_b
    a, g = jnp.split(h, 2, axis=-1)
    h = a * jax.nn.sigmoid(g)
    h = causal_dwconv(h, dw_w, dw_b)
    h = layer_norm(h, ln_g, ln_b)
    h = jax.nn.silu(h)
    return h @ pw2_w + pw2_b

def stick_breaking_attention(q, k, v):
    b, s, h, dh = q.shape
    nb = s // Q_BLOCK
    scale = 1.0 / math.sqrt(dh)
    kh = jnp.transpose(k, (0, 2, 1, 3))
    vh = jnp.transpose(v, (0, 2, 1, 3))
    qb = jnp.transpose(q.reshape(b, nb, Q_BLOCK, h, dh), (1, 0, 3, 2, 4))
    t0s = jnp.arange(nb, dtype=jnp.int32) * Q_BLOCK
    ts = jnp.arange(s, dtype=jnp.int32)

    def block(args):
        qblk, t0 = args
        z = jnp.einsum('bhqd,bhkd->bhqk', qblk, kh).astype(jnp.float32) * scale
        tq = t0 + jnp.arange(Q_BLOCK, dtype=jnp.int32)
        mask = ts[None, :] < tq[:, None]
        log_1m = jnp.where(mask, jax.nn.log_sigmoid(-z), 0.0)
        rev = lax.cumsum(log_1m, axis=3, reverse=True)
        log_a = jax.nn.log_sigmoid(z) + (rev - log_1m)
        a = jnp.where(mask, jnp.exp(log_a), 0.0)
        return jnp.einsum('bhqk,bhkd->bhqd', a.astype(vh.dtype), vh)

    out = lax.map(block, (qb, t0s))
    return jnp.transpose(out, (1, 0, 3, 2, 4)).reshape(b, s, h * dh)

def conv_gated_ffn(x, w_up, w_gate, conv_w, conv_b, w_down):
    u = x @ w_up
    g = causal_dwconv(x @ w_gate, conv_w, conv_b)
    return (jax.nn.silu(g) * u) @ w_down

def second_inputs(seed: int = 0) -> dict:
    key = jax.random.key(seed)
    ks = jax.random.split(key, 32)
    D, F = D_MODEL, FFN_DIM

    def nrm(k, shape, scale):
        return jax.random.normal(k, shape, jnp.float32) * scale

    return {
        "x": nrm(ks[0], (BATCH, SEQ, D), 1.0),
        "p": nrm(ks[1], (DEPTH_2, BATCH, SEQ, PLE_DIM), 1.0),
        "a_pw1_w": nrm(ks[2], (N_A, D, 2 * D), D ** -0.5),
        "a_pw1_b": nrm(ks[3], (N_A, 2 * D), 0.02),
        "a_dw_w": nrm(ks[4], (N_A, CONV_W, D), CONV_W ** -0.5),
        "a_dw_b": nrm(ks[5], (N_A, D), 0.02),
        "a_ln_g": 1.0 + nrm(ks[6], (N_A, D), 0.02),
        "a_ln_b": nrm(ks[7], (N_A, D), 0.02),
        "a_pw2_w": nrm(ks[8], (N_A, D, D), D ** -0.5 * DN_BETA),
        "a_pw2_b": nrm(ks[9], (N_A, D), 0.02),
        "b_wq": nrm(ks[10], (N_B, D, D), D ** -0.5),
        "kv_wk": nrm(ks[11], (D, D), D ** -0.5),
        "kv_wv": nrm(ks[12], (D, D), D ** -0.5 * DN_BETA),
        "b_wo": nrm(ks[13], (N_B, D, D), D ** -0.5 * DN_BETA),
        "ln_mix_g": 1.0 + nrm(ks[14], (DEPTH_2, D), 0.02),
        "ln_mix_b": nrm(ks[15], (DEPTH_2, D), 0.02),
        "ffn_w_up": nrm(ks[16], (DEPTH_2, D, F), D ** -0.5),
        "ffn_w_gate": nrm(ks[17], (DEPTH_2, D, F), D ** -0.5),
        "ffn_conv_w": nrm(ks[18], (DEPTH_2, FFN_CONV_W, F), FFN_CONV_W ** -0.5),
        "ffn_conv_b": nrm(ks[19], (DEPTH_2, F), 0.02),
        "ffn_w_down": nrm(ks[20], (DEPTH_2, F, D), F ** -0.5 * DN_BETA),
        "ple_w_gate": nrm(ks[21], (DEPTH_2, D, D), D ** -0.5),
        "ple_w_proj": nrm(ks[22], (DEPTH_2, PLE_DIM, D), PLE_DIM ** -0.5 * DN_BETA),
        "ln_ffn_g": 1.0 + nrm(ks[23], (DEPTH_2, D), 0.02),
        "ln_ffn_b": nrm(ks[24], (DEPTH_2, D), 0.02),
    }

def second_block(x, p, a_pw1_w, a_pw1_b, a_dw_w, a_dw_b, a_ln_g, a_ln_b, a_pw2_w, a_pw2_b,
              b_wq, kv_wk, kv_wv, b_wo, ln_mix_g, ln_mix_b,
              ffn_w_up, ffn_w_gate, ffn_conv_w, ffn_conv_b, ffn_w_down,
              ple_w_gate, ple_w_proj, ln_ffn_g, ln_ffn_b):
    b, s, d = x.shape
    k_shared = None
    v_shared = None
    for i in range(DEPTH_2):
        if i < N_A:
            mix = conformer_conv(x, a_pw1_w[i], a_pw1_b[i], a_dw_w[i], a_dw_b[i],
                                 a_ln_g[i], a_ln_b[i], a_pw2_w[i], a_pw2_b[i])
        else:
            j = i - N_A
            if k_shared is None:
                k_shared = (x @ kv_wk).reshape(b, s, N_HEADS, HEAD_DIM)
                v_shared = (x @ kv_wv).reshape(b, s, N_HEADS, HEAD_DIM)
            q = (x @ b_wq[j]).reshape(b, s, N_HEADS, HEAD_DIM)
            mix = stick_breaking_attention(q, k_shared, v_shared) @ b_wo[j]
        x = layer_norm(DN_ALPHA * x + mix, ln_mix_g[i], ln_mix_b[i])
        ffn = conv_gated_ffn(x, ffn_w_up[i], ffn_w_gate[i], ffn_conv_w[i], ffn_conv_b[i], ffn_w_down[i])
        ple = jax.nn.sigmoid(x @ ple_w_gate[i]) * (p[i] @ ple_w_proj[i])
        x = layer_norm(DN_ALPHA * x + ffn + ple, ln_ffn_g[i], ln_ffn_b[i])
    return x


def setup_inputs(seed=0):
    out = dict(first_inputs(seed))
    for name, value in second_inputs(seed + 1).items():
        if name != "x":
            out[name + "_2"] = value
    return out


def reference(
    x, c, w_ada, b_ada, norm_w, w_in, conv_w, conv_b, dt_bias, a_log, d_skip, ssm_norm_w, b_f,
    b_gate, w_proj_ssm, w_proj_att, w_out, final_norm_w, p_2, a_pw1_w_2, a_pw1_b_2, a_dw_w_2,
    a_dw_b_2, a_ln_g_2, a_ln_b_2, a_pw2_w_2, a_pw2_b_2, b_wq_2, kv_wk_2, kv_wv_2, b_wo_2,
    ln_mix_g_2, ln_mix_b_2, ffn_w_up_2, ffn_w_gate_2, ffn_conv_w_2, ffn_conv_b_2, ffn_w_down_2,
    ple_w_gate_2, ple_w_proj_2, ln_ffn_g_2, ln_ffn_b_2,
):
    x = first_block(
        x, c, w_ada, b_ada, norm_w, w_in, conv_w, conv_b, dt_bias, a_log, d_skip, ssm_norm_w,
        b_f, b_gate, w_proj_ssm, w_proj_att, w_out, final_norm_w,
    )
    return second_block(
        x, p_2, a_pw1_w_2, a_pw1_b_2, a_dw_w_2, a_dw_b_2, a_ln_g_2, a_ln_b_2, a_pw2_w_2,
        a_pw2_b_2, b_wq_2, kv_wk_2, kv_wv_2, b_wo_2, ln_mix_g_2, ln_mix_b_2, ffn_w_up_2,
        ffn_w_gate_2, ffn_conv_w_2, ffn_conv_b_2, ffn_w_down_2, ple_w_gate_2, ple_w_proj_2,
        ln_ffn_g_2, ln_ffn_b_2,
    )


_drawn_inputs = setup_inputs


def setup_inputs(seed=0):
    import zlib

    import numpy as np

    out = dict(_drawn_inputs(seed))
    spreads = {}
    factors = {'b_ada': 8.0,
     'norm_w': 4.372,
     'conv_b': 25.32,
     'd_skip': 200.0,
     'ssm_norm_w': 6.897,
     'b_gate': 29.973,
     'a_pw1_b_2': 8.0,
     'a_dw_b_2': 6.556,
     'a_ln_g_2': 75.281,
     'a_ln_b_2': 70.806,
     'a_pw2_b_2': 24.338,
     'ffn_conv_b_2': 8.0}
    for name, (base, spread) in spreads.items():
        noise = np.random.default_rng([zlib.crc32(name.encode()), seed]).standard_normal(out[name].shape)
        drawn = base * np.exp(spread * noise) if base else spread * noise
        out[name] = __import__('jax').numpy.asarray(drawn.astype(out[name].dtype))
    for name, factor in factors.items():
        out[name] = (out[name] * factor).astype(out[name].dtype)
    return out
```

```python
from contextlib import ExitStack

import numpy as np

import concourse.bass as bass
from concourse import mybir

F32 = mybir.dt.float32
F32R = mybir.dt.float32r
BF16 = mybir.dt.bfloat16
ACT = mybir.ActivationFunctionType
ALU = mybir.AluOpType
AX_X = mybir.AxisListType.X

P = 128
D = 1024
T = 512
KC = D // P
NT = T // P
SSM_HEADS, SSM_P, SSM_N, SSM_GROUPS = 16, 64, 64, 2
SSM_INNER = SSM_HEADS * SSM_P
HPG = SSM_HEADS // SSM_GROUPS
CONV_K = 4
XBC = SSM_INNER + 2 * SSM_GROUPS * SSM_N
XBC_C = XBC // P
FOX_HEADS = 8
SB_HEADS, SB_DIM = 16, 64
DW_K = 31
PAD = DW_K - 1
FFN = 2816
FC = FFN // P
FCONV_K = 3
PLE = 256
PC = PLE // P
LN_EPS, RMS_EPS = 1e-5, 1e-6
ALPHA = float((2.0 * 2) ** 0.25)
NEG = -1e30
HALF_ULP = 2.0 ** -24

Z0 = 0
XBC0 = Z0 + SSM_INNER
DT0 = XBC0 + XBC
Q0 = DT0 + SSM_HEADS
K0 = Q0 + D
V0 = K0 + D
ZA0 = V0 + D
FL0 = ZA0 + D
G0 = FL0 + FOX_HEADS
SMALL = 32 + FOX_HEADS

DOWN_S = 3
STAGES = [("xbc", XBC_C // 2), ("z", 4), ("ssm_out", 8), ("q", 4), ("k", 4), ("v", 4), ("za", 4), ("att_out", 8),
          ("w_out", 4), ("pw1", 8), ("pw2", 4), ("gate0", 4), ("up0", FC), ("down0", 4 * DOWN_S),
          ("q1", 4), ("k1", 4), ("v1", 4), ("wo", 4), ("gate1", 4), ("up1", FC), ("down1", 4 * DOWN_S)]
SLOT0, GROUP0 = {}, {}
_g = _b = 0
for _name, _n in STAGES:
    SLOT0[_name], GROUP0[_name] = _g, _b
    _g += _n
    _b += _n // DOWN_S if _name.startswith("down") else _n
NSLOTS = _g
COUNT = dict(STAGES)

PCOL, _c = {}, 0
for _name, _n in [("c", KC), ("norm_w", KC), ("b_ada", 3 * KC), ("conv_w", CONV_K * XBC_C), ("conv_b", XBC_C),
                  ("d_skip", KC), ("ssm_norm_w", KC), ("b_gate", 2 * KC), ("final_norm_w", KC), ("pw1_b", 2 * KC),
                  ("dw_w", DW_K * KC), ("dw_b", KC), ("ln_g", KC), ("ln_b", KC), ("pw2_b", KC), ("mix_g", 2 * KC),
                  ("mix_b", 2 * KC), ("fconv_w", 2 * FCONV_K * FC), ("fconv_b", 2 * FC), ("out_g", 2 * KC),
                  ("out_b", 2 * KC), ("small_b", 1), ("a_log", 1)]:
    PCOL[_name] = _c
    _c += _n
NPAR = _c


class Step:

    def __init__(self, first, turn=0):
        self.first, self.turn = first, turn

    def val(self, mul=1, add=0):
        return mul * self.first + add + 2 * mul * self.turn

    def half(self, mul=1, add=0):
        return (mul * self.first + add) // 2 + mul * self.turn

    def odd(self, mul=1, add=0):
        return (mul * self.first + add) % 2


class Chain:

    def __init__(self, eng, sem):
        self.eng, self.sem, self.base, self.k = eng, sem, 0, 0

    def did(self, ins):
        ins.then_inc(self.sem, 1)
        self.k += 1

    def settle(self):
        self.eng.wait_ge(self.sem, self.base + self.k)


def steps(eng, chain, n, per, body, head=0, tail=0):
    tail += (n - head - tail) % 2
    begin = chain.base + chain.k if chain else 0

    def one(s):
        if chain:
            chain.base, chain.k = begin + s.val(per), 0
        body(s)
        assert not chain or chain.k == per, (chain.k, per)

    for i in range(head):
        one(Step(i))
    turns = (n - head - tail) // 2
    if turns > 0:
        with eng.Fori(0, turns) as t:
            for i in range(2):
                one(Step(head + i, t))
    for i in range(n - tail, n):
        one(Step(i))
    if chain:
        chain.base, chain.k = begin + per * n, 0


def build(nc, w, w_ada, w_small, w_ple, p_t, x_t, par, out):
    with ExitStack() as ctx:
        KB = 1024
        base = (nc.sbuf_base + 31) // 32 * 32

        def at(name, kb, shape, dt=F32):
            return nc.alloc_sbuf_tensor_at(name, shape, dt, offset=base + int(kb * KB))

        def sem(name):
            return ctx.enter_context(nc.semaphore(name))

        X = at("X", 0, [P, KC, T])
        H = at("H", 16, [P, KC, T], F32R)
        L = at("L", 32, [P, KC, T], F32R)
        RAW = at("RAW", 48, [P, 2, 16, P])
        WH = at("WH", 64, [P, 2, 16, P], F32R)
        WL = at("WL", 80, [P, 2, 16, P], F32R)
        A = 96
        TT = at("TT", 188, [P, 4, T])
        CS = at("CS", 196, [P, T])
        MISC = 198
        ADA = [at(f"ADA{k}", A + 12 * k if k < 7 else 32, [P, 3 * D]) for k in range(KC)]
        ADAS = at("ADAS", 16, [P, 3 * D])
        XN = at("XN", A + 36, [P, KC, T])
        XC = at("XC", A + 0, [P, XBC_C, T])
        CE = at("CE", A + 20, [P, HPG, T])
        XD = at("XD", A + 36, [P, NT, SSM_INNER])
        XDD = at("XDD", A + 52, [P, NT, SSM_INNER])
        ST = at("ST", A + 68, [P, 3, T])
        BTOK = at("BTOK", A + 74, [P, NT, P])
        CBM = at("CBM", A + 76, [P, 2, T])
        MT = at("MT", A + 80, [P, 2, T])
        SM = at("SM", A + 84, [P, 4, T])
        ZS = at("ZS", A + 36, [P, KC, T])
        YH = at("YH", A + 68, [P, KC, T], F32R)
        YL = at("YL", A + 20, [P, KC, T], F32R)
        P1 = at("P1", A + 36, [P, KC, T])
        QK = at("QK", A + 52, [P, 2 * KC, T])
        VT = at("VT", A + 20, [P, KC, T])
        VTOK = at("VTOK", A + 0, [P, NT, D])
        PT = at("PT", A + 84, [P, NT, T])
        ZA = at("ZA", A + 0, [P, KC, T])
        MH = at("MH", A + 0, [P, KC, T], F32R)
        ML = at("ML", A + 52, [P, KC, T], F32R)
        SBC = sum(T - P * k for k in range(NT))
        EX = [at(f"EX{i}", A + 36 + 5 * i, [P, SBC]) for i in range(2)]
        AT = [at("AT0", A + 46, [P, SBC]), at("AT1", A + 84, [P, SBC])]
        HC = at("HC", A + 0, [P, KC, PAD + T])
        CV = at("CV", A + 20, [P, KC, T])
        FH = at("FH", A + 0, [P, FC, T], F32R)
        FL = at("FL", A + 44, [P, FC, T], F32R)
        PPL = at("PPL", A + 88, [P, PC, T], F32R)
        PWR = at("PWR", A + 36, [P, PC, D])
        WPH = at("WPH", A + 44, [P, PC, D], F32R)
        WPL = at("WPL", A + 52, [P, PC, D], F32R)
        PR = at("PR", A + 60, [P, PC, T])
        PPH = at("PPH", A + 64, [P, PC, T], F32R)
        PAR = at("PAR", MISC, [P, NPAR])
        o = MISC + NPAR * 4 / KB
        o = int(o * 32 + 1) / 32

        def small(name, shape, dt=F32):
            nonlocal o
            t = at(name, o, shape, dt)
            n = int(np.prod(shape[1:])) * (2 if dt == BF16 else 4)
            o += (n + 31) // 32 * 32 / KB
            return t

        IDENT = small("IDENT", [P, P])
        TRI = small("TRI", [P, P])
        IDB = small("IDB", [P, P], BF16)
        M_FOX = small("M_FOX", [P, P], BF16)
        M_SB = small("M_SB", [P, P], BF16)
        M_SSM = small("M_SSM", [P, P], BF16)
        ADAV = small("ADAV", [P, 3 * KC])
        GX = small("GX", [P, KC])
        CSIL = small("CSIL", [P, KC])
        COLS = small("COLS", [P, 6])
        MEANC, ONEC, NEGC, EPS_LN, EPS_RMS, SGN = (COLS[:, i:i + 1] for i in range(6))
        STAT = small("STAT", [P, 3, NT * FOX_HEADS])
        TOK = small("TOK", [P, 3, NT, SSM_HEADS])
        EL = small("EL", [P, HPG, NT])
        AEXP = small("AEXP", [P, 1])
        assert base + o * KB <= nc.sbuf_usable_end, (o, (nc.sbuf_usable_end - base) / KB)
        SWR = at("SWR", A + 84, [P, KC, SMALL])
        SWH = at("SWH", A + 86, [P, KC, SMALL], F32R)
        SWL = at("SWL", A + 88, [P, KC, SMALL], F32R)

        PS = ctx.enter_context(nc.psum_tensor("PS", [P, 8, T], F32))
        NB, MB = PS[:, 4, :], PS[:, 5, :]

        def col(name, i=0, n=1):
            return PAR[:, PCOL[name] + i:PCOL[name] + i + n]

        def dcol(name, i):
            if isinstance(i, int):
                return col(name, i)
            return PAR[:, bass.ds(i + PCOL[name], 1)]

        def rows(t, i, n):
            return t[:, i:i + n, :] if isinstance(i, int) else t[:, bass.ds(i, n), :]

        par_in, x_in, sw_in, c_ready = sem("par_in"), sem("x_in"), sem("sw_in"), sem("c_ready")
        ada_in = [sem(f"ada_in{k}") for k in range(KC)]
        const_ready = sem("const_ready")
        act_own, dve_own, pool_own = sem("act_own"), sem("dve_own"), sem("pool_own")
        raw_in = [sem("raw_in0"), sem("raw_in1")]
        w_hi, w_lo = sem("w_hi"), sem("w_lo")
        slot_done = sem("slot_done")
        bank_free = sem("bank_free")
        sw_hi, sw_lo = sem("sw_hi"), sem("sw_lo")
        ada_sum, ada_ps, ada_ready = sem("ada_sum"), sem("ada_ps"), sem("ada_ready")
        sq_ready, sq_used, std_ready = sem("sq_ready"), sem("sq_used"), sem("std_ready")
        t_ready, hi_ready, h_ready = sem("t_ready"), sem("hi_ready"), sem("h_ready")
        sum_ready, mean_ready, cen_ready = sem("sum_ready"), sem("mean_ready"), sem("cen_ready")
        xc_ready = sem("xc_ready")
        dt_ps, dt_u, dt_e, dt_w, dt_l, dt_x, dt_d, dt_rows = (sem(s) for s in (
            "dt_ps", "dt_u", "dt_e", "dt_w", "dt_l", "dt_x", "dt_d", "dt_rows"))
        tok_ps, tok_ready, bt_ps, bt_ready, cb_ps, cb_ready = (sem(s) for s in (
            "tok_ps", "tok_ready", "bt_ps", "bt_ready", "cb_ps", "cb_ready"))
        xt_ps, xt_used, e_ps, e_exp, ce_ready, st_ps, st_ready = (sem(s) for s in (
            "xt_ps", "xt_used", "e_ps", "e_exp", "ce_ready", "st_ps", "st_ready"))
        seg_ps, seg_ready, seg_exp, mt_ready, y_ps, y_used = (sem(s) for s in (
            "seg_ps", "seg_ready", "seg_exp", "mt_ready", "y_ps", "y_used"))
        zs_ready, yz_ready = sem("zs_ready"), sem("yz_ready")
        sig_ready = sem("sig_ready")
        vt_ps, vtok_ready = sem("vt_ps"), sem("vtok_ready")
        lg_ready, nm_ready, p_exp, pn_ready, tr_ready, pt_ready, pv_done, ot_ready = (sem(s) for s in (
            "lg_ready", "nm_ready", "p_exp", "pn_ready", "tr_ready", "pt_ready", "pv_done", "ot_ready"))
        za_ready, ya_ready, ya_hi, ya_lo = (sem(s) for s in ("za_ready", "ya_ready", "ya_hi", "ya_lo"))
        mg_ready, mg_hi, mg_lo = sem("mg_ready"), sem("mg_hi"), sem("mg_lo")
        cv_ready = sem("cv_ready")
        ple_in, ple_hi, ple_lo, pg_ready = sem("ple_in"), sem("ple_hi"), sem("ple_lo"), sem("pg_ready")
        gc_ready, sl_ready, ff_hi, ff_lo = (sem(s) for s in ("gc_ready", "sl_ready", "ff_hi", "ff_lo"))
        sz_ps, sz_exp, sp_ready, tri_done, a_ready, sb_pv, so_ready = (sem(s) for s in (
            "sz_ps", "sz_exp", "sp_ready", "tri_done", "a_ready", "sb_pv", "so_ready"))
        so_hi, so_lo = sem("so_hi"), sem("so_lo")
        out_ready, out_done = sem("out_ready"), sem("out_done")

        N_X, N_SSM, N_FINAL, N_CONV, N_MIX0, N_OUT0, N_MIX1, N_OUT1 = range(8)
        LN_OF = {N_CONV: 0, N_MIX0: 1, N_OUT0: 2, N_MIX1: 3, N_OUT1: 4}
        SIG0, _n = {}, 0
        for s in ("ssm_out", "att_out", "pw1", "gate0", "gate1"):
            SIG0[s] = _n
            _n += COUNT[s]
        SB_OFF = {0: 0, 1: T, 3: T + 3 * P, 2: 2 * T}

        block = ctx.enter_context(nc.Block())

        @block.gpsimd
        def _(pool):
            own = Chain(pool, pool_own)
            own.did(nc.gpsimd.memset(IDENT[:], 0.0))
            own.did(nc.gpsimd.memset(IDB[:], 0.0))
            own.did(nc.gpsimd.memset(M_FOX[:], 0.0))
            own.did(nc.gpsimd.memset(M_SB[:], 0.0))
            own.did(nc.gpsimd.memset(M_SSM[:], 0.0))
            own.did(nc.gpsimd.memset(TRI[:], -1.0))
            for c, v in ((MEANC, 1.0 / D), (ONEC, 1.0), (NEGC, -1.0), (EPS_LN, LN_EPS), (EPS_RMS, RMS_EPS)):
                own.did(nc.gpsimd.memset(c, v))
            own.did(nc.gpsimd.memset(SGN[0:32], 1.0))
            own.settle()
            own.did(nc.gpsimd.memset(SGN[32:64], -1.0))
            own.settle()

            def select(t, op, fill, cm, step):
                nc.gpsimd.affine_select(out=t[:], in_=t[:], compare_op=op, fill=fill, base=0,
                                        pattern=[[step, P]], channel_multiplier=cm).then_inc(const_ready, 1)

            select(IDENT, ALU.not_equal, 1.0, 1, -1)
            select(IDB, ALU.not_equal, 1.0, 1, -1)
            select(M_FOX, ALU.is_ge, NEG, 1, -1)
            select(M_SB, ALU.is_gt, NEG, -1, 1)
            select(M_SSM, ALU.is_ge, NEG, -1, 1)
            select(TRI, ALU.is_ge, 0.0, 1, -1)

        @block.sync
        def _(sp):
            sp.dma_start(PAR[:], par).then_inc(par_in, 16)
            sp.dma_start(X[:], x_t).then_inc(x_in, 16)
            sp.dma_start(SWR[:], w_small).then_inc(sw_in, 16)
            for g in range(2):
                sp.dma_start(RAW[:, g], w[g]).then_inc(raw_in[g], 16)
            n = NSLOTS - 2
            with sp.Fori(0, n // 2) as t:
                for i in range(2):
                    sp.wait_ge(w_lo, 2 * t + i + 1)
                    sp.dma_start(RAW[:, i], w[2 * t + (i + 2)]).then_inc(raw_in[i], 16)
            if n % 2:
                sp.wait_ge(w_lo, n)
                sp.dma_start(RAW[:, 0], w[NSLOTS - 1]).then_inc(raw_in[0], 16)
            for m in range(KC):
                sp.wait_ge(out_ready, m + 1)
                sp.dma_start(out[:, m, :], X[:, m, :]).then_inc(out_done, 16)
            sp.wait_ge(out_done, 16 * KC)

        @block.tensor
        def _(pe):
            own = None

            def product(ps, wh, wl, xh, xl, start, stop):
                nc.tensor.matmul(ps, wh, xh, start=start, stop=False)
                nc.tensor.matmul(ps, wh, xl, start=False, stop=False)
                return nc.tensor.matmul(ps, wl, xh, start=False, stop=stop)

            def slot(s, stage, units, ready=None, last=True, mul=1, part=0, ks=KC, group=None):
                g0 = SLOT0[stage] + part
                p = s.odd(mul, g0)
                b = s.odd(1, GROUP0[stage])
                pe.wait_ge(w_lo, s.val(mul, g0 + 1))
                if part == 0 and not (isinstance(s.val(), int) and s.val(1, GROUP0[stage]) < 2):
                    pe.wait_ge(bank_free, s.val(1, GROUP0[stage] - 1))
                for k in range(ks):
                    if ready:
                        pe.wait_ge(ready[0], ready[1] + ready[2] * (k + 1))
                    for u, (xh, xl) in enumerate(units):
                        i = u * KC + k
                        mm = product(PS[:, 2 * b + u, :], WH[:, p, i, :], WL[:, p, i, :], xh[:, part * KC + k, :],
                                     xl[:, part * KC + k, :], part == 0 and k == 0, last and k == ks - 1)
                mm.then_inc(slot_done, 1)

            def gemm(stage, units, ready=None):
                def one(s):
                    first = isinstance(s.val(), int) and s.val() == 0
                    slot(s, stage, units, ready if first else None)
                steps(pe, None, COUNT[stage], 0, one, head=2 if stage == "xbc" else 1 if ready else 0)

            hl, ylh = (H, L), (YH, YL)

            def norm(n):
                for m in range(KC):
                    pe.wait_ge(sq_ready, KC * n + m + 1)
                    nc.tensor.matmul(NB, MEANC.to_broadcast([P, P]), TT[:, m % 2, :], start=m == 0,
                                     stop=m == KC - 1).then_inc(sq_used, 1)

            def mean(n):
                pe.wait_ge(sum_ready, LN_OF[n] + 1)
                nc.tensor.matmul(MB, MEANC.to_broadcast([P, P]), TT[:, 2, :], start=True,
                                 stop=True).then_inc(mean_ready, 1)

            pe.wait_ge(const_ready, 6)
            norm(N_X)
            pe.wait_ge(ada_sum, 1)
            for m in range(3 * KC):
                mm = nc.tensor.matmul(PS[:, 5, m:m + 1], ADAS[:, m * P:(m + 1) * P], ONEC, start=True, stop=True)
            mm.then_inc(ada_ps, 1)

            gemm("xbc", (hl, hl), (h_ready, KC * N_X, 1))
            pe.wait_ge(sw_lo, 1)
            for k in range(KC):
                mm = product(PS[0:SMALL, 4, :], SWH[:, k, :], SWL[:, k, :], H[:, k, :], L[:, k, :], k == 0, k == KC - 1)
            mm.then_inc(dt_ps, 1)

            def xt(i):
                c, half = divmod(i, 2)
                if i >= 2:
                    pe.wait_ge(xt_used, i - 1)
                for j in range(4):
                    mm = nc.tensor.transpose(PS[:, 6 + i % 2, j * P:(j + 1) * P],
                                             XC[:, 4 * half + j, c * P:(c + 1) * P], IDENT[:])
                mm.then_inc(xt_ps, 1)

            pe.wait_ge(xc_ready, COUNT["xbc"])
            xt(0)
            xt(1)
            pe.wait_ge(dt_u, 1)
            for c in range(NT):
                mm = nc.tensor.transpose(PS[:, 4, c * P:(c + 1) * P], XC[:, KC, c * P:(c + 1) * P], IDENT[:])
            mm.then_inc(bt_ps, 1)
            pe.wait_ge(dt_rows, 1)
            src = [CS, SM[:, 3, :], SM[:, 1, :]]
            for i in range(3):
                for c in range(NT):
                    j = (i * NT + c) * SSM_HEADS
                    mm = nc.tensor.transpose(PS[:, 5, j:j + SSM_HEADS], src[i][0:SSM_HEADS, c * P:(c + 1) * P],
                                             IDENT[0:SSM_HEADS, 0:SSM_HEADS])
            mm.then_inc(tok_ps, 1)
            for i in range(2, 2 * NT):
                xt(i)
            pe.wait_ge(bt_ready, 1)
            pe.wait_ge(tok_ready, 1)
            for g in range(SSM_GROUPS):
                r = slice(g * SSM_N, (g + 1) * SSM_N)
                for c in range(NT):
                    cc = slice(c * P, (c + 1) * P)
                    mm = nc.tensor.matmul(PS[:, 4 + g, cc], XC[r, KC, cc], XC[r, KC + 1, cc], start=True, stop=True)
                mm.then_inc(cb_ps, 1)
            for r in range(HPG):
                if r < 2:
                    pe.wait_ge(xt_used, 2 * NT - 1 + r)
                else:
                    pe.wait_ge(e_exp, r - 1)
                for g in range(SSM_GROUPS):
                    h = g * HPG + r
                    mm = nc.tensor.matmul(PS[g * 64:g * 64 + 64, 6 + r % 2, :],
                                          IDENT[0:SSM_HEADS, h:h + 1].to_broadcast([SSM_HEADS, 64]),
                                          CS[0:SSM_HEADS, :], start=True, stop=True)
                mm.then_inc(e_ps, 1)
            pe.wait_ge(cb_ready, 2)
            for c in range(NT - 1):
                if c:
                    pe.wait_ge(st_ready, c)
                for g in range(SSM_GROUPS):
                    mm = nc.tensor.matmul(PS[g * 64:g * 64 + 64, 5, :], BTOK[:, c, g * SSM_N:(g + 1) * SSM_N],
                                          XDD[:, c, g * T:(g + 1) * T], start=True, stop=True)
                mm.then_inc(st_ps, 1)

            def seg(h):
                if h < 2:
                    pe.wait_ge(e_exp, HPG - 1 + h)
                else:
                    pe.wait_ge(seg_ready, h - 1)
                ps = PS[:, 6 + h % 2, :]
                nc.tensor.matmul(ps, IDENT[0:SSM_HEADS, h:h + 1].to_broadcast([SSM_HEADS, P]), CS[0:SSM_HEADS, :],
                                 start=True, stop=False)
                nc.tensor.matmul(ps, IDB[:], M_SSM[:].unsqueeze(1).to_broadcast([P, NT, P]), start=False,
                                 stop=True).then_inc(seg_ps, 1)

            def y(h):
                i, u = divmod(h, 2)
                g, r = divmod(h, HPG)
                pe.wait_ge(mt_ready, h + 1)
                if u == 0 and i >= 2:
                    pe.wait_ge(y_used, i - 1)
                if h == 0:
                    pe.wait_ge(st_ready, NT - 1)
                    pe.wait_ge(ce_ready, HPG)
                for c in range(NT):
                    cc = slice(c * P, (c + 1) * P)
                    ps = PS[u * 64:u * 64 + 64, 4 + i % 2, cc]
                    mm = nc.tensor.matmul(ps, XD[:, c, h * 64:h * 64 + 64], MT[:, h % 2, cc], start=c == 0,
                                          stop=True, skip_group_check=True)
                    if c:
                        mm = nc.tensor.matmul(ps, ST[g * 64:g * 64 + 64, c - 1, r * 64:r * 64 + 64],
                                              CE[g * 64:g * 64 + 64, r, cc], start=False, stop=True,
                                              skip_group_check=True)
                mm.then_inc(y_ps, 1)

            seg(0)
            for h in range(SSM_HEADS):
                if h + 1 < SSM_HEADS:
                    seg(h + 1)
                y(h)
            gemm("z", (hl, hl))
            norm(N_SSM)
            gemm("ssm_out", (ylh, hl), (h_ready, KC * N_SSM, 1))
            for s in ("q", "k", "v"):
                gemm(s, (hl, hl))

            def v_tokens(n0, done):
                pe.wait_ge(bank_free, done)
                for m in range(KC):
                    if m >= 2:
                        pe.wait_ge(vtok_ready, n0 + m - 1)
                    for c in range(NT):
                        mm = nc.tensor.transpose(PS[:, 4 + m % 2, c * P:(c + 1) * P], VT[:, m, c * P:(c + 1) * P],
                                                 IDENT[:])
                    mm.then_inc(vt_ps, 1)

            v_tokens(0, GROUP0["v"] + COUNT["v"])

            def logits(i):
                h, qb = divmod(i, NT)
                n = (qb + 1) * P
                if i < 2:
                    pe.wait_ge(vtok_ready, KC)
                else:
                    pe.wait_ge(p_exp, i - 1)
                ps = PS[:, 4 + i % 2, :]
                nc.tensor.matmul(ps[:, qb * P:n], IDB[:], M_FOX[:], start=True, stop=False, skip_group_check=True)
                nc.tensor.matmul(ps[:, 0:n], QK[:, h, qb * P:n], QK[:, KC + h, 0:n], start=False, stop=False,
                                 skip_group_check=True)
                nc.tensor.matmul(ps[:, 0:n], IDENT[32:32 + FOX_HEADS, 32 + h:33 + h].to_broadcast([FOX_HEADS, P]),
                                 CS[32:32 + FOX_HEADS, 0:n], start=False, stop=True,
                                 skip_group_check=True).then_inc(lg_ready, 1)

            def turn(i):
                h, qb = divmod(i, NT)
                pe.wait_ge(pn_ready, i + 1)
                if i:
                    pe.wait_ge(pt_ready, i)
                for kc in range(qb + 1):
                    mm = nc.tensor.transpose(PS[:, 6, kc * P:(kc + 1) * P], TT[:, i % 2, kc * P:(kc + 1) * P], IDENT[:])
                mm.then_inc(tr_ready, 1)

            def values(h):
                pe.wait_ge(pt_ready, NT * (h + 1))
                if h:
                    pe.wait_ge(ot_ready, h)
                for kc in range(NT):
                    mm = nc.tensor.matmul(PS[:, 7, kc * P:T], VTOK[:, kc, h * P:(h + 1) * P], PT[:, kc, kc * P:T],
                                          start=kc == 0, stop=True, skip_group_check=True)
                mm.then_inc(pv_done, 1)

            n = NT * FOX_HEADS
            for i in range(n + 2):
                if i < n:
                    logits(i)
                if 1 <= i <= n:
                    turn(i - 1)
                if i >= 2 and (i - 2) % NT == NT - 1:
                    values((i - 2) // NT)

            gemm("za", (hl, hl))
            pe.wait_ge(ya_lo, COUNT["za"])
            gemm("att_out", (ylh, hl))
            pe.wait_ge(mg_lo, COUNT["att_out"])
            gemm("w_out", ((MH, ML), (MH, ML)))
            norm(N_FINAL)

            gemm("pw1", (hl, hl), (h_ready, KC * N_FINAL, 1))
            mean(N_CONV)
            norm(N_CONV)
            gemm("pw2", (ylh, ylh), (h_ready, KC * N_CONV, 1))

            def feed_forward(layer, n_mix, n_out):
                mean(n_mix)
                norm(n_mix)
                gate = f"gate{layer}"
                pe.wait_ge(ple_lo, layer + 1)
                for j in range(COUNT[gate]):
                    s = Step(j)
                    slot(s, gate, (hl, hl), (h_ready, KC * n_mix, 1) if j == 0 else None)
                    b = s.odd(1, GROUP0[gate])
                    for u in range(2):
                        m = 2 * j + u
                        for k in range(PC):
                            mm = product(PS[:, 4 + 2 * b + u, :], WPH[:, k, m * P:(m + 1) * P],
                                         WPL[:, k, m * P:(m + 1) * P], PPH[:, k, :], PPL[:, k, :], k == 0, k == PC - 1)
                    mm.then_inc(pg_ready, 1)
                gemm(f"up{layer}", (hl, hl))
                pe.wait_ge(ff_lo, FC * (layer + 1))
                down = f"down{layer}"

                def one(s):
                    for part in range(DOWN_S):
                        slot(s, down, ((FH, FL), (FH, FL)), last=part == DOWN_S - 1, mul=DOWN_S, part=part,
                             ks=min(KC, FC - part * KC))
                steps(pe, None, 4, 0, one)
                mean(n_out)
                norm(n_out)

            feed_forward(0, N_MIX0, N_OUT0)
            for i, s in enumerate(("q1", "k1", "v1")):
                gemm(s, (hl, hl), (h_ready, KC * N_OUT0, 1) if i == 0 else None)
            v_tokens(KC, GROUP0["v1"] + COUNT["v1"])

            def zs(h):
                pb, c = (h % 2) * 64, h // 2
                r = slice(pb, pb + 64)
                if h == 0:
                    pe.wait_ge(vtok_ready, 2 * KC)
                if h >= 2:
                    pe.wait_ge(a_ready, h - 1)
                flat = PS[:, 4 * (h % 2):4 * (h % 2) + 3, :].rearrange("p b t -> p (b t)")
                for kc in (0, 1, 3, 2):
                    w = T - kc * P
                    reg = flat[:, SB_OFF[kc]:SB_OFF[kc] + w]
                    nc.tensor.matmul(reg, QK[r, KC + c, kc * P:(kc + 1) * P], QK[r, c, kc * P:T], start=kc != 3,
                                     stop=True, skip_group_check=True)
                    mm = nc.tensor.matmul(reg[:, 0:P], IDB[:], M_SB[:], start=False, stop=True, skip_group_check=True)
                mm.then_inc(sz_ps, 1)

            def tri(h):
                pe.wait_ge(sp_ready, h + 1)
                flat = PS[:, 4 * (h % 2):4 * (h % 2) + 3, :].rearrange("p b t -> p (b t)")
                ex = EX[h % 2]
                for kc in range(NT):
                    w = T - kc * P
                    mm = nc.tensor.matmul(flat[:, SB_OFF[kc]:SB_OFF[kc] + w], TRI[:], ex[:, SB_OFF[kc]:SB_OFF[kc] + w],
                                          start=False, stop=True, skip_group_check=True)
                    for jc in range(kc + 1, NT):
                        wj = T - jc * P
                        o = SB_OFF[kc] + (jc - kc) * P
                        mm = nc.tensor.matmul(flat[:, o:o + wj], NEGC.to_broadcast([P, P]),
                                              ex[:, SB_OFF[jc]:SB_OFF[jc] + wj], start=False, stop=True,
                                              skip_group_check=True)
                mm.then_inc(tri_done, 1)

            def sb_values(h):
                pb = (h % 2) * 64
                pe.wait_ge(a_ready, h + 1)
                if h >= 2:
                    pe.wait_ge(so_ready, h - 1)
                for kc in range(NT):
                    mm = nc.tensor.matmul(PS[pb:pb + 64, 4 * (h % 2) + 3, kc * P:T], VTOK[:, kc, h * 64:h * 64 + 64],
                                          AT[h % 2][:, SB_OFF[kc]:SB_OFF[kc] + T - kc * P], start=kc == 0,
                                          stop=True, skip_group_check=True)
                mm.then_inc(sb_pv, 1)

            for i in range(SB_HEADS + 2):
                if i < SB_HEADS:
                    zs(i)
                if 1 <= i <= SB_HEADS:
                    tri(i - 1)
                if i >= 2:
                    sb_values(i - 2)
            gemm("wo", (ylh, ylh), (so_lo, 0, 1))
            feed_forward(1, N_MIX1, N_OUT1)

        @block.scalar
        def _(act):
            own = Chain(act, act_own)
            a = nc.scalar.activation

            def split_hi(s, mul, g):
                if isinstance(s.val(), int) and s.val(mul, g) >= NSLOTS:
                    return
                p = s.odd(mul, g)
                act.wait_ge(raw_in[p], 16 * s.half(mul, g) + 16)
                if not (isinstance(s.val(), int) and s.val(mul, g) < 2):
                    act.wait_ge(slot_done, s.val(mul, g - 1))
                a(WH[:, p], RAW[:, p], ACT.Copy).then_inc(w_hi, 1)

            def slots(stage, body, per=0, tail=0, head=0):
                g0 = SLOT0[stage]

                def one(s):
                    split_hi(s, 1, g0 + 1)
                    body(s, s.odd(1, GROUP0[stage]))
                steps(act, own, COUNT[stage], per, one, tail=tail, head=head)

            def evacuated(s, stage):
                act.wait_ge(slot_done, s.val(1, SLOT0[stage] + 1))

            def squares(n, src, ready=None):
                for m in range(KC):
                    if ready:
                        act.wait_ge(ready[0], ready[1] + m + 1)
                    if KC * n + m >= 2:
                        act.wait_ge(sq_used, KC * n + m - 1)
                    a(TT[:, m % 2, :], src[:, m, :], ACT.Square).then_inc(sq_ready, 1)
                act.wait_ge(sq_used, KC * (n + 1))
                a(TT[:, 2, :], NB, ACT.Sqrt, bias=EPS_LN if n in LN_OF else EPS_RMS).then_inc(std_ready, 1)

            def norm_hi(n, dst, hi, bias=None, func=ACT.Identity):
                for m in range(KC):
                    act.wait_ge(t_ready, KC * n + m + 1)
                    if bias is None:
                        a(hi[:, m, :], dst[:, m, :], ACT.Copy).then_inc(hi_ready, 1)
                    else:
                        a(hi[:, m, :], dst[:, m, :], func, bias=bias(m))
                        a(dst[:, m, :], dst[:, m, :], func, bias=bias(m)).then_inc(hi_ready, 1)

            for k in range(KC):
                act.dma_start(ADA[k][:], w_ada[k]).then_inc(ada_in[k], 16)
            act.wait_ge(par_in, 16)
            a(CSIL[:], col("c", 0, KC), ACT.Silu).then_inc(c_ready, 1)
            a(AEXP[0:SSM_HEADS], PAR[0:SSM_HEADS, PCOL["a_log"]:PCOL["a_log"] + 1], ACT.Exp).then_inc(c_ready, 1)
            act.wait_ge(sw_in, 16)
            a(SWH[:], SWR[:], ACT.Copy).then_inc(sw_hi, 1)
            act.wait_ge(x_in, 16)
            act.wait_ge(const_ready, 6)
            squares(N_X, X)
            split_hi(Step(0), 1, 0)
            act.wait_ge(ada_ready, 1)
            norm_hi(N_X, XN, H, lambda m: ADAV[:, m:m + 1])

            def xbc(s, p):
                act.wait_ge(bank_free, s.val(1, GROUP0["xbc"] + 1))
                xc = rows(XC, s.val(2), 2)
                a(xc, xc, ACT.Silu).then_inc(xc_ready, 1)
            slots("xbc", xbc, head=2)

            act.wait_ge(dt_u, 2)
            a(SM[0:SMALL, 1, :], SM[0:SMALL, 1, :], ACT.Exp).then_inc(dt_e, 1)
            act.wait_ge(dt_w, 1)
            a(SM[0:SMALL, 3, :], SM[0:SMALL, 2, :], ACT.Ln).then_inc(dt_l, 1)
            act.wait_ge(bt_ps, 1)
            a(BTOK[:].rearrange("p c n -> p (c n)"), PS[:, 4, :], ACT.Copy).then_inc(bt_ready, 1)
            act.wait_ge(dt_x, 1)
            a(SM[0:SSM_HEADS, 1, :], SM[0:SSM_HEADS, 1, :], ACT.Exp).then_inc(dt_d, 1)
            act.wait_ge(cb_ps, 2)
            for g in range(SSM_GROUPS):
                a(CBM[:, g, :], PS[:, 4 + g, :], ACT.Copy).then_inc(cb_ready, 1)
            for r in range(HPG):
                act.wait_ge(e_ps, r + 1)
                a(EL[:, r, :], PS[:, 6 + r % 2, P - 1::P], ACT.Exp)
                a(CE[:, r, :], PS[:, 6 + r % 2, :], ACT.Exp).then_inc(e_exp, 1)
            for h in range(SSM_HEADS):
                act.wait_ge(seg_ready, h + 1)
                a(MT[:, h % 2, :], MT[:, h % 2, :], ACT.Exp).then_inc(seg_exp, 1)

            def z(s, p):
                evacuated(s, "z")
                act.wait_ge(bank_free, s.val(1, GROUP0["z"]))
                a(rows(ZS, s.val(2), 2), PS[:, 2 * p:2 * p + 2, :], ACT.Silu).then_inc(bank_free, 1)
            act.wait_ge(y_ps, SSM_HEADS)
            slots("z", z)
            squares(N_SSM, XC, (yz_ready, 0))
            norm_hi(N_SSM, XC, YH)

            def gates(stage, bias0, name):
                def body(s, p):
                    evacuated(s, stage)
                    a(TT[:, p, :], PS[:, 2 * p + 1, :], ACT.Sigmoid,
                      bias=dcol(name, s.val(1, bias0))).then_inc(sig_ready, 1)
                return body
            slots("ssm_out", gates("ssm_out", 0, "b_gate"))

            def copies(stage, dst, m0, scale):
                def body(s, p):
                    evacuated(s, stage)
                    act.wait_ge(bank_free, s.val(1, GROUP0[stage]))
                    a(rows(dst, s.val(2, m0), 2), PS[:, 2 * p:2 * p + 2, :], ACT.Copy,
                      scale=scale).then_inc(bank_free, 1)
                slots(stage, body)
            copies("q", QK, 0, float(P ** -0.5))
            copies("k", QK, KC, 1.0)
            copies("v", VT, 0, 1.0)

            def p_turned(i):
                h, qb = divmod(i, NT)
                act.wait_ge(tr_ready, i + 1)
                if qb == 0 and h:
                    act.wait_ge(pv_done, h)
                a(PT[:, 0:qb + 1, qb * P:(qb + 1) * P],
                  PS[:, 6, 0:(qb + 1) * P].rearrange("p (k q) -> p k q", q=P), ACT.Copy).then_inc(pt_ready, 1)

            n = NT * FOX_HEADS
            for i in range(n + 1):
                if i < n:
                    w_ = (i % NT + 1) * P
                    act.wait_ge(nm_ready, i + 1)
                    if i >= 2:
                        act.wait_ge(tr_ready, i - 1)
                    a(TT[:, i % 2, 0:w_], PS[:, 4 + i % 2, 0:w_], ACT.Exp, bias=STAT[:, 0, i:i + 1],
                      accum_out=STAT[:, 1, i:i + 1]).then_inc(p_exp, 1)
                if i:
                    p_turned(i - 1)

            def za(s, p):
                evacuated(s, "za")
                act.wait_ge(bank_free, s.val(1, GROUP0["za"]))
                a(rows(ZA, s.val(2), 2), PS[:, 2 * p:2 * p + 2, :], ACT.Silu).then_inc(bank_free, 1)
                act.wait_ge(ya_ready, s.val(1, 1))
                a(rows(YH, s.val(2), 2), rows(QK, s.val(2), 2), ACT.Copy).then_inc(ya_hi, 1)
            slots("za", za)

            def att_out(s, p):
                gates("att_out", KC, "b_gate")(s, p)
                act.wait_ge(mg_ready, s.val(1, 1))
                a(rows(MH, s.val(), 1), rows(P1, s.val(), 1), ACT.Copy).then_inc(mg_hi, 1)
            slots("att_out", att_out)
            slots("w_out", lambda s, p: None)
            act.wait_ge(bank_free, GROUP0["w_out"] + COUNT["w_out"])
            squares(N_FINAL, X)
            norm_hi(N_FINAL, X, H)

            def load_ple(layer):
                act.dma_start(PWR[:], w_ple[layer]).then_inc(ple_in, 16)
                act.dma_start(PR[:], p_t[layer]).then_inc(ple_in, 16)

            def split_ple_hi(layer):
                act.wait_ge(ple_in, 32 * (layer + 1))
                a(WPH[:], PWR[:], ACT.Copy)
                a(PPH[:], PR[:], ACT.Copy).then_inc(ple_hi, 1)

            load_ple(0)
            slots("pw1", gates("pw1", KC, "pw1_b"))
            squares(N_CONV, CV, (cen_ready, KC * LN_OF[N_CONV]))
            norm_hi(N_CONV, CV, YH, lambda m: col("ln_b", m), ACT.Silu)
            split_ple_hi(0)
            slots("pw2", lambda s, p: None)

            def feed_forward(layer, n_mix, n_out):
                squares(n_mix, X, (cen_ready, KC * LN_OF[n_mix]))
                norm_hi(n_mix, X, H, lambda m: col("mix_b", KC * layer + m))
                gate = f"gate{layer}"

                def gate_body(s, p):
                    evacuated(s, gate)
                    act.wait_ge(bank_free, s.val(1, GROUP0[gate]))
                    a(TT[:, 0:2, :], PS[:, 2 * p:2 * p + 2, :], ACT.Sigmoid).then_inc(sig_ready, 1)
                slots(gate, gate_body)
                up = f"up{layer}"

                def up_body(s, p):
                    act.wait_ge(gc_ready, s.val(1, FC * layer + 1))
                    a(TT[:, p, :], TT[:, 3, :], ACT.Silu).then_inc(sl_ready, 1)
                    act.wait_ge(bank_free, s.val(1, GROUP0[up] + 1))
                    a(rows(FH, s.val(), 1), TT[:, 3:4, :], ACT.Copy).then_inc(ff_hi, 1)
                slots(up, up_body)
                down = f"down{layer}"

                def down_one(s):
                    for part in range(DOWN_S):
                        split_hi(s, DOWN_S, SLOT0[down] + part + 1)
                steps(act, own, 4, 0, down_one, tail=2 if layer else 0)
                squares(n_out, X, (cen_ready, KC * LN_OF[n_out]))

            feed_forward(0, N_MIX0, N_OUT0)
            norm_hi(N_OUT0, X, H, lambda m: col("out_b", m))
            copies("q1", QK, 0, float(SB_DIM ** -0.5))
            copies("k1", QK, KC, 1.0)
            copies("v1", VT, 0, 1.0)

            for i in range(SB_HEADS + 1):
                if i < SB_HEADS:
                    flat = PS[:, 4 * (i % 2):4 * (i % 2) + 3, :].rearrange("p b t -> p (b t)")[:, 0:SBC]
                    ex = EX[i % 2]
                    act.wait_ge(sz_ps, i + 1)
                    if i >= 2:
                        act.wait_ge(tri_done, i - 1)
                    own.did(a(ex[:], flat, ACT.Abs))
                    own.settle()
                    own.did(a(ex[:], ex[:], ACT.Exp, scale=-1.0))
                    own.settle()
                    a(ex[:], ex[:], ACT.Ln, bias=1.0).then_inc(sz_exp, 1)
                if i:
                    h = i - 1
                    flat = PS[:, 4 * (h % 2):4 * (h % 2) + 3, :].rearrange("p b t -> p (b t)")[:, 0:SBC]
                    act.wait_ge(tri_done, h + 1)
                    if h >= 2:
                        act.wait_ge(sb_pv, h - 1)
                    a(AT[h % 2][:], flat, ACT.Exp).then_inc(a_ready, 1)
            act.wait_ge(so_ready, SB_HEADS)
            for m in range(KC):
                a(YH[:, m, :], QK[:, m, :], ACT.Copy).then_inc(so_hi, 1)
            act.wait_ge(so_lo, KC)
            load_ple(1)
            slots("wo", lambda s, p: None)
            split_ple_hi(1)
            feed_forward(1, N_MIX1, N_OUT1)
            for m in range(KC):
                act.wait_ge(t_ready, KC * N_OUT1 + m + 1)
                a(X[:, m, :], X[:, m, :], ACT.Identity, bias=col("out_b", KC + m)).then_inc(out_ready, 1)

        @block.vector
        def _(dve):
            own = Chain(dve, dve_own)
            v = nc.vector
            acc, tmp = TT[:, 2, :], TT[:, 3, :]

            def split_lo(s, mul, g):
                if isinstance(s.val(), int) and s.val(mul, g) >= NSLOTS:
                    return
                p = s.odd(mul, g)
                dve.wait_ge(w_hi, s.val(mul, g + 1))
                v.tensor_tensor(WL[:, p], RAW[:, p], WH[:, p].bitcast(F32), ALU.subtract).then_inc(w_lo, 1)

            def slots(stage, body, per=0, tail=0, head=0):
                g0 = SLOT0[stage]

                def one(s):
                    split_lo(s, 1, g0 + 1)
                    body(s, s.odd(1, GROUP0[stage]))
                steps(dve, own, COUNT[stage], per, one, tail=tail, head=head)

            def evacuated(s, stage, mul=1, more=0):
                dve.wait_ge(slot_done, s.val(mul, SLOT0[stage] + 1 + more))

            def free(s, stage, ins):
                ins.then_inc(bank_free, 1)

            def earlier_free(s, stage):
                dve.wait_ge(bank_free, s.val(1, GROUP0[stage]))

            def norm_out(n, src, dst, g, hi=None, lo=None):
                dve.wait_ge(std_ready, n + 1)
                own.did(v.reciprocal(acc, acc))
                own.settle()

                def low(m):
                    dve.wait_ge(hi_ready, KC * n + m + 1)
                    v.tensor_tensor(lo[:, m, :], dst[:, m, :], hi[:, m, :].bitcast(F32),
                                    ALU.subtract).then_inc(h_ready, 1)
                for m in range(KC):
                    v.scalar_tensor_tensor(dst[:, m, :], src[:, m, :], g(m), acc, ALU.mult,
                                           ALU.mult).then_inc(t_ready, 1)
                    if m and lo is not None:
                        low(m - 1)
                if lo is not None:
                    low(KC - 1)

            def center(n, src):
                dve.wait_ge(mean_ready, LN_OF[n] + 1)
                for m in range(KC):
                    v.tensor_tensor(src[:, m, :], src[:, m, :], MB, ALU.subtract).then_inc(cen_ready, 1)

            dve.wait_ge(c_ready, 2)
            dve.wait_ge(sw_hi, 1)
            v.tensor_tensor(SWL[:], SWR[:], SWH[:].bitcast(F32), ALU.subtract).then_inc(sw_lo, 1)
            for k in range(KC):
                dve.wait_ge(ada_in[k], 16)
                if k == 0:
                    ins = v.tensor_scalar(ADAS[:], ADA[0][:], CSIL[:, 0:1], None, ALU.mult)
                else:
                    own.settle()
                    ins = v.scalar_tensor_tensor(ADAS[:], ADA[k][:], CSIL[:, k:k + 1], ADAS[:], ALU.mult, ALU.add)
                if k < KC - 1:
                    own.did(ins)
            ins.then_inc(ada_sum, 1)
            split_lo(Step(0), 1, 0)
            dve.wait_ge(ada_ps, 1)
            dve.wait_ge(par_in, 16)
            own.did(v.tensor_tensor(ADAV[:], PS[:, 5, 0:3 * KC], col("b_ada", 0, 3 * KC), ALU.add))
            own.settle()
            own.did(v.tensor_scalar(GX[:], ADAV[:, KC:2 * KC], 1.0, None, ALU.add))
            own.settle()
            v.tensor_tensor(GX[:], GX[:], col("norm_w", 0, KC), ALU.mult).then_inc(ada_ready, 1)
            dve.wait_ge(ada_ready, 1)
            norm_out(N_X, X, XN, lambda m: GX[:, m:m + 1], H, L)

            def xbc(s, p):
                evacuated(s, "xbc")
                for tap in range(CONV_K):
                    d = tap
                    for u in range(2):
                        m = s.val(2, u)
                        w_ = dcol("conv_w", s.val(2, u + (CONV_K - 1 - tap) * XBC_C))
                        dst = rows(XC, m, 1)
                        ps = PS[:, 2 * p + u:2 * p + u + 1, :]
                        if tap == 0:
                            own.did(v.tensor_scalar(dst, ps, w_, dcol("conv_b", m), ALU.mult, ALU.add))
                        else:
                            ins = v.scalar_tensor_tensor(dst[:, :, d:T], ps[:, :, 0:T - d], w_, dst[:, :, d:T],
                                                         ALU.mult, ALU.add)
                            if tap == CONV_K - 1 and u == 1:
                                free(s, "xbc", ins)
                            else:
                                own.did(ins)
                    if tap < CONV_K - 1:
                        own.settle()
            slots("xbc", xbc, per=2 * CONV_K - 1)

            R = slice(0, SMALL)
            U, E, W1, LN1 = (SM[R, i, :] for i in range(4))
            T0, T1, T2, T3 = (TT[R, i, :] for i in range(4))
            dve.wait_ge(dt_ps, 1)
            v.tensor_scalar(U, PS[R, 4, :], PAR[R, PCOL["small_b"]:PCOL["small_b"] + 1], SGN[R], ALU.add,
                            ALU.mult).then_inc(dt_u, 1)
            dve.wait_ge(dt_u, 1)
            v.scalar_tensor_tensor(E, U, -1.0, U, ALU.mult, ALU.min).then_inc(dt_u, 1)
            dve.wait_ge(dt_e, 1)
            v.tensor_scalar(W1, E, 1.0, None, ALU.add).then_inc(dt_w, 1)
            dve.wait_ge(dt_w, 1)
            own.did(v.tensor_scalar(T0, W1, -1.0, HALF_ULP, ALU.add, ALU.max))
            own.did(v.tensor_scalar(T1, W1, 1.0, None, ALU.is_equal))
            own.settle()
            own.did(v.reciprocal(T0, T0))
            own.did(v.tensor_tensor(T1, T1, E, ALU.mult))
            own.settle()
            own.did(v.tensor_tensor(T0, T0, E, ALU.mult))
            dve.wait_ge(dt_l, 1)
            own.settle()
            own.did(v.tensor_tensor(T0, T0, LN1, ALU.mult))
            own.settle()
            own.did(v.tensor_tensor(T0, T0, T1, ALU.add))
            own.settle()
            own.did(v.scalar_tensor_tensor(LN1, U, 0.0, T0, ALU.max, ALU.add))
            own.settle()
            S = slice(0, SSM_HEADS)
            own.did(v.tensor_scalar(T2[S], LN1[S], AEXP[S], -1.0, ALU.mult, ALU.mult))
            own.settle()
            for c in range(NT):
                cc = slice(c * P, (c + 1) * P)
                own.did(v.tensor_tensor_scan(CS[S, cc], ONEC[S].to_broadcast([SSM_HEADS, P]), T2[S, cc], 0.0, ALU.mult,
                                             ALU.add))
            Fr = slice(32, 32 + FOX_HEADS)
            own.did(v.tensor_tensor_scan(CS[Fr, :], ONEC[Fr].to_broadcast([FOX_HEADS, T]), SM[Fr, 3, :], 0.0, ALU.mult,
                                         ALU.add))
            own.settle()
            cs = CS[S, :].rearrange("h (c t) -> h c t", c=NT)
            v.tensor_tensor(SM[S, 1, :].rearrange("h (c t) -> h c t", c=NT),
                            cs[:, :, P - 1:P].to_broadcast([SSM_HEADS, NT, P]), cs, ALU.subtract).then_inc(dt_x, 1)
            dve.wait_ge(dt_d, 1)
            v.tensor_tensor(SM[S, 1, :], SM[S, 1, :], SM[S, 3, :], ALU.mult).then_inc(dt_rows, 1)
            dve.wait_ge(tok_ps, 1)
            v.tensor_copy(TOK[:].rearrange("p a c h -> p (a c h)"),
                          PS[:, 5, 0:3 * NT * SSM_HEADS]).then_inc(tok_ready, 1)
            dve.wait_ge(tok_ready, 1)

            for i in range(2 * NT):
                c, half = divmod(i, 2)
                dve.wait_ge(xt_ps, i + 1)
                ps = PS[:, 6 + i % 2, :].rearrange("p (h d) -> p h d", d=SSM_P)
                hs = slice(half * 8, half * 8 + 8)
                fs = slice(half * T, (half + 1) * T)

                def scaled(dst, which):
                    return v.tensor_tensor(dst[:, c, fs].rearrange("p (h d) -> p h d", d=SSM_P), ps,
                                           TOK[:, which, c, hs].unsqueeze(2).to_broadcast([P, 8, SSM_P]), ALU.mult)
                ins = scaled(XD, 1)
                if c < NT - 1:
                    own.did(ins)
                    ins = scaled(XDD, 2)
                ins.then_inc(xt_used, 1)
            for r in range(HPG):
                dve.wait_ge(e_exp, r + 1)
                v.tensor_tensor(CE[:, r, :], CE[:, r, :], XC[:, KC + 1, :], ALU.mult).then_inc(ce_ready, 1)
            for c in range(NT - 1):
                dve.wait_ge(st_ps, c + 1)
                if c == 0:
                    v.tensor_copy(ST[:, 0, :], PS[:, 5, :]).then_inc(st_ready, 1)
                else:
                    own.did(v.tensor_tensor(ST[:, c, :].rearrange("p (r d) -> p r d", d=SSM_P),
                                            ST[:, c - 1, :].rearrange("p (r d) -> p r d", d=SSM_P),
                                            EL[:, :, c:c + 1].to_broadcast([P, HPG, SSM_P]), ALU.mult))
                    own.settle()
                    v.tensor_tensor(ST[:, c, :], ST[:, c, :], PS[:, 5, :], ALU.add).then_inc(st_ready, 1)
                dve.wait_ge(st_ready, c + 1)

            def seg(h):
                dve.wait_ge(seg_ps, h + 1)
                if h >= 2:
                    dve.wait_ge(y_ps, h - 1)
                v.tensor_tensor(MT[:, h % 2, :].rearrange("p (c t) -> p c t", c=NT),
                                PS[:, 6 + h % 2, :].rearrange("p (c t) -> p c t", c=NT),
                                TOK[:, 0, :, h:h + 1].to_broadcast([P, NT, P]), ALU.subtract).then_inc(seg_ready, 1)

            dve.wait_ge(cb_ready, 2)
            seg(0)
            for h in range(SSM_HEADS):
                if h + 1 < SSM_HEADS:
                    seg(h + 1)
                dve.wait_ge(seg_exp, h + 1)
                v.tensor_tensor(MT[:, h % 2, :], MT[:, h % 2, :], CBM[:, h // HPG, :], ALU.mult).then_inc(mt_ready, 1)
                if h % 2 == 0 and h:
                    i = h // 2 - 1
                    dve.wait_ge(y_ps, 2 * i + 2)
                    v.scalar_tensor_tensor(XC[:, i, :], XC[:, i, :], col("d_skip", i), PS[:, 4 + i % 2, :], ALU.mult,
                                           ALU.add).then_inc(y_used, 1)
            i = KC - 1
            dve.wait_ge(y_ps, SSM_HEADS)
            v.scalar_tensor_tensor(XC[:, i, :], XC[:, i, :], col("d_skip", i), PS[:, 4 + i % 2, :], ALU.mult,
                                   ALU.add).then_inc(y_used, 1)
            dve.wait_ge(y_used, KC)
            slots("z", lambda s, p: None)
            dve.wait_ge(bank_free, GROUP0["z"] + COUNT["z"])
            for m in range(KC):
                v.tensor_tensor(XC[:, m, :], XC[:, m, :], ZS[:, m, :], ALU.mult).then_inc(yz_ready, 1)
            dve.wait_ge(yz_ready, KC)
            norm_out(N_SSM, XC, XC, lambda m: col("ssm_norm_w", m), YH, YL)

            def ssm_out(s, p):
                earlier_free(s, "ssm_out")
                dve.wait_ge(sig_ready, s.val(1, SIG0["ssm_out"] + 1))
                free(s, "ssm_out", v.tensor_tensor(rows(P1, s.val(), 1), PS[:, 2 * p:2 * p + 1, :], TT[:, p:p + 1, :],
                                                   ALU.mult))
            slots("ssm_out", ssm_out)
            for s_ in ("q", "k", "v"):
                slots(s_, lambda s, p: None)

            def v_tokens(n0):
                for m in range(KC):
                    dve.wait_ge(vt_ps, n0 + m + 1)
                    v.tensor_copy(VTOK[:, :, m * P:(m + 1) * P],
                                  PS[:, 4 + m % 2, :].rearrange("p (c f) -> p c f", c=NT)).then_inc(vtok_ready, 1)
            v_tokens(0)

            n = NT * FOX_HEADS
            for i in range(n + 1):
                if i < n:
                    w_ = (i % NT + 1) * P
                    dve.wait_ge(lg_ready, i + 1)
                    own.did(v.tensor_reduce(STAT[:, 2, i:i + 1], PS[:, 4 + i % 2, 0:w_], AX_X, ALU.max))
                    own.settle()
                    v.tensor_scalar(STAT[:, 0, i:i + 1], STAT[:, 2, i:i + 1], -1.0, None, ALU.mult).then_inc(nm_ready, 1)
                if i:
                    j = i - 1
                    h, qb = divmod(j, NT)
                    w_ = (qb + 1) * P
                    dve.wait_ge(p_exp, j + 1)
                    own.did(v.reciprocal(STAT[:, 2, j:j + 1], STAT[:, 1, j:j + 1]))
                    own.settle()
                    v.tensor_scalar(TT[:, j % 2, 0:w_], TT[:, j % 2, 0:w_], STAT[:, 2, j:j + 1], None,
                                    ALU.mult).then_inc(pn_ready, 1)
                    if qb == 0 and h:
                        dve.wait_ge(pv_done, h)
                        v.tensor_copy(QK[:, h - 1, :], PS[:, 7, :]).then_inc(ot_ready, 1)
            dve.wait_ge(pv_done, FOX_HEADS)
            v.tensor_copy(QK[:, FOX_HEADS - 1, :], PS[:, 7, :]).then_inc(ot_ready, 1)
            dve.wait_ge(ot_ready, FOX_HEADS)

            def za(s, p):
                dve.wait_ge(bank_free, s.val(1, GROUP0["za"] + 1))
                q = rows(QK, s.val(2), 2)
                v.tensor_tensor(q, q, rows(ZA, s.val(2), 2), ALU.mult).then_inc(ya_ready, 1)
                dve.wait_ge(ya_hi, s.val(1, 1))
                v.tensor_tensor(rows(YL, s.val(2), 2), q, rows(YH, s.val(2), 2).bitcast(F32),
                                ALU.subtract).then_inc(ya_lo, 1)
            slots("za", za)

            def att_out(s, p):
                earlier_free(s, "att_out")
                dve.wait_ge(sig_ready, s.val(1, SIG0["att_out"] + 1))
                ins = v.tensor_tensor(TT[:, p:p + 1, :], PS[:, 2 * p:2 * p + 1, :], TT[:, p:p + 1, :], ALU.mult)
                free(s, "att_out", ins)
                dve.wait_ge(bank_free, s.val(1, GROUP0["att_out"] + 1))
                p1 = rows(P1, s.val(), 1)
                v.tensor_tensor(p1, p1, TT[:, p:p + 1, :], ALU.add).then_inc(mg_ready, 1)
                dve.wait_ge(mg_hi, s.val(1, 1))
                v.tensor_tensor(rows(ML, s.val(), 1), p1, rows(MH, s.val(), 1).bitcast(F32),
                                ALU.subtract).then_inc(mg_lo, 1)
            slots("att_out", att_out)

            def w_out(s, p):
                evacuated(s, "w_out")
                for u in range(2):
                    x = rows(X, s.val(2, u), 1)
                    m = s.val(2, u + 2 * KC)
                    g = ADAV[:, m:m + 1] if isinstance(m, int) else ADAV[:, bass.ds(m, 1)]
                    ins = v.scalar_tensor_tensor(x, PS[:, 2 * p + u:2 * p + u + 1, :], g, x, ALU.mult, ALU.add)
                free(s, "w_out", ins)
            slots("w_out", w_out)
            norm_out(N_FINAL, X, X, lambda m: col("final_norm_w", m), H, L)

            own.did(v.memset(HC[:, :, 0:PAD], 0.0))

            def pw1(s, p):
                dve.wait_ge(sig_ready, s.val(1, SIG0["pw1"] + 1))
                free(s, "pw1", v.scalar_tensor_tensor(rows(HC, s.val(), 1)[:, :, PAD:PAD + T],
                                                      PS[:, 2 * p:2 * p + 1, :], dcol("pw1_b", s.val()),
                                                      TT[:, p:p + 1, :], ALU.add, ALU.mult))
                dve.wait_ge(bank_free, s.val(1, GROUP0["pw1"] + 1))
                cv, hc = rows(CV, s.val(), 1), rows(HC, s.val(), 1)
                for k in range(DW_K):
                    w_ = dcol("dw_w", s.val(1, k * KC))
                    src = hc[:, :, k:k + T]
                    if k == 0:
                        own.did(v.tensor_scalar(cv, src, w_, dcol("dw_b", s.val()), ALU.mult, ALU.add))
                    else:
                        own.did(v.scalar_tensor_tensor(cv, src, w_, cv, ALU.mult, ALU.add))
                    own.settle()
            slots("pw1", pw1, per=DW_K)
            own.did(v.tensor_tensor(acc, CV[:, 0, :], CV[:, 1, :], ALU.add))
            for m in range(2, KC):
                own.settle()
                ins = v.tensor_tensor(acc, acc, CV[:, m, :], ALU.add)
                if m < KC - 1:
                    own.did(ins)
            ins.then_inc(sum_ready, 1)
            center(N_CONV, CV)
            norm_out(N_CONV, CV, CV, lambda m: col("ln_g", m), YH, YL)
            for m in range(KC):
                own.did(v.tensor_scalar(X[:, m, :], X[:, m, :], ALPHA, col("pw2_b", m), ALU.mult, ALU.add))

            def split_ple_lo(layer):
                dve.wait_ge(ple_hi, layer + 1)
                own.did(v.tensor_tensor(WPL[:], PWR[:], WPH[:].bitcast(F32), ALU.subtract))
                v.tensor_tensor(PPL[:], PR[:], PPH[:].bitcast(F32), ALU.subtract).then_inc(ple_lo, 1)

            split_ple_lo(0)
            own.did(v.memset(acc, 0.0))
            own.settle()

            def sums(s, last=None):
                for u in range(2):
                    own.settle()
                    own.did(v.tensor_tensor(acc, acc, X[:, s.val(2, u), :] if isinstance(s.val(), int) else
                                            rows(X, s.val(2, u), 1).rearrange("p a t -> p (a t)"), ALU.add))

            def added(stage, mul=1, more=0, first=1.0):
                def body(s, p):
                    evacuated(s, stage, mul, more)
                    x = rows(X, s.val(2), 2)
                    ps = PS[:, 2 * p:2 * p + 2, :]
                    if first == 1.0:
                        ins = v.tensor_tensor(x, x, ps, ALU.add)
                    else:
                        ins = v.scalar_tensor_tensor(x, x, first, ps, ALU.mult, ALU.add)
                    free(s, stage, ins)
                    dve.wait_ge(bank_free, s.val(1, GROUP0[stage] + 1))
                    sums(s)
                return body
            slots("pw2", added("pw2"), per=2)

            def ln_front(n):
                own.settle()
                v.tensor_copy(X[:, 0, 0:1], X[:, 0, 0:1]).then_inc(sum_ready, 1)
                center(n, X)

            def feed_forward(layer, n_mix, n_out, g_out):
                ln_front(n_mix)
                norm_out(n_mix, X, X, lambda m: col("mix_g", KC * layer + m), H, L)
                gate = f"gate{layer}"

                def gate_body(s, p):
                    dve.wait_ge(sig_ready, s.val(1, SIG0[gate] + 1))
                    dve.wait_ge(pg_ready, s.val(1, COUNT[gate] * layer + 1))
                    own.did(v.tensor_tensor(TT[:, 0:2, :], TT[:, 0:2, :], PS[:, 4 + 2 * p:6 + 2 * p, :], ALU.mult))
                    own.settle()
                    x = rows(X, s.val(2), 2)
                    free(s, gate, v.scalar_tensor_tensor(x, x, ALPHA, TT[:, 0:2, :], ALU.mult, ALU.add))
                slots(gate, gate_body, per=1)
                up = f"up{layer}"

                def up_body(s, p):
                    evacuated(s, up)
                    gate_ps = PS[:, 2 * p + 1:2 * p + 2, :]
                    c = TT[:, 3:4, :]
                    if not (isinstance(s.val(), int) and s.val(1, layer) == 0):
                        dve.wait_ge(ff_lo, s.val(1, FC * layer))
                    for d in range(FCONV_K):
                        w_ = dcol("fconv_w", s.val(1, (layer * FCONV_K + FCONV_K - 1 - d) * FC))
                        if d == 0:
                            own.did(v.tensor_scalar(c, gate_ps, w_, dcol("fconv_b", s.val(1, layer * FC)), ALU.mult,
                                                    ALU.add))
                            own.settle()
                        else:
                            ins = v.scalar_tensor_tensor(c[:, :, d:T], gate_ps[:, :, 0:T - d], w_, c[:, :, d:T],
                                                         ALU.mult, ALU.add)
                            if d == FCONV_K - 1:
                                ins.then_inc(gc_ready, 1)
                            else:
                                own.did(ins)
                                own.settle()
                    dve.wait_ge(sl_ready, s.val(1, FC * layer + 1))
                    free(s, up, v.tensor_tensor(c, TT[:, p:p + 1, :], PS[:, 2 * p:2 * p + 1, :], ALU.mult))
                    dve.wait_ge(ff_hi, s.val(1, FC * layer + 1))
                    v.tensor_tensor(rows(FL, s.val(), 1), c, rows(FH, s.val(), 1).bitcast(F32),
                                    ALU.subtract).then_inc(ff_lo, 1)
                slots(up, up_body, per=FCONV_K - 1, head=1)
                own.did(v.memset(acc, 0.0))
                down = f"down{layer}"

                def down_one(s):
                    for part in range(DOWN_S):
                        split_lo(s, DOWN_S, SLOT0[down] + part + 1)
                    added(down, DOWN_S, DOWN_S - 1)(s, s.odd(1, GROUP0[down]))
                steps(dve, own, 4, 2, down_one, tail=2 if layer else 0)
                ln_front(n_out)
                if layer == 0:
                    norm_out(n_out, X, X, g_out, H, L)
                else:
                    norm_out(n_out, X, X, g_out)

            feed_forward(0, N_MIX0, N_OUT0, lambda m: col("out_g", m))
            for s_ in ("q1", "k1", "v1"):
                slots(s_, lambda s, p: None)
            v_tokens(KC)

            for i in range(SB_HEADS + 2):
                if i < SB_HEADS:
                    flat = PS[:, 4 * (i % 2):4 * (i % 2) + 3, :].rearrange("p b t -> p (b t)")[:, 0:SBC]
                    dve.wait_ge(sz_exp, i + 1)
                    v.scalar_tensor_tensor(EX[i % 2][:], flat, 0.0, EX[i % 2][:], ALU.max, ALU.add).then_inc(sp_ready, 1)
                if i >= 2:
                    h = i - 2
                    pb = (h % 2) * 64
                    dve.wait_ge(sb_pv, h + 1)
                    v.tensor_copy(QK[pb:pb + 64, h // 2, :], PS[pb:pb + 64, 4 * (h % 2) + 3, :]).then_inc(so_ready, 1)
            for m in range(KC):
                dve.wait_ge(so_hi, m + 1)
                v.tensor_tensor(YL[:, m, :], QK[:, m, :], YH[:, m, :].bitcast(F32), ALU.subtract).then_inc(so_lo, 1)
            own.did(v.memset(acc, 0.0))
            slots("wo", added("wo", first=ALPHA), per=2)
            split_ple_lo(1)
            feed_forward(1, N_MIX1, N_OUT1, lambda m: col("out_g", KC + m))


def _unit(w, m, k0=0):
    blk = w[k0 * P:(k0 + KC) * P, m * P:(m + 1) * P]
    if blk.shape[0] < KC * P:
        blk = np.concatenate([blk, np.zeros((KC * P - blk.shape[0], P), w.dtype)])
    return blk.reshape(KC, P, P).transpose(1, 0, 2)


def _slots(i):
    w_in = i["w_in"]
    cut = lambda a, n: w_in[:, a:a + n]
    pairs = lambda a: [(_unit(a, 2 * j), _unit(a, 2 * j + 1)) for j in range(a.shape[1] // (2 * P))]
    both = lambda a, b: [(_unit(a, j), _unit(b, j)) for j in range(a.shape[1] // P)]
    down = lambda a: [(_unit(a, 2 * j, KC * s), _unit(a, 2 * j + 1, KC * s))
                      for j in range(KC // 2) for s in range(DOWN_S)]
    pw1 = i["a_pw1_w_2"][0]
    parts = [pairs(cut(XBC0, XBC)), pairs(cut(Z0, D)), both(i["w_proj_ssm"], cut(G0, D)), pairs(cut(Q0, D)),
             pairs(cut(K0, D)), pairs(cut(V0, D)), pairs(cut(ZA0, D)), both(i["w_proj_att"], cut(G0 + D, D)),
             pairs(i["w_out"]), both(pw1[:, 0:D], pw1[:, D:2 * D]), pairs(i["a_pw2_w_2"][0])]

    def ffn(layer):
        return [pairs(i["ple_w_gate_2"][layer]), both(i["ffn_w_up_2"][layer], i["ffn_w_gate_2"][layer]),
                down(i["ffn_w_down_2"][layer])]
    parts += ffn(0) + [pairs(i["b_wq_2"][0]), pairs(i["kv_wk_2"]), pairs(i["kv_wv_2"]), pairs(i["b_wo_2"][0])] + ffn(1)
    out = [np.stack(s, axis=1) for part in parts for s in part]
    return np.stack(out).reshape(NSLOTS, P, 2 * KC * P)


def _params(i):
    col = lambda a: np.asarray(a).reshape(-1, P).T
    rows = {
        "c": i["c"], "norm_w": i["norm_w"], "b_ada": i["b_ada"], "conv_w": i["conv_w"], "conv_b": i["conv_b"],
        "d_skip": np.repeat(i["d_skip"], SSM_P), "ssm_norm_w": i["ssm_norm_w"], "b_gate": i["b_gate"],
        "final_norm_w": i["final_norm_w"], "pw1_b": i["a_pw1_b_2"], "dw_w": i["a_dw_w_2"], "dw_b": i["a_dw_b_2"],
        "ln_g": i["a_ln_g_2"], "ln_b": i["a_ln_b_2"], "pw2_b": i["a_pw2_b_2"], "mix_g": i["ln_mix_g_2"],
        "mix_b": i["ln_mix_b_2"], "fconv_w": i["ffn_conv_w_2"], "fconv_b": i["ffn_conv_b_2"],
        "out_g": i["ln_ffn_g_2"], "out_b": i["ln_ffn_b_2"],
    }
    par = np.zeros((P, NPAR), np.float32)
    for name, a in rows.items():
        c = col(a)
        par[:, PCOL[name]:PCOL[name] + c.shape[1]] = c
    par[0:SSM_HEADS, PCOL["small_b"]] = i["dt_bias"]
    par[32:32 + FOX_HEADS, PCOL["small_b"]] = i["b_f"]
    par[0:SSM_HEADS, PCOL["a_log"]] = i["a_log"]
    return par


def kernel(**inputs):
    import concourse.bacc as bacc
    from concourse.bass_utils import run_bass_kernel_spmd

    i = {k: np.asarray(a) for k, a in inputs.items()}
    chunks = lambda a: a.reshape(-1, P, a.shape[-1]).transpose(1, 0, 2)
    w_small = np.zeros((D, SMALL), np.float32)
    w_small[:, 0:SSM_HEADS] = i["w_in"][:, DT0:DT0 + SSM_HEADS]
    w_small[:, 32:SMALL] = i["w_in"][:, FL0:FL0 + FOX_HEADS]
    arrays = {
        "w": _slots(i),
        "w_ada": i["w_ada"].reshape(KC, P, 3 * D),
        "w_small": chunks(w_small),
        "w_ple": np.stack([chunks(i["ple_w_proj_2"][n]) for n in range(2)]),
        "p_t": np.stack([chunks(i["p_2"][n, 0].T) for n in range(2)]),
        "x_t": chunks(i["x"][0].T),
        "par": _params(i),
    }
    arrays = {k: np.ascontiguousarray(a) for k, a in arrays.items()}
    nc = bacc.Bacc("TRN2", target_bir_lowering=False, num_devices=1)
    aps = [nc.dram_tensor(k, a.shape, F32, kind="ExternalInput").ap() for k, a in arrays.items()]
    out = nc.dram_tensor("out", (P, KC, T), F32, kind="ExternalOutput").ap()
    build(nc, *aps, out)
    r = run_bass_kernel_spmd(nc, [arrays], core_ids=[0])
    return np.asarray(r.results[0]["out"]).transpose(2, 1, 0).reshape(1, T, D)
```

```python
from contextlib import ExitStack

import numpy as np

import concourse.bass as bass
from concourse import mybir

F32 = mybir.dt.float32
F32R = mybir.dt.float32r
BF16 = mybir.dt.bfloat16
ACT = mybir.ActivationFunctionType
ALU = mybir.AluOpType
AX_X = mybir.AxisListType.X

P = 128
D = 1024
T = 512
KC = D // P
NT = T // P
SSM_HEADS, SSM_P, SSM_N, SSM_GROUPS = 16, 64, 64, 2
SSM_INNER = SSM_HEADS * SSM_P
HPG = SSM_HEADS // SSM_GROUPS
CONV_K = 4
XBC = SSM_INNER + 2 * SSM_GROUPS * SSM_N
XBC_C = XBC // P
FOX_HEADS = 8
SB_HEADS, SB_DIM = 16, 64
DW_K = 31
PAD = DW_K - 1
PE_TAPS = 10
FFN = 2816
FC = FFN // P
FCONV_K = 3
PLE = 256
PC = PLE // P
LN_EPS, RMS_EPS = 1e-5, 1e-6
ALPHA = float((2.0 * 2) ** 0.25)
NEG = -1e30
HALF_ULP = 2.0 ** -24

Z0 = 0
XBC0 = Z0 + SSM_INNER
DT0 = XBC0 + XBC
Q0 = DT0 + SSM_HEADS
K0 = Q0 + D
V0 = K0 + D
ZA0 = V0 + D
FL0 = ZA0 + D
G0 = FL0 + FOX_HEADS
SMALL = 32 + FOX_HEADS

DOWN_S = 3
STAGES = [("xbc", XBC_C // 2), ("z", 4), ("q", 4), ("ssm_out", 8), ("k", 4), ("v", 4), ("za", 4), ("att_out", 8),
          ("w_out", 4), ("pw1", 8), ("pw2", 4), ("gate0", 4), ("up0", FC), ("down0", 4 * DOWN_S),
          ("q1", 4), ("k1", 4), ("v1", 4), ("wo", 4), ("gate1", 4), ("up1", FC), ("down1", 4 * DOWN_S)]
SLOT0, GROUP0 = {}, {}
_g = _b = 0
for _name, _n in STAGES:
    SLOT0[_name], GROUP0[_name] = _g, _b
    _g += _n
    _b += _n // DOWN_S if _name.startswith("down") else _n
NSLOTS = _g
COUNT = dict(STAGES)

PCOL, _c = {}, 0
for _name, _n in [("c", KC), ("norm_w", KC), ("b_ada", 3 * KC), ("conv_w", CONV_K * XBC_C), ("conv_b", XBC_C),
                  ("d_skip", KC), ("ssm_norm_w", KC), ("b_gate", 2 * KC), ("final_norm_w", KC), ("pw1_b", 2 * KC),
                  ("dw_w", DW_K * KC), ("dw_b", KC), ("ln_g", KC), ("ln_b", KC), ("pw2_b", KC), ("mix_g", 2 * KC),
                  ("mix_b", 2 * KC), ("fconv_w", 2 * FCONV_K * FC), ("fconv_b", 2 * FC), ("out_g", 2 * KC),
                  ("out_b", 2 * KC), ("small_b", 1), ("a_log", 1)]:
    PCOL[_name] = _c
    _c += _n
NPAR = _c


class Step:

    def __init__(self, first, turn=0):
        self.first, self.turn = first, turn

    def val(self, mul=1, add=0):
        return mul * self.first + add + 2 * mul * self.turn

    def half(self, mul=1, add=0):
        return (mul * self.first + add) // 2 + mul * self.turn

    def odd(self, mul=1, add=0):
        return (mul * self.first + add) % 2


class Chain:

    def __init__(self, eng, sem):
        self.eng, self.sem, self.base, self.k = eng, sem, 0, 0

    def did(self, ins):
        ins.then_inc(self.sem, 1)
        self.k += 1

    def settle(self, but=0):
        self.eng.wait_ge(self.sem, self.base + self.k - but)


def steps(eng, chain, n, per, body, head=0, tail=0):
    tail += (n - head - tail) % 2
    begin = chain.base + chain.k if chain else 0

    def one(s):
        if chain:
            chain.base, chain.k = begin + s.val(per), 0
        body(s)
        assert not chain or chain.k == per, (chain.k, per)

    for i in range(head):
        one(Step(i))
    turns = (n - head - tail) // 2
    if turns > 0:
        with eng.Fori(0, turns) as t:
            for i in range(2):
                one(Step(head + i, t))
    for i in range(n - tail, n):
        one(Step(i))
    if chain:
        chain.base, chain.k = begin + per * n, 0


def build(nc, w, w_ada, w_small, w_ple, p_t, x_t, par, out):
    with ExitStack() as ctx:
        KB = 1024
        base = (nc.sbuf_base + 31) // 32 * 32

        def at(name, kb, shape, dt=F32):
            return nc.alloc_sbuf_tensor_at(name, shape, dt, offset=base + int(kb * KB))

        def sem(name):
            return ctx.enter_context(nc.semaphore(name))

        X = at("X", 0, [P, KC, T])
        H = at("H", 16, [P, KC, T], F32R)
        L = at("L", 32, [P, KC, T], F32R)
        RAW = at("RAW", 48, [P, 2, 16, P])
        WH = at("WH", 64, [P, 2, 16, P], F32R)
        WL = at("WL", 80, [P, 2, 16, P], F32R)
        A = 96
        TT = at("TT", 188, [P, 4, T])
        CS = at("CS", 196, [P, T])
        MISC = 198
        ADA = [at(f"ADA{k}", A + 12 * k if k < 7 else 32, [P, 3 * D]) for k in range(KC)]
        ADAS = at("ADAS", 16, [P, 3 * D])
        XN = at("XN", A + 36, [P, KC, T])
        XC = at("XC", A + 0, [P, XBC_C, T])
        CE = at("CE", A + 20, [P, HPG, T])
        XD = at("XD", A + 36, [P, NT, SSM_INNER])
        XDD = at("XDD", A + 52, [P, NT, SSM_INNER])
        ST = at("ST", A + 68, [P, 3, T])
        SELE = at("SELE", A + 68, [P, HPG, P], F32R)
        BTOK = at("BTOK", A + 74, [P, NT, P])
        CBM = at("CBM", A + 76, [P, 2, T])
        MT = at("MT", A + 80, [P, 2, T])
        SM = at("SM", A + 84, [P, 4, T])
        ZS = at("ZS", A + 36, [P, KC, T])
        YH = at("YH", A + 68, [P, KC, T], F32R)
        YL = at("YL", A + 20, [P, KC, T], F32R)
        P1 = at("P1", A + 36, [P, KC, T])
        QK = at("QK", A + 52, [P, 2 * KC, T])
        VTOK = at("VTOK", A + 0, [P, NT, D])
        PT = at("PT", A + 84, [P, NT, T])
        ZA = at("ZA", A + 0, [P, KC, T])
        MH = at("MH", A + 0, [P, KC, T], F32R)
        ML = at("ML", A + 52, [P, KC, T], F32R)
        SBC = sum(T - P * k for k in range(NT))
        EX = [at(f"EX{i}", A + 36 + 5 * i, [P, SBC]) for i in range(2)]
        AT = [at("AT0", A + 46, [P, SBC]), at("AT1", A + 84, [P, SBC])]
        HC = at("HC", A + 0, [P, KC, PAD + T])
        CV = at("CV", A + 20, [P, KC, T])
        DG = at("DG", A + 36, [P, 2, 2, PE_TAPS, P], F32R)
        CVB = at("CVB", A + 60, [P, 1, T])
        DW = at("DW", A + 62, [P, 2, PE_TAPS * KC], F32R)
        DWC = at("DWC", A + 66, [P, 2, 2, PE_TAPS])
        HCH = at("HCH", A + 68, [P, 2, PAD + T], F32R)
        HCL = at("HCL", A + 73, [P, 2, PAD + T], F32R)
        FH = at("FH", A + 0, [P, FC, T], F32R)
        FL = at("FL", A + 44, [P, FC, T], F32R)
        PPL = at("PPL", A + 88, [P, PC, T], F32R)
        PWR = at("PWR", A + 36, [P, PC, D])
        WPH = at("WPH", A + 44, [P, PC, D], F32R)
        WPL = at("WPL", A + 52, [P, PC, D], F32R)
        PR = at("PR", A + 60, [P, PC, T])
        PPH = at("PPH", A + 64, [P, PC, T], F32R)
        PAR = at("PAR", MISC, [P, NPAR])
        o = MISC + NPAR * 4 / KB
        o = int(o * 32 + 1) / 32

        def small(name, shape, dt=F32):
            nonlocal o
            t = at(name, o, shape, dt)
            n = int(np.prod(shape[1:])) * (2 if dt == BF16 else 4)
            o += (n + 31) // 32 * 32 / KB
            return t

        IDENT = small("IDENT", [P, P])
        TRI = small("TRI", [P, P])
        IDB = small("IDB", [P, P], BF16)
        M_FOX = small("M_FOX", [P, P], BF16)
        M_SB = small("M_SB", [P, P], BF16)
        M_SSM = small("M_SSM", [P, P], BF16)
        ADAV = small("ADAV", [P, 3 * KC])
        GX = small("GX", [P, KC])
        CSIL = small("CSIL", [P, KC])
        COLS = small("COLS", [P, 6])
        MEANC, ONEC, NEGC, EPS_LN, EPS_RMS, SGN = (COLS[:, i:i + 1] for i in range(6))
        STAT = small("STAT", [P, 3, NT * FOX_HEADS])
        TOK = small("TOK", [P, 3, NT, SSM_HEADS])
        EL = small("EL", [P, HPG, NT])
        AEXP = small("AEXP", [P, 1])
        CSX = small("CSX", [P, T], F32R)
        SEL = small("SEL", [P, 64], F32R)
        assert base + o * KB <= nc.sbuf_usable_end, (o, (nc.sbuf_usable_end - base) / KB)
        SWR = at("SWR", A + 84, [P, KC, SMALL])
        SWH = at("SWH", A + 86, [P, KC, SMALL], F32R)
        SWL = at("SWL", A + 88, [P, KC, SMALL], F32R)

        PS = ctx.enter_context(nc.psum_tensor("PS", [P, 8, T], F32))
        NB, MB = PS[:, 4, :], PS[:, 5, :]

        def col(name, i=0, n=1):
            return PAR[:, PCOL[name] + i:PCOL[name] + i + n]

        def dcol(name, i):
            if isinstance(i, int):
                return col(name, i)
            return PAR[:, bass.ds(i + PCOL[name], 1)]

        def rows(t, i, n):
            return t[:, i:i + n, :] if isinstance(i, int) else t[:, bass.ds(i, n), :]

        par_in, x_in, sw_in, c_ready = sem("par_in"), sem("x_in"), sem("sw_in"), sem("c_ready")
        ada_in = [sem(f"ada_in{k}") for k in range(KC)]
        const_ready = sem("const_ready")
        act_own, dve_own, pool_own = sem("act_own"), sem("dve_own"), sem("pool_own")
        raw_in = [sem("raw_in0"), sem("raw_in1")]
        w_hi, w_lo = sem("w_hi"), sem("w_lo")
        slot_done = sem("slot_done")
        bank_free = sem("bank_free")
        sw_hi, sw_lo = sem("sw_hi"), sem("sw_lo")
        ada_sum, ada_ps, ada_ready = sem("ada_sum"), sem("ada_ps"), sem("ada_ready")
        sq_ready, sq_used, std_ready = sem("sq_ready"), sem("sq_used"), sem("std_ready")
        t_ready, hi_ready, h_ready = sem("t_ready"), sem("hi_ready"), sem("h_ready")
        sum_ready, mean_ready, cen_ready = sem("sum_ready"), sem("mean_ready"), sem("cen_ready")
        xc_ready = sem("xc_ready")
        dt_ps, dt_u, dt_e, dt_w, dt_l, dt_x, dt_d, dt_rows = (sem(s) for s in (
            "dt_ps", "dt_u", "dt_e", "dt_w", "dt_l", "dt_x", "dt_d", "dt_rows"))
        tok_ps, tok_ready, bt_ps, bt_ready, cb_ps, cb_ready = (sem(s) for s in (
            "tok_ps", "tok_ready", "bt_ps", "bt_ready", "cb_ps", "cb_ready"))
        xt_ps, xt_used, e_ps, e_exp, ce_ready, st_ps, st_ready = (sem(s) for s in (
            "xt_ps", "xt_used", "e_ps", "e_exp", "ce_ready", "st_ps", "st_ready"))
        seg_ps, seg_ready, seg_exp, mt_ready, y_ps, y_used = (sem(s) for s in (
            "seg_ps", "seg_ready", "seg_exp", "mt_ready", "y_ps", "y_used"))
        zs_ready, yz_ready = sem("zs_ready"), sem("yz_ready")
        sig_ready = sem("sig_ready")
        lg_ready, nm_ready, p_exp, pn_ready, tr_ready, pt_ready, pv_done, ot_ready = (sem(s) for s in (
            "lg_ready", "nm_ready", "p_exp", "pn_ready", "tr_ready", "pt_ready", "pv_done", "ot_ready"))
        za_ready, ya_ready, ya_hi, ya_lo = (sem(s) for s in ("za_ready", "ya_ready", "ya_hi", "ya_lo"))
        mg_ready, mg_hi, mg_lo = sem("mg_ready"), sem("mg_hi"), sem("mg_lo")
        hc_hi, hc_lo, dw_hi, dwc_ready, dg_ready, cp_ps = (sem(s) for s in (
            "hc_hi", "hc_lo", "dw_hi", "dwc_ready", "dg_ready", "cp_ps"))
        sele_ready = sem("sele_ready")
        cs_ready, csx_hi, csx_lo = sem("cs_ready"), sem("csx_hi"), sem("csx_lo")
        ple_in, ple_hi, ple_lo, pg_ready = sem("ple_in"), sem("ple_hi"), sem("ple_lo"), sem("pg_ready")
        gc_ready, sl_ready, ff_hi, ff_lo = (sem(s) for s in ("gc_ready", "sl_ready", "ff_hi", "ff_lo"))
        sz_ps, sz_exp, sp_ready, tri_done, a_ready, sb_pv, so_ready = (sem(s) for s in (
            "sz_ps", "sz_exp", "sp_ready", "tri_done", "a_ready", "sb_pv", "so_ready"))
        so_hi, so_lo = sem("so_hi"), sem("so_lo")
        out_ready, out_done = sem("out_ready"), sem("out_done")

        N_X, N_SSM, N_FINAL, N_CONV, N_MIX0, N_OUT0, N_MIX1, N_OUT1 = range(8)
        LN_OF = {N_CONV: 0, N_MIX0: 1, N_OUT0: 2, N_MIX1: 3, N_OUT1: 4}
        SIG0, _n = {}, 0
        for s in ("ssm_out", "att_out", "pw1", "gate0", "gate1"):
            SIG0[s] = _n
            _n += COUNT[s]
        Q_PART = [range(0), range(0, 4), range(4, 8), range(0)]
        SB_OFF = {0: 0, 1: T, 3: T + 3 * P, 2: 2 * T}

        block = ctx.enter_context(nc.Block())

        @block.gpsimd
        def _(pool):
            own = Chain(pool, pool_own)
            own.did(nc.gpsimd.memset(IDENT[:], 0.0))
            own.did(nc.gpsimd.memset(IDB[:], 0.0))
            own.did(nc.gpsimd.memset(M_FOX[:], 0.0))
            own.did(nc.gpsimd.memset(M_SB[:], 0.0))
            own.did(nc.gpsimd.memset(M_SSM[:], 0.0))
            own.did(nc.gpsimd.memset(TRI[:], -1.0))
            own.did(nc.gpsimd.memset(CS[:], 0.0))
            for c, v in ((MEANC, 1.0 / D), (ONEC, 1.0), (NEGC, -1.0), (EPS_LN, LN_EPS), (EPS_RMS, RMS_EPS)):
                own.did(nc.gpsimd.memset(c, v))
            own.did(nc.gpsimd.memset(SGN[0:32], 1.0))
            own.settle()
            own.did(nc.gpsimd.memset(SGN[32:64], -1.0))
            own.settle()

            def select(t, op, fill, cm, step):
                nc.gpsimd.affine_select(out=t[:], in_=t[:], compare_op=op, fill=fill, base=0,
                                        pattern=[[step, P]], channel_multiplier=cm).then_inc(const_ready, 1)

            select(IDENT, ALU.not_equal, 1.0, 1, -1)
            select(IDB, ALU.not_equal, 1.0, 1, -1)
            select(M_FOX, ALU.is_ge, NEG, 1, -1)
            select(M_SB, ALU.is_gt, NEG, -1, 1)
            select(M_SSM, ALU.is_ge, NEG, -1, 1)
            select(TRI, ALU.is_ge, 0.0, 1, -1)

            pool.wait_ge(const_ready, 6)

            def diagonals(s):
                p = s.odd()
                pool.wait_ge(dwc_ready, s.val(1, 1))
                for part in range(2):
                    for k in range(PE_TAPS):
                        ins = nc.gpsimd.tensor_scalar(DG[:, p, part, k, :], IDENT[:], DWC[:, p, part, k:k + 1], None,
                                                      ALU.mult)
                ins.then_inc(dg_ready, 1)
            for m in range(KC):
                diagonals(Step(m))

        @block.sync
        def _(sp):
            sp.dma_start(PAR[:], par).then_inc(par_in, 16)
            sp.dma_start(X[:], x_t).then_inc(x_in, 16)
            sp.dma_start(SWR[:], w_small).then_inc(sw_in, 16)
            for g in range(2):
                sp.dma_start(RAW[:, g], w[g]).then_inc(raw_in[g], 16)
            n = NSLOTS - 2
            with sp.Fori(0, n // 2) as t:
                for i in range(2):
                    sp.wait_ge(w_lo, 2 * t + i + 1)
                    sp.dma_start(RAW[:, i], w[2 * t + (i + 2)]).then_inc(raw_in[i], 16)
            if n % 2:
                sp.wait_ge(w_lo, n)
                sp.dma_start(RAW[:, 0], w[NSLOTS - 1]).then_inc(raw_in[0], 16)
            for m in range(KC):
                sp.wait_ge(out_ready, m + 1)
                sp.dma_start(out[:, m, :], X[:, m, :]).then_inc(out_done, 16)
            sp.wait_ge(out_done, 16 * KC)

        @block.tensor
        def _(pe):
            own = None

            def product(ps, wh, wl, xh, xl, start, stop):
                nc.tensor.matmul(ps, wh, xh, start=start, stop=False)
                nc.tensor.matmul(ps, wh, xl, start=False, stop=False)
                return nc.tensor.matmul(ps, wl, xh, start=False, stop=stop)

            def slot(s, stage, units, ready=None, last=True, mul=1, part=0, ks=KC, group=None):
                g0 = SLOT0[stage] + part
                p = s.odd(mul, g0)
                b = s.odd(1, GROUP0[stage])
                pe.wait_ge(w_lo, s.val(mul, g0 + 1))
                if part == 0 and not (isinstance(s.val(), int) and s.val(1, GROUP0[stage]) < 2):
                    pe.wait_ge(bank_free, s.val(1, GROUP0[stage] - 1))
                for k in range(ks):
                    if ready:
                        pe.wait_ge(ready[0], ready[1](k))
                    for u, (xh, xl) in enumerate(units):
                        i = u * KC + k
                        mm = product(PS[:, 2 * b + u, :], WH[:, p, i, :], WL[:, p, i, :], xh[:, part * KC + k, :],
                                     xl[:, part * KC + k, :], part == 0 and k == 0, last and k == ks - 1)
                mm.then_inc(slot_done, 1)

            def gemm(stage, units, ready=None):
                def one(s):
                    first = isinstance(s.val(), int) and s.val() == 0
                    slot(s, stage, units, ready if first else None)
                steps(pe, None, COUNT[stage], 0, one, head=2 if stage == "xbc" else 1 if ready else 0)

            hl, ylh = (H, L), (YH, YL)

            def normed(n):
                return h_ready, lambda k: KC * n + k + 1

            def token_major(stage):
                def one(s):
                    p, b = s.odd(1, SLOT0[stage]), s.odd(1, GROUP0[stage])
                    pe.wait_ge(w_lo, s.val(1, SLOT0[stage] + 1))
                    pe.wait_ge(bank_free, s.val(1, GROUP0[stage] - 1))
                    for k in range(KC):
                        wh, wl = WH[:, p, k::KC, :], WL[:, p, k::KC, :]
                        for c in range(NT):
                            cc = slice(c * P, (c + 1) * P)
                            ps = PS[:, 2 * b + c // 2, (c % 2) * 2 * P:(c % 2 + 1) * 2 * P]
                            nc.tensor.matmul(ps, H[:, k, cc], wh, start=k == 0 and c % 2 == 0, stop=False,
                                             skip_group_check=True)
                            nc.tensor.matmul(ps, H[:, k, cc], wl, start=False, stop=False, skip_group_check=True)
                            mm = nc.tensor.matmul(ps, L[:, k, cc], wh, start=False, stop=k == KC - 1,
                                                  skip_group_check=True)
                    mm.then_inc(slot_done, 1)
                steps(pe, None, COUNT[stage], 0, one)

            def norm(n):
                for m in range(KC):
                    pe.wait_ge(sq_ready, KC * n + m + 1)
                    nc.tensor.matmul(NB, MEANC.to_broadcast([P, P]), TT[:, m % 2, :], start=m == 0,
                                     stop=m == KC - 1).then_inc(sq_used, 1)

            def mean(n):
                pe.wait_ge(sum_ready, LN_OF[n] + 1)
                nc.tensor.matmul(MB, MEANC.to_broadcast([P, P]), TT[:, 2, :], start=True,
                                 stop=True).then_inc(mean_ready, 1)

            pe.wait_ge(const_ready, 6)
            norm(N_X)
            pe.wait_ge(ada_sum, 1)
            for m in range(3 * KC):
                mm = nc.tensor.matmul(PS[:, 5, m:m + 1], ADAS[:, m * P:(m + 1) * P], ONEC, start=True, stop=True)
            mm.then_inc(ada_ps, 1)

            gemm("xbc", (hl, hl), normed(N_X))
            pe.wait_ge(sw_lo, 1)
            for k in range(KC):
                mm = product(PS[0:SMALL, 4, :], SWH[:, k, :], SWL[:, k, :], H[:, k, :], L[:, k, :], k == 0, k == KC - 1)
            mm.then_inc(dt_ps, 1)

            def xt(i):
                c, half = divmod(i, 2)
                if i >= 2:
                    pe.wait_ge(xt_used, i - 1)
                for j in range(4):
                    mm = nc.tensor.transpose(PS[:, 6 + i % 2, j * P:(j + 1) * P],
                                             XC[:, 4 * half + j, c * P:(c + 1) * P], IDENT[:])
                mm.then_inc(xt_ps, 1)

            pe.wait_ge(xc_ready, COUNT["xbc"])
            xt(0)
            xt(1)
            pe.wait_ge(dt_u, 1)
            for c in range(NT):
                mm = nc.tensor.transpose(PS[:, 4, c * P:(c + 1) * P], XC[:, KC, c * P:(c + 1) * P], IDENT[:])
            mm.then_inc(bt_ps, 1)
            pe.wait_ge(dt_rows, 1)
            src = [CS, SM[:, 3, :], SM[:, 1, :]]
            for i in range(3):
                for c in range(NT):
                    j = (i * NT + c) * SSM_HEADS
                    mm = nc.tensor.transpose(PS[:, 5, j:j + SSM_HEADS], src[i][0:SSM_HEADS, c * P:(c + 1) * P],
                                             IDENT[0:SSM_HEADS, 0:SSM_HEADS])
            mm.then_inc(tok_ps, 1)
            for i in range(2, 2 * NT):
                xt(i)
            pe.wait_ge(bt_ready, 1)
            pe.wait_ge(tok_ready, 1)
            for g in range(SSM_GROUPS):
                r = slice(g * SSM_N, (g + 1) * SSM_N)
                for c in range(NT):
                    cc = slice(c * P, (c + 1) * P)
                    mm = nc.tensor.matmul(PS[:, 4 + g, cc], XC[r, KC, cc], XC[r, KC + 1, cc], start=True, stop=True)
                mm.then_inc(cb_ps, 1)
            pe.wait_ge(csx_lo, 1)
            pe.wait_ge(sele_ready, 1)
            for r in range(HPG):
                if r < 2:
                    pe.wait_ge(xt_used, 2 * NT - 1 + r)
                else:
                    pe.wait_ge(e_exp, r - 1)
                nc.tensor.matmul(PS[:, 6 + r % 2, :], SELE[:, r, :], CSX[:], start=True, stop=True).then_inc(e_ps, 1)
            pe.wait_ge(cb_ready, 2)
            for c in range(NT - 1):
                if c:
                    pe.wait_ge(st_ready, c)
                for g in range(SSM_GROUPS):
                    mm = nc.tensor.matmul(PS[g * 64:g * 64 + 64, 5, :], BTOK[:, c, g * SSM_N:(g + 1) * SSM_N],
                                          XDD[:, c, g * T:(g + 1) * T], start=True, stop=True)
                mm.then_inc(st_ps, 1)

            def seg(h):
                if h < 2:
                    pe.wait_ge(e_exp, HPG - 1 + h)
                else:
                    pe.wait_ge(seg_ready, h - 1)
                ps = PS[:, 6 + h % 2, :]
                nc.tensor.matmul(ps, SEL[:, h:h + 1].to_broadcast([P, P]), CSX[:], start=True, stop=False)
                nc.tensor.matmul(ps, IDB[:], M_SSM[:].unsqueeze(1).to_broadcast([P, NT, P]), start=False,
                                 stop=True).then_inc(seg_ps, 1)

            def y(h):
                i, u = divmod(h, 2)
                g, r = divmod(h, HPG)
                pe.wait_ge(mt_ready, h + 1)
                if u == 0 and i >= 2:
                    pe.wait_ge(y_used, i - 1)
                if h == 0:
                    pe.wait_ge(st_ready, NT - 1)
                    pe.wait_ge(ce_ready, HPG)
                for c in range(NT):
                    cc = slice(c * P, (c + 1) * P)
                    ps = PS[u * 64:u * 64 + 64, 4 + i % 2, cc]
                    mm = nc.tensor.matmul(ps, XD[:, c, h * 64:h * 64 + 64], MT[:, h % 2, cc], start=c == 0,
                                          stop=True, skip_group_check=True)
                    if c:
                        mm = nc.tensor.matmul(ps, ST[g * 64:g * 64 + 64, c - 1, r * 64:r * 64 + 64],
                                              CE[g * 64:g * 64 + 64, r, cc], start=False, stop=True,
                                              skip_group_check=True)
                mm.then_inc(y_ps, 1)

            seg(0)
            for h in range(SSM_HEADS):
                if h + 1 < SSM_HEADS:
                    seg(h + 1)
                y(h)
            gemm("z", (hl, hl))
            for j in range(COUNT["q"]):
                slot(Step(j), "q", (hl, hl))
                if j == 0:
                    norm(N_SSM)
            gemm("ssm_out", (ylh, hl), normed(N_SSM))
            gemm("k", (hl, hl))
            token_major("v")

            def logits(i):
                h, qb = divmod(i, NT)
                n = (qb + 1) * P
                if i < 2:
                    pe.wait_ge(bank_free, GROUP0["v"] + COUNT["v"])
                else:
                    pe.wait_ge(p_exp, i - 1)
                ps = PS[:, 4 + i % 2, :]
                nc.tensor.matmul(ps[:, qb * P:n], IDB[:], M_FOX[:], start=True, stop=False, skip_group_check=True)
                nc.tensor.matmul(ps[:, 0:n], QK[:, h, qb * P:n], QK[:, KC + h, 0:n], start=False, stop=False,
                                 skip_group_check=True)
                nc.tensor.matmul(ps[:, 0:n], SEL[:, 32 + h:33 + h].to_broadcast([P, P]), CSX[:, 0:n], start=False,
                                 stop=True, skip_group_check=True).then_inc(lg_ready, 1)

            def turn(i):
                h, qb = divmod(i, NT)
                pe.wait_ge(pn_ready, i + 1)
                if i:
                    pe.wait_ge(pt_ready, i)
                for kc in range(qb + 1):
                    mm = nc.tensor.transpose(PS[:, 6, kc * P:(kc + 1) * P], TT[:, i % 2, kc * P:(kc + 1) * P], IDENT[:])
                mm.then_inc(tr_ready, 1)

            def values(h):
                pe.wait_ge(pt_ready, NT * (h + 1))
                if h:
                    pe.wait_ge(ot_ready, h)
                for kc in range(NT):
                    mm = nc.tensor.matmul(PS[:, 7, kc * P:T], VTOK[:, kc, h * P:(h + 1) * P], PT[:, kc, kc * P:T],
                                          start=kc == 0, stop=True, skip_group_check=True)
                mm.then_inc(pv_done, 1)

            n = NT * FOX_HEADS
            for i in range(n + 2):
                if i < n:
                    logits(i)
                if 1 <= i <= n:
                    turn(i - 1)
                if i >= 2 and (i - 2) % NT == NT - 1:
                    values((i - 2) // NT)

            gemm("za", (hl, hl))
            gemm("att_out", (ylh, hl), (ya_lo, lambda k: k // 2 + 1))
            gemm("w_out", ((MH, ML), (MH, ML)), (mg_lo, lambda k: k + 1))
            norm(N_FINAL)

            def taps(s, ahead):
                p = s.odd(1, -ahead)
                pe.wait_ge(dg_ready, s.val(1, 1 - ahead))
                pe.wait_ge(hc_lo, s.val(1, 1 - ahead))
                for k in range(PE_TAPS):
                    mm = product(PS[:, 6 + p, :], DG[:, p, 0, k, :], DG[:, p, 1, k, :], HCH[:, p, k:k + T],
                                 HCL[:, p, k:k + T], k == 0, k == PE_TAPS - 1)
                mm.then_inc(cp_ps, 1)

            def pw1(s):
                first = isinstance(s.val(), int) and s.val() == 0
                slot(s, "pw1", (hl, hl), normed(N_FINAL) if first else None)
                if not first:
                    taps(s, 1)
            steps(pe, None, KC, 0, pw1, head=1)
            taps(Step(KC - 1), 0)
            mean(N_CONV)
            norm(N_CONV)
            gemm("pw2", (ylh, ylh), normed(N_CONV))

            def feed_forward(layer, n_mix, n_out):
                mean(n_mix)
                norm(n_mix)
                gate = f"gate{layer}"
                pe.wait_ge(ple_lo, layer + 1)
                for j in range(COUNT[gate]):
                    s = Step(j)
                    slot(s, gate, (hl, hl), normed(n_mix) if j == 0 else None)
                    b = s.odd(1, GROUP0[gate])
                    for u in range(2):
                        m = 2 * j + u
                        for k in range(PC):
                            mm = product(PS[:, 4 + 2 * b + u, :], WPH[:, k, m * P:(m + 1) * P],
                                         WPL[:, k, m * P:(m + 1) * P], PPH[:, k, :], PPL[:, k, :], k == 0, k == PC - 1)
                    mm.then_inc(pg_ready, 1)
                gemm(f"up{layer}", (hl, hl))
                down = f"down{layer}"

                def one(s):
                    for part in range(DOWN_S):
                        pe.wait_ge(ff_lo, FC * layer + min(KC * (part + 1), FC))
                        slot(s, down, ((FH, FL), (FH, FL)), last=part == DOWN_S - 1, mul=DOWN_S, part=part,
                             ks=min(KC, FC - part * KC))
                steps(pe, None, 4, 0, one)
                mean(n_out)
                norm(n_out)

            feed_forward(0, N_MIX0, N_OUT0)
            gemm("q1", (hl, hl), normed(N_OUT0))
            gemm("k1", (hl, hl))
            token_major("v1")

            def zs(h):
                pb, c = (h % 2) * 64, h // 2
                r = slice(pb, pb + 64)
                if h == 0:
                    pe.wait_ge(bank_free, GROUP0["v1"] + COUNT["v1"])
                if h >= 2:
                    pe.wait_ge(a_ready, h - 1)
                flat = PS[:, 4 * (h % 2):4 * (h % 2) + 3, :].rearrange("p b t -> p (b t)")
                for kc in (0, 1, 3, 2):
                    w = T - kc * P
                    reg = flat[:, SB_OFF[kc]:SB_OFF[kc] + w]
                    nc.tensor.matmul(reg, QK[r, KC + c, kc * P:(kc + 1) * P], QK[r, c, kc * P:T], start=kc != 3,
                                     stop=True, skip_group_check=True)
                    mm = nc.tensor.matmul(reg[:, 0:P], IDB[:], M_SB[:], start=False, stop=True, skip_group_check=True)
                mm.then_inc(sz_ps, 1)

            def tri(h):
                pe.wait_ge(sp_ready, h + 1)
                flat = PS[:, 4 * (h % 2):4 * (h % 2) + 3, :].rearrange("p b t -> p (b t)")
                ex = EX[h % 2]
                for kc in range(NT):
                    w = T - kc * P
                    mm = nc.tensor.matmul(flat[:, SB_OFF[kc]:SB_OFF[kc] + w], TRI[:], ex[:, SB_OFF[kc]:SB_OFF[kc] + w],
                                          start=False, stop=True, skip_group_check=True)
                    for jc in range(kc + 1, NT):
                        wj = T - jc * P
                        o = SB_OFF[kc] + (jc - kc) * P
                        mm = nc.tensor.matmul(flat[:, o:o + wj], NEGC.to_broadcast([P, P]),
                                              ex[:, SB_OFF[jc]:SB_OFF[jc] + wj], start=False, stop=True,
                                              skip_group_check=True)
                mm.then_inc(tri_done, 1)

            def sb_values(h):
                pb = (h % 2) * 64
                pe.wait_ge(a_ready, h + 1)
                if h >= 2:
                    pe.wait_ge(so_ready, h - 1)
                for kc in range(NT):
                    mm = nc.tensor.matmul(PS[pb:pb + 64, 4 * (h % 2) + 3, kc * P:T], VTOK[:, kc, h * 64:h * 64 + 64],
                                          AT[h % 2][:, SB_OFF[kc]:SB_OFF[kc] + T - kc * P], start=kc == 0,
                                          stop=True, skip_group_check=True)
                mm.then_inc(sb_pv, 1)

            for i in range(SB_HEADS + 2):
                if i < SB_HEADS:
                    zs(i)
                if 1 <= i <= SB_HEADS:
                    tri(i - 1)
                if i >= 2:
                    sb_values(i - 2)
            gemm("wo", (ylh, ylh), (so_lo, lambda k: k + 1))
            feed_forward(1, N_MIX1, N_OUT1)

        @block.scalar
        def _(act):
            own = Chain(act, act_own)
            a = nc.scalar.activation

            def split_hi(s, mul, g):
                if isinstance(s.val(), int) and s.val(mul, g) >= NSLOTS:
                    return
                p = s.odd(mul, g)
                act.wait_ge(raw_in[p], 16 * s.half(mul, g) + 16)
                if not (isinstance(s.val(), int) and s.val(mul, g) < 2):
                    act.wait_ge(slot_done, s.val(mul, g - 1))
                a(WH[:, p], RAW[:, p], ACT.Copy).then_inc(w_hi, 1)

            def slots(stage, body, per=0, tail=0, head=0):
                g0 = SLOT0[stage]

                def one(s):
                    split_hi(s, 1, g0 + 1)
                    body(s, s.odd(1, GROUP0[stage]))
                steps(act, own, COUNT[stage], per, one, tail=tail, head=head)

            def evacuated(s, stage):
                act.wait_ge(slot_done, s.val(1, SLOT0[stage] + 1))

            def squares(n, src, ready=None):
                for m in range(KC):
                    if ready:
                        act.wait_ge(ready[0], ready[1] + m + 1)
                    if KC * n + m >= 2:
                        act.wait_ge(sq_used, KC * n + m - 1)
                    a(TT[:, m % 2, :], src[:, m, :], ACT.Square).then_inc(sq_ready, 1)
                act.wait_ge(sq_used, KC * (n + 1))
                a(TT[:, 2, :], NB, ACT.Sqrt, bias=EPS_LN if n in LN_OF else EPS_RMS).then_inc(std_ready, 1)

            def norm_hi(n, dst, hi, bias=None, func=ACT.Identity, ms=range(KC)):
                for m in ms:
                    act.wait_ge(t_ready, KC * n + m + 1)
                    if bias is None:
                        a(hi[:, m, :], dst[:, m, :], ACT.Copy).then_inc(hi_ready, 1)
                    else:
                        a(hi[:, m, :], dst[:, m, :], func, bias=bias(m))
                        a(dst[:, m, :], dst[:, m, :], func, bias=bias(m)).then_inc(hi_ready, 1)

            for k in range(KC):
                act.dma_start(ADA[k][:], w_ada[k]).then_inc(ada_in[k], 16)
            act.wait_ge(par_in, 16)
            a(CSIL[:], col("c", 0, KC), ACT.Silu).then_inc(c_ready, 1)
            a(AEXP[0:SSM_HEADS], PAR[0:SSM_HEADS, PCOL["a_log"]:PCOL["a_log"] + 1], ACT.Exp).then_inc(c_ready, 1)
            act.wait_ge(sw_in, 16)
            a(SWH[:], SWR[:], ACT.Copy).then_inc(sw_hi, 1)
            act.wait_ge(x_in, 16)
            act.wait_ge(const_ready, 6)
            squares(N_X, X)
            split_hi(Step(0), 1, 0)
            act.wait_ge(ada_ready, 1)
            norm_hi(N_X, XN, H, lambda m: ADAV[:, m:m + 1])

            def xbc(s, p):
                act.wait_ge(bank_free, s.val(1, GROUP0["xbc"] + 1))
                xc = rows(XC, s.val(2), 2)
                a(xc, xc, ACT.Silu).then_inc(xc_ready, 1)
            slots("xbc", xbc, head=2)

            act.wait_ge(dt_u, 2)
            a(SM[0:SMALL, 1, :], SM[0:SMALL, 1, :], ACT.Exp).then_inc(dt_e, 1)
            act.wait_ge(dt_w, 1)
            a(SM[0:SMALL, 3, :], SM[0:SMALL, 2, :], ACT.Ln).then_inc(dt_l, 1)
            act.wait_ge(bt_ps, 1)
            a(BTOK[:].rearrange("p c n -> p (c n)"), PS[:, 4, :], ACT.Copy).then_inc(bt_ready, 1)
            act.wait_ge(cs_ready, 1)
            a(CSX[0:64], CS[0:64], ACT.Copy).then_inc(csx_hi, 1)
            act.wait_ge(dt_x, 1)
            a(SM[0:SSM_HEADS, 1, :], SM[0:SSM_HEADS, 1, :], ACT.Exp).then_inc(dt_d, 1)
            act.wait_ge(cb_ps, 2)
            for g in range(SSM_GROUPS):
                a(CBM[:, g, :], PS[:, 4 + g, :], ACT.Copy).then_inc(cb_ready, 1)
            for r in range(HPG):
                act.wait_ge(e_ps, r + 1)
                a(EL[:, r, :], PS[:, 6 + r % 2, P - 1::P], ACT.Exp)
                a(CE[:, r, :], PS[:, 6 + r % 2, :], ACT.Exp).then_inc(e_exp, 1)
            for h in range(SSM_HEADS):
                act.wait_ge(seg_ready, h + 1)
                a(MT[:, h % 2, :], MT[:, h % 2, :], ACT.Exp).then_inc(seg_exp, 1)

            def z(s, p):
                evacuated(s, "z")
                act.wait_ge(bank_free, s.val(1, GROUP0["z"]))
                a(rows(ZS, s.val(2), 2), PS[:, 2 * p:2 * p + 2, :], ACT.Silu).then_inc(bank_free, 1)
            act.wait_ge(y_ps, SSM_HEADS)
            slots("z", z)

            def gates(stage, bias0, name):
                def body(s, p):
                    evacuated(s, stage)
                    a(TT[:, p, :], PS[:, 2 * p + 1, :], ACT.Sigmoid,
                      bias=dcol(name, s.val(1, bias0))).then_inc(sig_ready, 1)
                return body

            def copy(stage, dst, m0, scale):
                def body(s, p):
                    evacuated(s, stage)
                    act.wait_ge(bank_free, s.val(1, GROUP0[stage]))
                    a(rows(dst, s.val(2, m0), 2), PS[:, 2 * p:2 * p + 2, :], ACT.Copy,
                      scale=scale).then_inc(bank_free, 1)
                return body

            def v_copy(stage):
                def body(s, p):
                    evacuated(s, stage)
                    f = s.val(2 * P)
                    dst = VTOK[:, :, f:f + 2 * P] if isinstance(f, int) else VTOK[:, :, bass.ds(f, 2 * P)]
                    a(dst, PS[:, 2 * p:2 * p + 2, :].rearrange("p b (c f) -> p (b c) f", c=2),
                      ACT.Copy).then_inc(bank_free, 1)
                return body

            for j in range(COUNT["q"]):
                split_hi(Step(j), 1, SLOT0["q"] + 1)
                if j == 0:
                    squares(N_SSM, XC, (yz_ready, 0))
                else:
                    norm_hi(N_SSM, XC, YH, ms=Q_PART[j])
                copy("q", QK, 0, float(P ** -0.5))(Step(j), j % 2 ^ GROUP0["q"] % 2)
            slots("ssm_out", gates("ssm_out", 0, "b_gate"))
            slots("k", copy("k", QK, KC, 1.0))
            slots("v", v_copy("v"))

            def p_turned(i):
                h, qb = divmod(i, NT)
                act.wait_ge(tr_ready, i + 1)
                if qb == 0 and h:
                    act.wait_ge(pv_done, h)
                a(PT[:, 0:qb + 1, qb * P:(qb + 1) * P],
                  PS[:, 6, 0:(qb + 1) * P].rearrange("p (k q) -> p k q", q=P), ACT.Copy).then_inc(pt_ready, 1)

            n = NT * FOX_HEADS
            for i in range(n + 1):
                if i < n:
                    w_ = (i % NT + 1) * P
                    act.wait_ge(nm_ready, i + 1)
                    if i >= 2:
                        act.wait_ge(tr_ready, i - 1)
                    a(TT[:, i % 2, 0:w_], PS[:, 4 + i % 2, 0:w_], ACT.Exp, bias=STAT[:, 0, i:i + 1],
                      accum_out=STAT[:, 1, i:i + 1]).then_inc(p_exp, 1)
                if i:
                    p_turned(i - 1)

            def za(s, p):
                evacuated(s, "za")
                act.wait_ge(bank_free, s.val(1, GROUP0["za"]))
                a(rows(ZA, s.val(2), 2), PS[:, 2 * p:2 * p + 2, :], ACT.Silu).then_inc(bank_free, 1)
                act.wait_ge(ya_ready, s.val(1, 1))
                a(rows(YH, s.val(2), 2), rows(QK, s.val(2), 2), ACT.Copy).then_inc(ya_hi, 1)
            slots("za", za)

            def att_out(s, p):
                gates("att_out", KC, "b_gate")(s, p)
                act.wait_ge(mg_ready, s.val(1, 1))
                a(rows(MH, s.val(), 1), rows(P1, s.val(), 1), ACT.Copy).then_inc(mg_hi, 1)
            slots("att_out", att_out)
            slots("w_out", lambda s, p: None)
            act.wait_ge(bank_free, GROUP0["w_out"] + COUNT["w_out"])
            squares(N_FINAL, X)
            norm_hi(N_FINAL, X, H)

            def load_ple(layer):
                act.dma_start(PWR[:], w_ple[layer]).then_inc(ple_in, 16)
                act.dma_start(PR[:], p_t[layer]).then_inc(ple_in, 16)

            def split_ple_hi(layer):
                act.wait_ge(ple_in, 32 * (layer + 1))
                a(WPH[:], PWR[:], ACT.Copy)
                a(PPH[:], PR[:], ACT.Copy).then_inc(ple_hi, 1)

            a(DW[:, 0, :], col("dw_w", 0, PE_TAPS * KC), ACT.Copy).then_inc(dw_hi, 1)

            def pw1(s, p):
                gates("pw1", KC, "pw1_b")(s, p)
                act.wait_ge(bank_free, s.val(1, GROUP0["pw1"] + 1))
                q = s.odd()
                a(HCH[:, q:q + 1, :], rows(HC, s.val(), 1), ACT.Copy).then_inc(hc_hi, 1)
            slots("pw1", pw1)
            act.wait_ge(sum_ready, LN_OF[N_CONV] + 1)
            load_ple(0)
            squares(N_CONV, CV, (cen_ready, KC * LN_OF[N_CONV]))
            norm_hi(N_CONV, CV, YH, lambda m: col("ln_b", m), ACT.Silu)
            split_ple_hi(0)
            slots("pw2", lambda s, p: None)

            def feed_forward(layer, n_mix, n_out):
                squares(n_mix, X, (cen_ready, KC * LN_OF[n_mix]))
                norm_hi(n_mix, X, H, lambda m: col("mix_b", KC * layer + m))
                gate = f"gate{layer}"

                def gate_body(s, p):
                    evacuated(s, gate)
                    act.wait_ge(bank_free, s.val(1, GROUP0[gate]))
                    a(TT[:, 0:2, :], PS[:, 2 * p:2 * p + 2, :], ACT.Sigmoid).then_inc(sig_ready, 1)
                slots(gate, gate_body)
                up = f"up{layer}"

                def up_body(s, p):
                    act.wait_ge(gc_ready, s.val(1, FC * layer + 1))
                    a(TT[:, p, :], TT[:, 3, :], ACT.Silu).then_inc(sl_ready, 1)
                    act.wait_ge(bank_free, s.val(1, GROUP0[up] + 1))
                    a(rows(FH, s.val(), 1), TT[:, 3:4, :], ACT.Copy).then_inc(ff_hi, 1)
                slots(up, up_body)
                down = f"down{layer}"

                def down_one(s):
                    for part in range(DOWN_S):
                        split_hi(s, DOWN_S, SLOT0[down] + part + 1)
                steps(act, own, 4, 0, down_one, tail=2 if layer else 0)
                squares(n_out, X, (cen_ready, KC * LN_OF[n_out]))

            feed_forward(0, N_MIX0, N_OUT0)
            norm_hi(N_OUT0, X, H, lambda m: col("out_b", m))
            slots("q1", copy("q1", QK, 0, float(SB_DIM ** -0.5)))
            slots("k1", copy("k1", QK, KC, 1.0))
            slots("v1", v_copy("v1"))

            for i in range(SB_HEADS + 1):
                if i < SB_HEADS:
                    flat = PS[:, 4 * (i % 2):4 * (i % 2) + 3, :].rearrange("p b t -> p (b t)")[:, 0:SBC]
                    ex = EX[i % 2]
                    act.wait_ge(sz_ps, i + 1)
                    if i >= 2:
                        act.wait_ge(tri_done, i - 1)
                    own.did(a(ex[:], flat, ACT.Abs))
                    own.settle()
                    own.did(a(ex[:], ex[:], ACT.Exp, scale=-1.0))
                    own.settle()
                    a(ex[:], ex[:], ACT.Ln, bias=1.0).then_inc(sz_exp, 1)
                if i:
                    h = i - 1
                    flat = PS[:, 4 * (h % 2):4 * (h % 2) + 3, :].rearrange("p b t -> p (b t)")[:, 0:SBC]
                    act.wait_ge(tri_done, h + 1)
                    if h >= 2:
                        act.wait_ge(sb_pv, h - 1)
                    a(AT[h % 2][:], flat, ACT.Exp).then_inc(a_ready, 1)
            act.wait_ge(so_ready, SB_HEADS)
            for m in range(KC):
                a(YH[:, m, :], QK[:, m, :], ACT.Copy).then_inc(so_hi, 1)
            act.wait_ge(so_lo, KC)
            load_ple(1)
            slots("wo", lambda s, p: None)
            split_ple_hi(1)
            feed_forward(1, N_MIX1, N_OUT1)
            for m in range(KC):
                act.wait_ge(t_ready, KC * N_OUT1 + m + 1)
                a(X[:, m, :], X[:, m, :], ACT.Identity, bias=col("out_b", KC + m)).then_inc(out_ready, 1)

        @block.vector
        def _(dve):
            own = Chain(dve, dve_own)
            v = nc.vector
            acc, tmp = TT[:, 2, :], TT[:, 3, :]

            def split_lo(s, mul, g):
                if isinstance(s.val(), int) and s.val(mul, g) >= NSLOTS:
                    return
                p = s.odd(mul, g)
                dve.wait_ge(w_hi, s.val(mul, g + 1))
                v.tensor_tensor(WL[:, p], RAW[:, p], WH[:, p].bitcast(F32), ALU.subtract).then_inc(w_lo, 1)

            def slots(stage, body, per=0, tail=0, head=0):
                g0 = SLOT0[stage]

                def one(s):
                    split_lo(s, 1, g0 + 1)
                    body(s, s.odd(1, GROUP0[stage]))
                steps(dve, own, COUNT[stage], per, one, tail=tail, head=head)

            def evacuated(s, stage, mul=1, more=0):
                dve.wait_ge(slot_done, s.val(mul, SLOT0[stage] + 1 + more))

            def free(s, stage, ins):
                ins.then_inc(bank_free, 1)

            def earlier_free(s, stage):
                dve.wait_ge(bank_free, s.val(1, GROUP0[stage]))

            def norm_out(n, src, dst, g, hi=None, lo=None, ms=range(KC)):
                if 0 in ms:
                    dve.wait_ge(std_ready, n + 1)
                    own.did(v.reciprocal(acc, acc))
                    own.settle()

                def low(m):
                    dve.wait_ge(hi_ready, KC * n + m + 1)
                    v.tensor_tensor(lo[:, m, :], dst[:, m, :], hi[:, m, :].bitcast(F32),
                                    ALU.subtract).then_inc(h_ready, 1)
                for m in ms:
                    v.scalar_tensor_tensor(dst[:, m, :], src[:, m, :], g(m), acc, ALU.mult,
                                           ALU.mult).then_inc(t_ready, 1)
                    if m > ms[0] and lo is not None:
                        low(m - 1)
                if lo is not None and ms:
                    low(ms[-1])

            def center(n, src):
                dve.wait_ge(mean_ready, LN_OF[n] + 1)
                for m in range(KC):
                    v.tensor_tensor(src[:, m, :], src[:, m, :], MB, ALU.subtract).then_inc(cen_ready, 1)

            dve.wait_ge(const_ready, 6)
            own.did(v.tensor_tensor(SEL[:], IDENT[:, 0:64], IDENT[:, 64:P], ALU.add))
            dve.wait_ge(c_ready, 2)
            dve.wait_ge(sw_hi, 1)
            v.tensor_tensor(SWL[:], SWR[:], SWH[:].bitcast(F32), ALU.subtract).then_inc(sw_lo, 1)
            for k in range(KC):
                dve.wait_ge(ada_in[k], 16)
                if k == 0:
                    ins = v.tensor_scalar(ADAS[:], ADA[0][:], CSIL[:, 0:1], None, ALU.mult)
                else:
                    own.settle()
                    ins = v.scalar_tensor_tensor(ADAS[:], ADA[k][:], CSIL[:, k:k + 1], ADAS[:], ALU.mult, ALU.add)
                if k < KC - 1:
                    own.did(ins)
            ins.then_inc(ada_sum, 1)
            split_lo(Step(0), 1, 0)
            dve.wait_ge(ada_ps, 1)
            dve.wait_ge(par_in, 16)
            own.did(v.tensor_tensor(ADAV[:], PS[:, 5, 0:3 * KC], col("b_ada", 0, 3 * KC), ALU.add))
            own.settle()
            own.did(v.tensor_scalar(GX[:], ADAV[:, KC:2 * KC], 1.0, None, ALU.add))
            own.settle()
            v.tensor_tensor(GX[:], GX[:], col("norm_w", 0, KC), ALU.mult).then_inc(ada_ready, 1)
            dve.wait_ge(ada_ready, 1)
            norm_out(N_X, X, XN, lambda m: GX[:, m:m + 1], H, L)

            sel = SEL[:, 0:SSM_HEADS].bitcast(F32).rearrange("p (g r) -> p g r", g=SSM_GROUPS)
            for g in range(SSM_GROUPS):
                ins = v.tensor_copy(SELE[:, :, g * 64:g * 64 + 64], sel[:, g, :].unsqueeze(2).to_broadcast([P, HPG, 64]))
            ins.then_inc(sele_ready, 1)

            def xbc(s, p):
                evacuated(s, "xbc")
                for tap in range(CONV_K):
                    d = tap
                    for u in range(2):
                        m = s.val(2, u)
                        w_ = dcol("conv_w", s.val(2, u + (CONV_K - 1 - tap) * XBC_C))
                        dst = rows(XC, m, 1)
                        ps = PS[:, 2 * p + u:2 * p + u + 1, :]
                        if tap == 0:
                            own.did(v.tensor_scalar(dst, ps, w_, dcol("conv_b", m), ALU.mult, ALU.add))
                        else:
                            ins = v.scalar_tensor_tensor(dst[:, :, d:T], ps[:, :, 0:T - d], w_, dst[:, :, d:T],
                                                         ALU.mult, ALU.add)
                            if tap == CONV_K - 1 and u == 1:
                                free(s, "xbc", ins)
                            else:
                                own.did(ins)
                    if tap < CONV_K - 1:
                        own.settle()
            slots("xbc", xbc, per=2 * CONV_K - 1)

            R = slice(0, SMALL)
            U, E, W1, LN1 = (SM[R, i, :] for i in range(4))
            T0, T1, T2, T3 = (TT[R, i, :] for i in range(4))
            dve.wait_ge(dt_ps, 1)
            v.tensor_scalar(U, PS[R, 4, :], PAR[R, PCOL["small_b"]:PCOL["small_b"] + 1], SGN[R], ALU.add,
                            ALU.mult).then_inc(dt_u, 1)
            dve.wait_ge(dt_u, 1)
            v.scalar_tensor_tensor(E, U, -1.0, U, ALU.mult, ALU.min).then_inc(dt_u, 1)
            dve.wait_ge(dt_e, 1)
            v.tensor_scalar(W1, E, 1.0, None, ALU.add).then_inc(dt_w, 1)
            dve.wait_ge(dt_w, 1)
            own.did(v.tensor_scalar(T0, W1, -1.0, HALF_ULP, ALU.add, ALU.max))
            own.did(v.tensor_scalar(T1, W1, 1.0, None, ALU.is_equal))
            own.settle()
            own.did(v.reciprocal(T0, T0))
            own.did(v.tensor_tensor(T1, T1, E, ALU.mult))
            own.settle()
            own.did(v.tensor_tensor(T0, T0, E, ALU.mult))
            dve.wait_ge(dt_l, 1)
            own.settle()
            own.did(v.tensor_tensor(T0, T0, LN1, ALU.mult))
            own.settle()
            own.did(v.tensor_tensor(T0, T0, T1, ALU.add))
            own.settle()
            own.did(v.scalar_tensor_tensor(LN1, U, 0.0, T0, ALU.max, ALU.add))
            own.settle()
            S = slice(0, SSM_HEADS)
            own.did(v.tensor_scalar(T2[S], LN1[S], AEXP[S], -1.0, ALU.mult, ALU.mult))
            own.settle()
            for c in range(NT):
                cc = slice(c * P, (c + 1) * P)
                own.did(v.tensor_tensor_scan(CS[S, cc], ONEC[S].to_broadcast([SSM_HEADS, P]), T2[S, cc], 0.0, ALU.mult,
                                             ALU.add))
            Fr = slice(32, 32 + FOX_HEADS)
            v.tensor_tensor_scan(CS[Fr, :], ONEC[Fr].to_broadcast([FOX_HEADS, T]), SM[Fr, 3, :], 0.0, ALU.mult,
                                 ALU.add).then_inc(cs_ready, 1)
            own.settle()
            cs = CS[S, :].rearrange("h (c t) -> h c t", c=NT)
            v.tensor_tensor(SM[S, 1, :].rearrange("h (c t) -> h c t", c=NT),
                            cs[:, :, P - 1:P].to_broadcast([SSM_HEADS, NT, P]), cs, ALU.subtract).then_inc(dt_x, 1)
            dve.wait_ge(csx_hi, 1)
            v.tensor_tensor(CSX[64:P], CS[0:64], CSX[0:64].bitcast(F32), ALU.subtract).then_inc(csx_lo, 1)
            dve.wait_ge(dt_d, 1)
            v.tensor_tensor(SM[S, 1, :], SM[S, 1, :], SM[S, 3, :], ALU.mult).then_inc(dt_rows, 1)
            dve.wait_ge(tok_ps, 1)
            v.tensor_copy(TOK[:].rearrange("p a c h -> p (a c h)"),
                          PS[:, 5, 0:3 * NT * SSM_HEADS]).then_inc(tok_ready, 1)
            dve.wait_ge(tok_ready, 1)

            for i in range(2 * NT):
                c, half = divmod(i, 2)
                dve.wait_ge(xt_ps, i + 1)
                ps = PS[:, 6 + i % 2, :].rearrange("p (h d) -> p h d", d=SSM_P)
                hs = slice(half * 8, half * 8 + 8)
                fs = slice(half * T, (half + 1) * T)

                def scaled(dst, which):
                    return v.tensor_tensor(dst[:, c, fs].rearrange("p (h d) -> p h d", d=SSM_P), ps,
                                           TOK[:, which, c, hs].unsqueeze(2).to_broadcast([P, 8, SSM_P]), ALU.mult)
                ins = scaled(XD, 1)
                if c < NT - 1:
                    own.did(ins)
                    ins = scaled(XDD, 2)
                ins.then_inc(xt_used, 1)
            for r in range(HPG):
                dve.wait_ge(e_exp, r + 1)
                v.tensor_tensor(CE[:, r, :], CE[:, r, :], XC[:, KC + 1, :], ALU.mult).then_inc(ce_ready, 1)
            for c in range(NT - 1):
                dve.wait_ge(st_ps, c + 1)
                if c == 0:
                    v.tensor_copy(ST[:, 0, :], PS[:, 5, :]).then_inc(st_ready, 1)
                else:
                    own.did(v.tensor_tensor(ST[:, c, :].rearrange("p (r d) -> p r d", d=SSM_P),
                                            ST[:, c - 1, :].rearrange("p (r d) -> p r d", d=SSM_P),
                                            EL[:, :, c:c + 1].to_broadcast([P, HPG, SSM_P]), ALU.mult))
                    own.settle()
                    v.tensor_tensor(ST[:, c, :], ST[:, c, :], PS[:, 5, :], ALU.add).then_inc(st_ready, 1)
                dve.wait_ge(st_ready, c + 1)

            def seg(h):
                dve.wait_ge(seg_ps, h + 1)
                if h >= 2:
                    dve.wait_ge(y_ps, h - 1)
                v.tensor_tensor(MT[:, h % 2, :].rearrange("p (c t) -> p c t", c=NT),
                                PS[:, 6 + h % 2, :].rearrange("p (c t) -> p c t", c=NT),
                                TOK[:, 0, :, h:h + 1].to_broadcast([P, NT, P]), ALU.subtract).then_inc(seg_ready, 1)

            dve.wait_ge(cb_ready, 2)
            seg(0)
            for h in range(SSM_HEADS):
                if h + 1 < SSM_HEADS:
                    seg(h + 1)
                dve.wait_ge(seg_exp, h + 1)
                v.tensor_tensor(MT[:, h % 2, :], MT[:, h % 2, :], CBM[:, h // HPG, :], ALU.mult).then_inc(mt_ready, 1)
                if h % 2 == 0 and h:
                    i = h // 2 - 1
                    dve.wait_ge(y_ps, 2 * i + 2)
                    v.scalar_tensor_tensor(XC[:, i, :], XC[:, i, :], col("d_skip", i), PS[:, 4 + i % 2, :], ALU.mult,
                                           ALU.add).then_inc(y_used, 1)
            i = KC - 1
            dve.wait_ge(y_ps, SSM_HEADS)
            v.scalar_tensor_tensor(XC[:, i, :], XC[:, i, :], col("d_skip", i), PS[:, 4 + i % 2, :], ALU.mult,
                                   ALU.add).then_inc(y_used, 1)
            dve.wait_ge(y_used, KC)
            slots("z", lambda s, p: None)
            for j in range(COUNT["q"]):
                split_lo(Step(j), 1, SLOT0["q"] + 1)
                if j == 0:
                    for m in range(KC):
                        dve.wait_ge(bank_free, GROUP0["z"] + m // 2 + 1)
                        v.tensor_tensor(XC[:, m, :], XC[:, m, :], ZS[:, m, :], ALU.mult).then_inc(yz_ready, 1)
                    dve.wait_ge(yz_ready, KC)
                else:
                    norm_out(N_SSM, XC, XC, lambda m: col("ssm_norm_w", m), YH, YL, Q_PART[j])

            def ssm_out(s, p):
                earlier_free(s, "ssm_out")
                dve.wait_ge(sig_ready, s.val(1, SIG0["ssm_out"] + 1))
                free(s, "ssm_out", v.tensor_tensor(rows(P1, s.val(), 1), PS[:, 2 * p:2 * p + 1, :], TT[:, p:p + 1, :],
                                                   ALU.mult))
            slots("ssm_out", ssm_out)
            for s_ in ("k", "v"):
                slots(s_, lambda s, p: None)

            n = NT * FOX_HEADS
            for i in range(n + 1):
                if i < n:
                    w_ = (i % NT + 1) * P
                    dve.wait_ge(lg_ready, i + 1)
                    own.did(v.tensor_reduce(STAT[:, 2, i:i + 1], PS[:, 4 + i % 2, 0:w_], AX_X, ALU.max))
                    own.settle()
                    v.tensor_scalar(STAT[:, 0, i:i + 1], STAT[:, 2, i:i + 1], -1.0, None, ALU.mult).then_inc(nm_ready, 1)
                if i:
                    j = i - 1
                    h, qb = divmod(j, NT)
                    w_ = (qb + 1) * P
                    dve.wait_ge(p_exp, j + 1)
                    own.did(v.reciprocal(STAT[:, 2, j:j + 1], STAT[:, 1, j:j + 1]))
                    own.settle()
                    v.tensor_scalar(TT[:, j % 2, 0:w_], TT[:, j % 2, 0:w_], STAT[:, 2, j:j + 1], None,
                                    ALU.mult).then_inc(pn_ready, 1)
                    if qb == 0 and h:
                        dve.wait_ge(pv_done, h)
                        v.tensor_copy(QK[:, h - 1, :], PS[:, 7, :]).then_inc(ot_ready, 1)
            dve.wait_ge(pv_done, FOX_HEADS)
            v.tensor_copy(QK[:, FOX_HEADS - 1, :], PS[:, 7, :]).then_inc(ot_ready, 1)
            dve.wait_ge(ot_ready, FOX_HEADS)

            def za(s, p):
                dve.wait_ge(bank_free, s.val(1, GROUP0["za"] + 1))
                q = rows(QK, s.val(2), 2)
                v.tensor_tensor(q, q, rows(ZA, s.val(2), 2), ALU.mult).then_inc(ya_ready, 1)
                dve.wait_ge(ya_hi, s.val(1, 1))
                v.tensor_tensor(rows(YL, s.val(2), 2), q, rows(YH, s.val(2), 2).bitcast(F32),
                                ALU.subtract).then_inc(ya_lo, 1)
            slots("za", za)

            def att_out(s, p):
                earlier_free(s, "att_out")
                dve.wait_ge(sig_ready, s.val(1, SIG0["att_out"] + 1))
                ins = v.tensor_tensor(TT[:, p:p + 1, :], PS[:, 2 * p:2 * p + 1, :], TT[:, p:p + 1, :], ALU.mult)
                free(s, "att_out", ins)
                dve.wait_ge(bank_free, s.val(1, GROUP0["att_out"] + 1))
                p1 = rows(P1, s.val(), 1)
                v.tensor_tensor(p1, p1, TT[:, p:p + 1, :], ALU.add).then_inc(mg_ready, 1)
                dve.wait_ge(mg_hi, s.val(1, 1))
                v.tensor_tensor(rows(ML, s.val(), 1), p1, rows(MH, s.val(), 1).bitcast(F32),
                                ALU.subtract).then_inc(mg_lo, 1)
            slots("att_out", att_out)

            def w_out(s, p):
                evacuated(s, "w_out")
                for u in range(2):
                    x = rows(X, s.val(2, u), 1)
                    m = s.val(2, u + 2 * KC)
                    g = ADAV[:, m:m + 1] if isinstance(m, int) else ADAV[:, bass.ds(m, 1)]
                    ins = v.scalar_tensor_tensor(x, PS[:, 2 * p + u:2 * p + u + 1, :], g, x, ALU.mult, ALU.add)
                free(s, "w_out", ins)
            slots("w_out", w_out)
            norm_out(N_FINAL, X, X, lambda m: col("final_norm_w", m), H, L)

            own.did(v.memset(HC[:, :, 0:PAD], 0.0))

            dve.wait_ge(dw_hi, 1)
            own.did(v.tensor_tensor(DW[:, 1, :], col("dw_w", 0, PE_TAPS * KC), DW[:, 0, :].bitcast(F32), ALU.subtract))
            own.settle()
            own.did(v.memset(acc, 0.0))

            def taps_added(s, ahead, between=None):
                dve.wait_ge(cp_ps, s.val(1, 1 - ahead))
                cv = rows(CV, s.val(1, -ahead), 1)
                q = s.odd(1, -ahead)
                own.did(v.tensor_tensor(cv, cv, PS[:, 6 + q:7 + q, :], ALU.add))
                if between:
                    between()
                own.settle()
                own.did(v.tensor_tensor(TT[:, 2:3, :], TT[:, 2:3, :], cv, ALU.add))

            def pw1(s, p):
                dve.wait_ge(sig_ready, s.val(1, SIG0["pw1"] + 1))
                free(s, "pw1", v.scalar_tensor_tensor(rows(HC, s.val(), 1)[:, :, PAD:PAD + T],
                                                      PS[:, 2 * p:2 * p + 1, :], dcol("pw1_b", s.val()),
                                                      TT[:, p:p + 1, :], ALU.add, ALU.mult))
                dve.wait_ge(bank_free, s.val(1, GROUP0["pw1"] + 1))
                cv, hc = rows(CV, s.val(), 1), rows(HC, s.val(), 1)
                q, m = s.odd(), s.val()
                dw = DW[:].bitcast(F32).rearrange("p a (k m) -> p a k m", m=KC)
                v.tensor_copy(DWC[:, q].unsqueeze(3), dw[:, :, :, m:m + 1] if isinstance(m, int) else
                              dw[:, :, :, bass.ds(m, 1)]).then_inc(dwc_ready, 1)
                dsts = (cv, CVB[:])
                for n, k in enumerate(range(PE_TAPS, DW_K)):
                    w_ = dcol("dw_w", s.val(1, k * KC))
                    src, dst = hc[:, :, k:k + T], dsts[n % 2]
                    if n == 0:
                        own.did(v.tensor_scalar(dst, src, w_, dcol("dw_b", s.val()), ALU.mult, ALU.add))
                    elif n == 1:
                        own.did(v.tensor_scalar(dst, src, w_, None, ALU.mult))
                    else:
                        own.settle(1)
                        own.did(v.scalar_tensor_tensor(dst, src, w_, dst, ALU.mult, ALU.add))
                    if n == 2:
                        dve.wait_ge(hc_hi, s.val(1, 1))
                        v.tensor_tensor(HCL[:, q:q + 1, :], hc, HCH[:, q:q + 1, :].bitcast(F32),
                                        ALU.subtract).then_inc(hc_lo, 1)
                own.settle()
                both = lambda: own.did(v.tensor_tensor(cv, cv, CVB[:], ALU.add))
                if isinstance(s.val(), int) and s.val() == 0:
                    both()
                    own.settle()
                    own.did(v.memset(acc, 0.0))
                    own.settle()
                    own.did(v.memset(acc, 0.0))
                else:
                    taps_added(s, 1, both)
            slots("pw1", pw1, per=DW_K - PE_TAPS + 3, head=1)
            own.settle()
            taps_added(Step(KC - 1), 0)
            own.settle()
            v.tensor_copy(TT[:, 2, 0:1], TT[:, 2, 0:1]).then_inc(sum_ready, 1)
            center(N_CONV, CV)
            norm_out(N_CONV, CV, CV, lambda m: col("ln_g", m), YH, YL)
            for m in range(KC):
                own.did(v.tensor_scalar(X[:, m, :], X[:, m, :], ALPHA, col("pw2_b", m), ALU.mult, ALU.add))

            def split_ple_lo(layer):
                dve.wait_ge(ple_hi, layer + 1)
                own.did(v.tensor_tensor(WPL[:], PWR[:], WPH[:].bitcast(F32), ALU.subtract))
                v.tensor_tensor(PPL[:], PR[:], PPH[:].bitcast(F32), ALU.subtract).then_inc(ple_lo, 1)

            split_ple_lo(0)
            own.did(v.memset(acc, 0.0))
            own.settle()

            def sums(s, last=None):
                for u in range(2):
                    own.settle()
                    own.did(v.tensor_tensor(acc, acc, X[:, s.val(2, u), :] if isinstance(s.val(), int) else
                                            rows(X, s.val(2, u), 1).rearrange("p a t -> p (a t)"), ALU.add))

            def added(stage, mul=1, more=0, first=1.0):
                def body(s, p):
                    evacuated(s, stage, mul, more)
                    x = rows(X, s.val(2), 2)
                    ps = PS[:, 2 * p:2 * p + 2, :]
                    if first == 1.0:
                        ins = v.tensor_tensor(x, x, ps, ALU.add)
                    else:
                        ins = v.scalar_tensor_tensor(x, x, first, ps, ALU.mult, ALU.add)
                    free(s, stage, ins)
                    dve.wait_ge(bank_free, s.val(1, GROUP0[stage] + 1))
                    sums(s)
                return body
            slots("pw2", added("pw2"), per=2)

            def ln_front(n):
                own.settle()
                v.tensor_copy(X[:, 0, 0:1], X[:, 0, 0:1]).then_inc(sum_ready, 1)
                center(n, X)

            def feed_forward(layer, n_mix, n_out, g_out):
                ln_front(n_mix)
                norm_out(n_mix, X, X, lambda m: col("mix_g", KC * layer + m), H, L)
                gate = f"gate{layer}"

                def gate_body(s, p):
                    dve.wait_ge(sig_ready, s.val(1, SIG0[gate] + 1))
                    dve.wait_ge(pg_ready, s.val(1, COUNT[gate] * layer + 1))
                    own.did(v.tensor_tensor(TT[:, 0:2, :], TT[:, 0:2, :], PS[:, 4 + 2 * p:6 + 2 * p, :], ALU.mult))
                    own.settle()
                    x = rows(X, s.val(2), 2)
                    free(s, gate, v.scalar_tensor_tensor(x, x, ALPHA, TT[:, 0:2, :], ALU.mult, ALU.add))
                slots(gate, gate_body, per=1)
                up = f"up{layer}"

                def up_body(s, p):
                    evacuated(s, up)
                    gate_ps = PS[:, 2 * p + 1:2 * p + 2, :]
                    c = TT[:, 3:4, :]
                    if not (isinstance(s.val(), int) and s.val(1, layer) == 0):
                        dve.wait_ge(ff_lo, s.val(1, FC * layer))
                    for d in range(FCONV_K):
                        w_ = dcol("fconv_w", s.val(1, (layer * FCONV_K + FCONV_K - 1 - d) * FC))
                        if d == 0:
                            own.did(v.tensor_scalar(c, gate_ps, w_, dcol("fconv_b", s.val(1, layer * FC)), ALU.mult,
                                                    ALU.add))
                            own.settle()
                        else:
                            ins = v.scalar_tensor_tensor(c[:, :, d:T], gate_ps[:, :, 0:T - d], w_, c[:, :, d:T],
                                                         ALU.mult, ALU.add)
                            if d == FCONV_K - 1:
                                ins.then_inc(gc_ready, 1)
                            else:
                                own.did(ins)
                                own.settle()
                    dve.wait_ge(sl_ready, s.val(1, FC * layer + 1))
                    free(s, up, v.tensor_tensor(c, TT[:, p:p + 1, :], PS[:, 2 * p:2 * p + 1, :], ALU.mult))
                    dve.wait_ge(ff_hi, s.val(1, FC * layer + 1))
                    v.tensor_tensor(rows(FL, s.val(), 1), c, rows(FH, s.val(), 1).bitcast(F32),
                                    ALU.subtract).then_inc(ff_lo, 1)
                slots(up, up_body, per=FCONV_K - 1, head=1)
                own.did(v.memset(acc, 0.0))
                down = f"down{layer}"

                def down_one(s):
                    for part in range(DOWN_S):
                        split_lo(s, DOWN_S, SLOT0[down] + part + 1)
                    added(down, DOWN_S, DOWN_S - 1)(s, s.odd(1, GROUP0[down]))
                steps(dve, own, 4, 2, down_one, tail=2 if layer else 0)
                ln_front(n_out)
                if layer == 0:
                    norm_out(n_out, X, X, g_out, H, L)
                else:
                    norm_out(n_out, X, X, g_out)

            feed_forward(0, N_MIX0, N_OUT0, lambda m: col("out_g", m))
            for s_ in ("q1", "k1", "v1"):
                slots(s_, lambda s, p: None)

            for i in range(SB_HEADS + 2):
                if i < SB_HEADS:
                    flat = PS[:, 4 * (i % 2):4 * (i % 2) + 3, :].rearrange("p b t -> p (b t)")[:, 0:SBC]
                    dve.wait_ge(sz_exp, i + 1)
                    v.scalar_tensor_tensor(EX[i % 2][:], flat, 0.0, EX[i % 2][:], ALU.max, ALU.add).then_inc(sp_ready, 1)
                if i >= 2:
                    h = i - 2
                    pb = (h % 2) * 64
                    dve.wait_ge(sb_pv, h + 1)
                    v.tensor_copy(QK[pb:pb + 64, h // 2, :], PS[pb:pb + 64, 4 * (h % 2) + 3, :]).then_inc(so_ready, 1)
            for m in range(KC):
                dve.wait_ge(so_hi, m + 1)
                v.tensor_tensor(YL[:, m, :], QK[:, m, :], YH[:, m, :].bitcast(F32), ALU.subtract).then_inc(so_lo, 1)
            own.did(v.memset(acc, 0.0))
            slots("wo", added("wo", first=ALPHA), per=2)
            split_ple_lo(1)
            feed_forward(1, N_MIX1, N_OUT1, lambda m: col("out_g", KC + m))


def _unit(w, m, k0=0):
    blk = w[k0 * P:(k0 + KC) * P, m * P:(m + 1) * P]
    if blk.shape[0] < KC * P:
        blk = np.concatenate([blk, np.zeros((KC * P - blk.shape[0], P), w.dtype)])
    return blk.reshape(KC, P, P).transpose(1, 0, 2)


def _slots(i):
    w_in = i["w_in"]
    cut = lambda a, n: w_in[:, a:a + n]
    pairs = lambda a: [(_unit(a, 2 * j), _unit(a, 2 * j + 1)) for j in range(a.shape[1] // (2 * P))]
    both = lambda a, b: [(_unit(a, j), _unit(b, j)) for j in range(a.shape[1] // P)]
    down = lambda a: [(_unit(a, 2 * j, KC * s), _unit(a, 2 * j + 1, KC * s))
                      for j in range(KC // 2) for s in range(DOWN_S)]
    pw1 = i["a_pw1_w_2"][0]
    parts = [pairs(cut(XBC0, XBC)), pairs(cut(Z0, D)), pairs(cut(Q0, D)), both(i["w_proj_ssm"], cut(G0, D)),
             pairs(cut(K0, D)), pairs(cut(V0, D)), pairs(cut(ZA0, D)), both(i["w_proj_att"], cut(G0 + D, D)),
             pairs(i["w_out"]), both(pw1[:, 0:D], pw1[:, D:2 * D]), pairs(i["a_pw2_w_2"][0])]

    def ffn(layer):
        return [pairs(i["ple_w_gate_2"][layer]), both(i["ffn_w_up_2"][layer], i["ffn_w_gate_2"][layer]),
                down(i["ffn_w_down_2"][layer])]
    parts += ffn(0) + [pairs(i["b_wq_2"][0]), pairs(i["kv_wk_2"]), pairs(i["kv_wv_2"]), pairs(i["b_wo_2"][0])] + ffn(1)
    out = [np.stack(s, axis=1) for part in parts for s in part]
    return np.stack(out).reshape(NSLOTS, P, 2 * KC * P)


def _params(i):
    col = lambda a: np.asarray(a).reshape(-1, P).T
    rows = {
        "c": i["c"], "norm_w": i["norm_w"], "b_ada": i["b_ada"], "conv_w": i["conv_w"], "conv_b": i["conv_b"],
        "d_skip": np.repeat(i["d_skip"], SSM_P), "ssm_norm_w": i["ssm_norm_w"], "b_gate": i["b_gate"],
        "final_norm_w": i["final_norm_w"], "pw1_b": i["a_pw1_b_2"], "dw_w": i["a_dw_w_2"], "dw_b": i["a_dw_b_2"],
        "ln_g": i["a_ln_g_2"], "ln_b": i["a_ln_b_2"], "pw2_b": i["a_pw2_b_2"], "mix_g": i["ln_mix_g_2"],
        "mix_b": i["ln_mix_b_2"], "fconv_w": i["ffn_conv_w_2"], "fconv_b": i["ffn_conv_b_2"],
        "out_g": i["ln_ffn_g_2"], "out_b": i["ln_ffn_b_2"],
    }
    par = np.zeros((P, NPAR), np.float32)
    for name, a in rows.items():
        c = col(a)
        par[:, PCOL[name]:PCOL[name] + c.shape[1]] = c
    par[0:SSM_HEADS, PCOL["small_b"]] = i["dt_bias"]
    par[32:32 + FOX_HEADS, PCOL["small_b"]] = i["b_f"]
    par[0:SSM_HEADS, PCOL["a_log"]] = i["a_log"]
    return par


def kernel(**inputs):
    import concourse.bacc as bacc
    from concourse.bass_utils import run_bass_kernel_spmd

    i = {k: np.asarray(a) for k, a in inputs.items()}
    chunks = lambda a: a.reshape(-1, P, a.shape[-1]).transpose(1, 0, 2)
    w_small = np.zeros((D, SMALL), np.float32)
    w_small[:, 0:SSM_HEADS] = i["w_in"][:, DT0:DT0 + SSM_HEADS]
    w_small[:, 32:SMALL] = i["w_in"][:, FL0:FL0 + FOX_HEADS]
    arrays = {
        "w": _slots(i),
        "w_ada": i["w_ada"].reshape(KC, P, 3 * D),
        "w_small": chunks(w_small),
        "w_ple": np.stack([chunks(i["ple_w_proj_2"][n]) for n in range(2)]),
        "p_t": np.stack([chunks(i["p_2"][n, 0].T) for n in range(2)]),
        "x_t": chunks(i["x"][0].T),
        "par": _params(i),
    }
    arrays = {k: np.ascontiguousarray(a) for k, a in arrays.items()}
    nc = bacc.Bacc("TRN2", target_bir_lowering=False, num_devices=1)
    aps = [nc.dram_tensor(k, a.shape, F32, kind="ExternalInput").ap() for k, a in arrays.items()]
    out = nc.dram_tensor("out", (P, KC, T), F32, kind="ExternalOutput").ap()
    build(nc, *aps, out)
    r = run_bass_kernel_spmd(nc, [arrays], core_ids=[0])
    return np.asarray(r.results[0]["out"]).transpose(2, 1, 0).reshape(1, T, D)
```

```python
from contextlib import ExitStack

import numpy as np

import concourse.bass as bass
from concourse import mybir

F32 = mybir.dt.float32
F32R = mybir.dt.float32r
BF16 = mybir.dt.bfloat16
ACT = mybir.ActivationFunctionType
ALU = mybir.AluOpType
AX_X = mybir.AxisListType.X

P = 128
D = 1024
T = 512
KC = D // P
NT = T // P
SSM_HEADS, SSM_P, SSM_N, SSM_GROUPS = 16, 64, 64, 2
SSM_INNER = SSM_HEADS * SSM_P
HPG = SSM_HEADS // SSM_GROUPS
CONV_K = 4
XBC = SSM_INNER + 2 * SSM_GROUPS * SSM_N
XBC_C = XBC // P
FOX_HEADS = 8
SB_HEADS, SB_DIM = 16, 64
DW_K = 31
PAD = DW_K - 1
PE_TAPS = 11
FFN = 2816
FC = FFN // P
FCONV_K = 3
PLE = 256
PC = PLE // P
LN_EPS, RMS_EPS = 1e-5, 1e-6
ALPHA = float((2.0 * 2) ** 0.25)
NEG = -1e30
HALF_ULP = 2.0 ** -24

Z0 = 0
XBC0 = Z0 + SSM_INNER
DT0 = XBC0 + XBC
Q0 = DT0 + SSM_HEADS
K0 = Q0 + D
V0 = K0 + D
ZA0 = V0 + D
FL0 = ZA0 + D
G0 = FL0 + FOX_HEADS
SMALL = 32 + FOX_HEADS

DOWN_S = 3
STAGES = [("xbc", XBC_C // 2), ("q", 4), ("z", 4), ("k", 4), ("ssm_out", 8), ("v", 4), ("za", 4), ("att_out", 8),
          ("w_out", 4), ("pw1", 8), ("pw2", 4), ("gate0", 4), ("up0", FC), ("down0", 4 * DOWN_S),
          ("q1", 4), ("k1", 4), ("v1", 4), ("wo", 4), ("gate1", 4), ("up1", FC), ("down1", 4 * DOWN_S)]
SLOT0, GROUP0 = {}, {}
_g = _b = 0
for _name, _n in STAGES:
    SLOT0[_name], GROUP0[_name] = _g, _b
    _g += _n
    _b += _n // DOWN_S if _name.startswith("down") else _n
NSLOTS = _g
COUNT = dict(STAGES)

PCOL, _c = {}, 0
for _name, _n in [("c", KC), ("norm_w", KC), ("b_ada", 3 * KC), ("conv_w", CONV_K * XBC_C), ("conv_b", XBC_C),
                  ("d_skip", KC), ("ssm_norm_w", KC), ("b_gate", 2 * KC), ("final_norm_w", KC), ("pw1_b", 2 * KC),
                  ("dw_w", DW_K * KC), ("dw_b", KC), ("ln_g", KC), ("ln_b", KC), ("pw2_b", KC), ("mix_g", 2 * KC),
                  ("mix_b", 2 * KC), ("fconv_w", 2 * FCONV_K * FC), ("fconv_b", 2 * FC), ("out_g", 2 * KC),
                  ("out_b", 2 * KC), ("small_b", 1), ("a_log", 1)]:
    PCOL[_name] = _c
    _c += _n
NPAR = _c


class Step:

    def __init__(self, first, turn=0):
        self.first, self.turn = first, turn

    def val(self, mul=1, add=0):
        return mul * self.first + add + 2 * mul * self.turn

    def half(self, mul=1, add=0):
        return (mul * self.first + add) // 2 + mul * self.turn

    def odd(self, mul=1, add=0):
        return (mul * self.first + add) % 2


class Chain:

    def __init__(self, eng, sem):
        self.eng, self.sem, self.base, self.k = eng, sem, 0, 0

    def did(self, ins):
        ins.then_inc(self.sem, 1)
        self.k += 1

    def settle(self, but=0):
        self.eng.wait_ge(self.sem, self.base + self.k - but)


def steps(eng, chain, n, per, body, head=0, tail=0):
    tail += (n - head - tail) % 2
    begin = chain.base + chain.k if chain else 0

    def one(s):
        if chain:
            chain.base, chain.k = begin + s.val(per), 0
        body(s)
        assert not chain or chain.k == per, (chain.k, per)

    for i in range(head):
        one(Step(i))
    turns = (n - head - tail) // 2
    if turns > 0:
        with eng.Fori(0, turns) as t:
            for i in range(2):
                one(Step(head + i, t))
    for i in range(n - tail, n):
        one(Step(i))
    if chain:
        chain.base, chain.k = begin + per * n, 0


def build(nc, w, w_ada, w_small, w_ple, p_t, x_t, par, out):
    with ExitStack() as ctx:
        KB = 1024
        base = (nc.sbuf_base + 31) // 32 * 32

        def at(name, kb, shape, dt=F32):
            return nc.alloc_sbuf_tensor_at(name, shape, dt, offset=base + int(kb * KB))

        def sem(name):
            return ctx.enter_context(nc.semaphore(name))

        X = at("X", 0, [P, KC, T])
        H = at("H", 16, [P, KC, T], F32R)
        L = at("L", 32, [P, KC, T], F32R)
        RAW = at("RAW", 48, [P, 2, 16, P])
        WH = at("WH", 64, [P, 2, 16, P], F32R)
        WL = at("WL", 80, [P, 2, 16, P], F32R)
        A = 96
        TT = at("TT", 188, [P, 4, T])
        CS = at("CS", 196, [P, T])
        MISC = 198
        ADA = [at(f"ADA{k}", (A + 12 * k) if k < 6 else (16, 32)[k - 6], [P, 3 * D]) for k in range(KC)]
        ADAS = at("ADAS", A + 72, [P, 3 * D])
        XN = at("XN", A + 0, [P, KC, T])
        XC = at("XC", A + 0, [P, XBC_C, T])
        CE = at("CE", A + 20, [P, HPG, T])
        XD = at("XD", A + 36, [P, NT, SSM_INNER])
        XDD = at("XDD", A + 52, [P, NT, SSM_INNER])
        ST = at("ST", A + 68, [P, 3, T])
        SELE = at("SELE", A + 68, [P, HPG, P], F32R)
        BTOK = at("BTOK", A + 74, [P, NT, P])
        CBM = at("CBM", A + 76, [P, 2, T])
        MT = at("MT", A + 80, [P, 2, T])
        SM = at("SM", A + 84, [P, 4, T])
        ZS = at("ZS", A + 36, [P, KC, T])
        YHS = at("YHS", A + 36, [P, KC, T], F32R)
        YH = at("YH", A + 68, [P, KC, T], F32R)
        YL = at("YL", A + 20, [P, KC, T], F32R)
        P1 = at("P1", A + 0, [P, KC, T])
        QK = at("QK", A + 52, [P, 2 * KC, T])
        VTOK_F = at("VTOK_F", A + 20, [P, NT, D])
        VTOK = at("VTOK", A + 0, [P, NT, D])
        YLA = at("YLA", A + 52, [P, KC, T], F32R)
        PT = at("PT", A + 84, [P, NT, T])
        ZA = at("ZA", A + 36, [P, KC, T])
        MH = at("MH", A + 36, [P, KC, T], F32R)
        ML = at("ML", A + 20, [P, KC, T], F32R)
        SBC = sum(T - P * k for k in range(NT))
        EX = [at(f"EX{i}", A + 36 + 5 * i, [P, SBC]) for i in range(2)]
        EXH = [at(f"EXH{i}", A + 16 + 5 * i, [P, SBC], F32R) for i in range(2)]
        EXL = [at(f"EXL{i}", A + 26 + 5 * i, [P, SBC], F32R) for i in range(2)]
        AT = [at("AT0", A + 46, [P, SBC]), at("AT1", A + 84, [P, SBC])]
        HC = at("HC", A + 0, [P, KC, PAD + T])
        CV = at("CV", A + 20, [P, KC, T])
        DG = at("DG", A + 36, [P, 2, 2, PE_TAPS, P], F32R)
        CVB = at("CVB", A + 60, [P, 1, T])
        DW = at("DW", A + 62, [P, 2, PE_TAPS * KC], F32R)
        DWC = at("DWC", A + 66, [P, 2, 2, PE_TAPS])
        HCH = at("HCH", A + 68, [P, 2, PAD + T], F32R)
        HCL = at("HCL", A + 73, [P, 2, PAD + T], F32R)
        FH = at("FH", A + 0, [P, FC, T], F32R)
        FL = at("FL", A + 44, [P, FC, T], F32R)
        PPL = at("PPL", A + 88, [P, PC, T], F32R)
        PWR = at("PWR", A + 36, [P, PC, D])
        WPH = at("WPH", A + 44, [P, PC, D], F32R)
        WPL = at("WPL", A + 52, [P, PC, D], F32R)
        PR = at("PR", A + 60, [P, PC, T])
        PPH = at("PPH", A + 64, [P, PC, T], F32R)
        PO = at("PO", A + 0, [P, KC, T])
        PAR = at("PAR", MISC, [P, NPAR])
        o = MISC + NPAR * 4 / KB
        o = int(o * 32 + 1) / 32

        def small(name, shape, dt=F32):
            nonlocal o
            t = at(name, o, shape, dt)
            n = int(np.prod(shape[1:])) * (2 if dt == BF16 else 4)
            o += (n + 31) // 32 * 32 / KB
            return t

        IDENT = small("IDENT", [P, P])
        TRI = small("TRI", [P, P])
        IDB = small("IDB", [P, P], BF16)
        M_FOX = small("M_FOX", [P, P], BF16)
        M_SB = small("M_SB", [P, P], BF16)
        M_SSM = small("M_SSM", [P, P], BF16)
        ADAV = small("ADAV", [P, 3 * KC])
        GX = small("GX", [P, KC])
        CSIL = small("CSIL", [P, KC])
        COLS = small("COLS", [P, 6])
        MEANC, ONEC, NEGC, EPS_LN, EPS_RMS, SGN = (COLS[:, i:i + 1] for i in range(6))
        STAT = small("STAT", [P, 3, NT * FOX_HEADS])
        TOK = small("TOK", [P, 3, NT, SSM_HEADS])
        EL = small("EL", [P, HPG, NT])
        AEXP = small("AEXP", [P, 1])
        CSX = small("CSX", [P, T], F32R)
        SEL = small("SEL", [P, 64], F32R)
        TRIR = small("TRIR", [P, P + 1], F32R)
        assert base + o * KB <= nc.sbuf_usable_end, (o, (nc.sbuf_usable_end - base) / KB)
        SWR = at("SWR", A + 84, [P, KC, SMALL])
        SWH = at("SWH", A + 86, [P, KC, SMALL], F32R)
        SWL = at("SWL", A + 88, [P, KC, SMALL], F32R)

        PS = ctx.enter_context(nc.psum_tensor("PS", [P, 8, T], F32))
        NB, MB = PS[:, 4, :], PS[:, 5, :]

        def col(name, i=0, n=1):
            return PAR[:, PCOL[name] + i:PCOL[name] + i + n]

        def dcol(name, i):
            if isinstance(i, int):
                return col(name, i)
            return PAR[:, bass.ds(i + PCOL[name], 1)]

        def rows(t, i, n):
            return t[:, i:i + n, :] if isinstance(i, int) else t[:, bass.ds(i, n), :]

        par_in, x_in, sw_in, c_ready = sem("par_in"), sem("x_in"), sem("sw_in"), sem("c_ready")
        ada_in = [sem(f"ada_in{k}") for k in range(KC)]
        const_ready = sem("const_ready")
        act_own, dve_own, pool_own = sem("act_own"), sem("dve_own"), sem("pool_own")
        raw_in = [sem("raw_in0"), sem("raw_in1")]
        w_hi, w_lo = sem("w_hi"), sem("w_lo")
        slot_done = sem("slot_done")
        bank_free = sem("bank_free")
        sw_hi, sw_lo = sem("sw_hi"), sem("sw_lo")
        ada_sum, ada_ps, ada_ready = sem("ada_sum"), sem("ada_ps"), sem("ada_ready")
        sq_ready, sq_used, std_ready = sem("sq_ready"), sem("sq_used"), sem("std_ready")
        t_ready, hi_ready, h_ready = sem("t_ready"), sem("hi_ready"), sem("h_ready")
        sum_ready, mean_ready, cen_ready = sem("sum_ready"), sem("mean_ready"), sem("cen_ready")
        xc_ready = sem("xc_ready")
        dt_ps, dt_u, dt_e, dt_w, dt_l, dt_x, dt_d, dt_rows = (sem(s) for s in (
            "dt_ps", "dt_u", "dt_e", "dt_w", "dt_l", "dt_x", "dt_d", "dt_rows"))
        tok_ps, tok_ready, bt_ps, bt_ready, cb_ps, cb_ready = (sem(s) for s in (
            "tok_ps", "tok_ready", "bt_ps", "bt_ready", "cb_ps", "cb_ready"))
        xt_ps, xt_used, e_ps, e_exp, ce_ready, st_ps, st_ready = (sem(s) for s in (
            "xt_ps", "xt_used", "e_ps", "e_exp", "ce_ready", "st_ps", "st_ready"))
        seg_ps, seg_ready, seg_exp, mt_ready, y_ps, y_used = (sem(s) for s in (
            "seg_ps", "seg_ready", "seg_exp", "mt_ready", "y_ps", "y_used"))
        zs_ready, yz_ready = sem("zs_ready"), sem("yz_ready")
        sig_ready = sem("sig_ready")
        lg_ready, nm_ready, p_exp, pn_ready, tr_ready, pt_ready, pv_done, ot_ready = (sem(s) for s in (
            "lg_ready", "nm_ready", "p_exp", "pn_ready", "tr_ready", "pt_ready", "pv_done", "ot_ready"))
        ya_ready, ya_hi, ya_lo = (sem(s) for s in ("ya_ready", "ya_hi", "ya_lo"))
        mg_ready, mg_hi, mg_lo = sem("mg_ready"), sem("mg_hi"), sem("mg_lo")
        hc_hi, hc_lo, dw_hi, dwc_ready, dg_ready, cp_ps = (sem(s) for s in (
            "hc_hi", "hc_lo", "dw_hi", "dwc_ready", "dg_ready", "cp_ps"))
        sele_ready = sem("sele_ready")
        cs_ready, csx_hi, csx_lo = sem("cs_ready"), sem("csx_hi"), sem("csx_lo")
        ple_in, ple_hi, ple_lo, pg_ready, pg_used = (sem(s) for s in (
            "ple_in", "ple_hi", "ple_lo", "pg_ready", "pg_used"))
        gc_ready, sl_ready, ff_hi, ff_lo = (sem(s) for s in ("gc_ready", "sl_ready", "ff_hi", "ff_lo"))
        tri_ready = sem("tri_ready")
        sz_ps, sz_exp, sp_ready, sp_hi, sp_lo = (sem(s) for s in (
            "sz_ps", "sz_exp", "sp_ready", "sp_hi", "sp_lo"))
        tri_done, a_ready, sb_pv, so_ready = (sem(s) for s in ("tri_done", "a_ready", "sb_pv", "so_ready"))
        so_hi, so_lo = sem("so_hi"), sem("so_lo")
        out_ready, out_done = sem("out_ready"), sem("out_done")

        ADA_PARTS = (1, 0, 2)
        N_X, N_SSM, N_FINAL, N_CONV, N_MIX0, N_OUT0, N_MIX1, N_OUT1 = range(8)
        LN_OF = {N_CONV: 0, N_MIX0: 1, N_OUT0: 2, N_MIX1: 3, N_OUT1: 4}
        SIG0, _n = {}, 0
        for s in ("ssm_out", "att_out", "pw1", "gate0", "gate1"):
            SIG0[s] = _n
            _n += COUNT[s]
        K_PART = [range(0), range(0, 4), range(4, 8), range(0)]
        GATE_LAG = 3
        def ple_bank(layer, j):
            return 2 * ((GROUP0[f"gate{layer}"] + 1) % 2) if j % 2 else 6

        SB_OFF = {0: 0, 1: T, 3: T + 3 * P, 2: 2 * T}
        SB_PARTS = (slice(T, SBC), slice(0, T))

        block = ctx.enter_context(nc.Block())

        @block.gpsimd
        def _(pool):
            own = Chain(pool, pool_own)
            own.did(nc.gpsimd.memset(IDENT[:], 0.0))
            own.did(nc.gpsimd.memset(IDB[:], 0.0))
            own.did(nc.gpsimd.memset(M_FOX[:], 0.0))
            own.did(nc.gpsimd.memset(M_SB[:], 0.0))
            own.did(nc.gpsimd.memset(M_SSM[:], 0.0))
            own.did(nc.gpsimd.memset(TRI[:], -1.0))
            own.did(nc.gpsimd.memset(CS[:], 0.0))
            for c, v in ((MEANC, 1.0 / D), (ONEC, 1.0), (NEGC, -1.0), (EPS_LN, LN_EPS), (EPS_RMS, RMS_EPS)):
                own.did(nc.gpsimd.memset(c, v))
            own.did(nc.gpsimd.memset(SGN[0:32], 1.0))
            own.settle()
            own.did(nc.gpsimd.memset(SGN[32:64], -1.0))
            own.settle()

            def select(t, op, fill, cm, step):
                nc.gpsimd.affine_select(out=t[:], in_=t[:], compare_op=op, fill=fill, base=0,
                                        pattern=[[step, P]], channel_multiplier=cm).then_inc(const_ready, 1)

            select(IDENT, ALU.not_equal, 1.0, 1, -1)
            select(IDB, ALU.not_equal, 1.0, 1, -1)
            select(M_FOX, ALU.is_ge, NEG, 1, -1)
            select(M_SB, ALU.is_gt, NEG, -1, 1)
            select(M_SSM, ALU.is_ge, NEG, -1, 1)
            select(TRI, ALU.is_ge, 0.0, 1, -1)

            pool.wait_ge(const_ready, 6)

            def diagonals(s):
                p = s.odd()
                pool.wait_ge(dwc_ready, s.val(1, 1))
                for part in range(2):
                    for k in range(PE_TAPS):
                        ins = nc.gpsimd.tensor_scalar(DG[:, p, part, k, :], IDENT[:], DWC[:, p, part, k:k + 1], None,
                                                      ALU.mult)
                ins.then_inc(dg_ready, 1)
            for m in range(KC):
                diagonals(Step(m))

        @block.sync
        def _(sp):
            sp.dma_start(PAR[:], par).then_inc(par_in, 16)
            sp.dma_start(X[:], x_t).then_inc(x_in, 16)
            sp.dma_start(SWR[:], w_small).then_inc(sw_in, 16)
            sp.wait_ge(ada_in[KC - 3], 16)
            for g in range(2):
                sp.dma_start(RAW[:, g], w[g]).then_inc(raw_in[g], 16)
            n = NSLOTS - 2
            with sp.Fori(0, n // 2) as t:
                for i in range(2):
                    sp.wait_ge(w_lo, 2 * t + i + 1)
                    sp.dma_start(RAW[:, i], w[2 * t + (i + 2)]).then_inc(raw_in[i], 16)
            if n % 2:
                sp.wait_ge(w_lo, n)
                sp.dma_start(RAW[:, 0], w[NSLOTS - 1]).then_inc(raw_in[0], 16)
            for m in range(KC):
                sp.wait_ge(out_ready, m + 1)
                sp.dma_start(out[:, m, :], X[:, m, :]).then_inc(out_done, 16)
            sp.wait_ge(out_done, 16 * KC)

        @block.tensor
        def _(pe):
            own = None

            def product(ps, wh, wl, xh, xl, start, stop):
                nc.tensor.matmul(ps, wh, xh, start=start, stop=False)
                nc.tensor.matmul(ps, wh, xl, start=False, stop=False)
                return nc.tensor.matmul(ps, wl, xh, start=False, stop=stop)

            def slot(s, stage, units, ready=None, last=True, mul=1, part=0, ks=KC, group=None):
                g0 = SLOT0[stage] + part
                p = s.odd(mul, g0)
                b = s.odd(1, GROUP0[stage])
                pe.wait_ge(w_lo, s.val(mul, g0 + 1))
                if part == 0 and not (isinstance(s.val(), int) and s.val(1, GROUP0[stage]) < 2):
                    pe.wait_ge(bank_free, s.val(1, GROUP0[stage] - 1))
                for k in range(ks):
                    if ready:
                        pe.wait_ge(ready[0], ready[1](k))
                    for u, (xh, xl) in enumerate(units):
                        i = u * KC + k
                        mm = product(PS[:, 2 * b + u, :], WH[:, p, i, :], WL[:, p, i, :], xh[:, part * KC + k, :],
                                     xl[:, part * KC + k, :], part == 0 and k == 0, last and k == ks - 1)
                mm.then_inc(slot_done, 1)

            def gemm(stage, units, ready=None):
                def one(s):
                    first = isinstance(s.val(), int) and s.val() == 0
                    slot(s, stage, units, ready if first else None)
                steps(pe, None, COUNT[stage], 0, one, head=2 if stage == "xbc" else 1 if ready else 0)

            def slot_step(i, stage, units):
                j, k = divmod(i, KC)
                p, b = (SLOT0[stage] + j) % 2, (GROUP0[stage] + j) % 2
                if k == 0:
                    pe.wait_ge(w_lo, SLOT0[stage] + j + 1)
                    pe.wait_ge(bank_free, GROUP0[stage] + j - 1)
                for u, (xh, xl) in enumerate(units):
                    n = u * KC + k
                    mm = product(PS[:, 2 * b + u, :], WH[:, p, n, :], WL[:, p, n, :], xh[:, k, :], xl[:, k, :], k == 0,
                                 k == KC - 1)
                if k == KC - 1:
                    mm.then_inc(slot_done, 1)

            hl, ylh = (H, L), (YH, YL)

            def normed(n):
                return h_ready, lambda k: KC * n + k + 1

            def token_major(stage):
                def one(s):
                    p, b = s.odd(1, SLOT0[stage]), s.odd(1, GROUP0[stage])
                    pe.wait_ge(w_lo, s.val(1, SLOT0[stage] + 1))
                    pe.wait_ge(bank_free, s.val(1, GROUP0[stage] - 1))
                    for k in range(KC):
                        wh, wl = WH[:, p, k::KC, :], WL[:, p, k::KC, :]
                        for c in range(NT):
                            cc = slice(c * P, (c + 1) * P)
                            ps = PS[:, 2 * b + c // 2, (c % 2) * 2 * P:(c % 2 + 1) * 2 * P]
                            nc.tensor.matmul(ps, H[:, k, cc], wh, start=k == 0 and c % 2 == 0, stop=False,
                                             skip_group_check=True)
                            nc.tensor.matmul(ps, H[:, k, cc], wl, start=False, stop=False, skip_group_check=True)
                            mm = nc.tensor.matmul(ps, L[:, k, cc], wh, start=False, stop=k == KC - 1,
                                                  skip_group_check=True)
                    mm.then_inc(slot_done, 1)
                steps(pe, None, COUNT[stage], 0, one)

            def norm(n):
                for m in range(KC):
                    pe.wait_ge(sq_ready, KC * n + m + 1)
                    nc.tensor.matmul(NB, MEANC.to_broadcast([P, P]), TT[:, m % 2, :], start=m == 0,
                                     stop=m == KC - 1).then_inc(sq_used, 1)

            def mean(n):
                pe.wait_ge(sum_ready, LN_OF[n] + 1)
                nc.tensor.matmul(MB, MEANC.to_broadcast([P, P]), TT[:, 2, :], start=True,
                                 stop=True).then_inc(mean_ready, 1)

            pe.wait_ge(const_ready, 6)
            norm(N_X)
            for i, part in enumerate(ADA_PARTS):
                pe.wait_ge(ada_sum, i + 1)
                for m in range(part * KC, (part + 1) * KC):
                    mm = nc.tensor.matmul(PS[:, 5 + i // 2, m:m + 1], ADAS[:, m * P:(m + 1) * P], ONEC, start=True, stop=True)
                mm.then_inc(ada_ps, 1)

            gemm("xbc", (hl, hl), normed(N_X))
            pe.wait_ge(sw_lo, 1)
            for k in range(KC):
                mm = product(PS[0:SMALL, 4, :], SWH[:, k, :], SWL[:, k, :], H[:, k, :], L[:, k, :], k == 0, k == KC - 1)
            mm.then_inc(dt_ps, 1)
            slot(Step(0), "q", (hl, hl))

            def xt(i):
                c, half = divmod(i, 2)
                if i >= 2:
                    pe.wait_ge(xt_used, i - 1)
                for j in range(4):
                    mm = nc.tensor.transpose(PS[:, 6 + i % 2, j * P:(j + 1) * P],
                                             XC[:, 4 * half + j, c * P:(c + 1) * P], IDENT[:])
                mm.then_inc(xt_ps, 1)

            pe.wait_ge(xc_ready, COUNT["xbc"])
            xt(0)
            xt(1)
            pe.wait_ge(dt_u, 1)
            for c in range(NT):
                mm = nc.tensor.transpose(PS[:, 4, c * P:(c + 1) * P], XC[:, KC, c * P:(c + 1) * P], IDENT[:])
            mm.then_inc(bt_ps, 1)
            slot(Step(1), "q", (hl, hl))
            pe.wait_ge(dt_rows, 1)
            src = [CS, SM[:, 3, :], SM[:, 1, :]]
            for i in range(3):
                for c in range(NT):
                    j = (i * NT + c) * SSM_HEADS
                    mm = nc.tensor.transpose(PS[:, 5, j:j + SSM_HEADS], src[i][0:SSM_HEADS, c * P:(c + 1) * P],
                                             IDENT[0:SSM_HEADS, 0:SSM_HEADS])
            mm.then_inc(tok_ps, 1)
            for i in range(2, 2 * NT):
                xt(i)
            pe.wait_ge(bt_ready, 1)
            pe.wait_ge(tok_ready, 1)
            for g in range(SSM_GROUPS):
                r = slice(g * SSM_N, (g + 1) * SSM_N)
                for c in range(NT):
                    cc = slice(c * P, (c + 1) * P)
                    mm = nc.tensor.matmul(PS[:, 4 + g, cc], XC[r, KC, cc], XC[r, KC + 1, cc], start=True, stop=True)
                mm.then_inc(cb_ps, 1)
            pe.wait_ge(csx_lo, 1)
            pe.wait_ge(sele_ready, 1)
            for r in range(HPG):
                if r < 2:
                    pe.wait_ge(xt_used, 2 * NT - 1 + r)
                else:
                    pe.wait_ge(e_exp, r - 1)
                nc.tensor.matmul(PS[:, 6 + r % 2, :], SELE[:, r, :], CSX[:], start=True, stop=True).then_inc(e_ps, 1)
            pe.wait_ge(cb_ready, 2)
            for c in range(NT - 1):
                if c:
                    pe.wait_ge(st_ready, c)
                for g in range(SSM_GROUPS):
                    mm = nc.tensor.matmul(PS[g * 64:g * 64 + 64, 5, :], BTOK[:, c, g * SSM_N:(g + 1) * SSM_N],
                                          XDD[:, c, g * T:(g + 1) * T], start=True, stop=True)
                mm.then_inc(st_ps, 1)

            def seg(h):
                if h < 2:
                    pe.wait_ge(e_exp, HPG - 1 + h)
                else:
                    pe.wait_ge(seg_ready, h - 1)
                ps = PS[:, 6 + h % 2, :]
                nc.tensor.matmul(ps, SEL[:, h:h + 1].to_broadcast([P, P]), CSX[:], start=True, stop=False)
                nc.tensor.matmul(ps, IDB[:], M_SSM[:].unsqueeze(1).to_broadcast([P, NT, P]), start=False,
                                 stop=True).then_inc(seg_ps, 1)

            def y(h):
                i, u = divmod(h, 2)
                g, r = divmod(h, HPG)
                pe.wait_ge(mt_ready, h + 1)
                if u == 0 and i >= 2:
                    pe.wait_ge(y_used, i - 1)
                if h == 0:
                    pe.wait_ge(st_ready, NT - 1)
                    pe.wait_ge(ce_ready, HPG)
                for c in range(NT):
                    cc = slice(c * P, (c + 1) * P)
                    ps = PS[u * 64:u * 64 + 64, 4 + i % 2, cc]
                    mm = nc.tensor.matmul(ps, XD[:, c, h * 64:h * 64 + 64], MT[:, h % 2, cc], start=c == 0,
                                          stop=True, skip_group_check=True)
                    if c:
                        mm = nc.tensor.matmul(ps, ST[g * 64:g * 64 + 64, c - 1, r * 64:r * 64 + 64],
                                              CE[g * 64:g * 64 + 64, r, cc], start=False, stop=True,
                                              skip_group_check=True)
                mm.then_inc(y_ps, 1)

            seg(0)
            for h in range(SSM_HEADS):
                if h + 1 < SSM_HEADS:
                    seg(h + 1)
                slot_step(2 * KC + h, "q", (hl, hl))
                y(h)
            gemm("z", (hl, hl))
            for j in range(COUNT["k"]):
                slot(Step(j), "k", (hl, hl))
                if j == 0:
                    norm(N_SSM)
            gemm("ssm_out", ((YHS, YL), hl), normed(N_SSM))
            token_major("v")

            def logits(i):
                h, qb = divmod(i, NT)
                n = (qb + 1) * P
                if i < 2:
                    pe.wait_ge(bank_free, GROUP0["v"] + COUNT["v"])
                else:
                    pe.wait_ge(p_exp, i - 1)
                ps = PS[:, 4 + i % 2, :]
                nc.tensor.matmul(ps[:, qb * P:n], IDB[:], M_FOX[:], start=True, stop=False, skip_group_check=True)
                nc.tensor.matmul(ps[:, 0:n], QK[:, h, qb * P:n], QK[:, KC + h, 0:n], start=False, stop=False,
                                 skip_group_check=True)
                nc.tensor.matmul(ps[:, 0:n], SEL[:, 32 + h:33 + h].to_broadcast([P, P]), CSX[:, 0:n], start=False,
                                 stop=True, skip_group_check=True).then_inc(lg_ready, 1)

            def turn(i):
                h, qb = divmod(i, NT)
                pe.wait_ge(pn_ready, i + 1)
                if i:
                    pe.wait_ge(pt_ready, i)
                for kc in range(qb + 1):
                    mm = nc.tensor.transpose(PS[:, 6, kc * P:(kc + 1) * P], TT[:, i % 2, kc * P:(kc + 1) * P], IDENT[:])
                mm.then_inc(tr_ready, 1)

            def values(h):
                pe.wait_ge(pt_ready, NT * (h + 1))
                if h:
                    pe.wait_ge(ot_ready, h)
                for kc in range(NT):
                    mm = nc.tensor.matmul(PS[:, 7, kc * P:T], VTOK_F[:, kc, h * P:(h + 1) * P], PT[:, kc, kc * P:T],
                                          start=kc == 0, stop=True, skip_group_check=True)
                mm.then_inc(pv_done, 1)

            n = NT * FOX_HEADS
            for i in range(n + 2):
                if i < n:
                    logits(i)
                    slot_step(i, "za", (hl, hl))
                if 1 <= i <= n:
                    turn(i - 1)
                if i >= 2 and (i - 2) % NT == NT - 1:
                    values((i - 2) // NT)

            gemm("att_out", ((YH, YLA), hl), (ya_lo, lambda k: k + 1))
            gemm("w_out", ((MH, ML), (MH, ML)), (mg_lo, lambda k: k + 1))
            norm(N_FINAL)

            def taps(s, ahead):
                p = s.odd(1, -ahead)
                pe.wait_ge(dg_ready, s.val(1, 1 - ahead))
                pe.wait_ge(hc_lo, s.val(1, 1 - ahead))
                for k in range(PE_TAPS):
                    mm = product(PS[:, 6 + p, :], DG[:, p, 0, k, :], DG[:, p, 1, k, :], HCH[:, p, k:k + T],
                                 HCL[:, p, k:k + T], k == 0, k == PE_TAPS - 1)
                mm.then_inc(cp_ps, 1)

            def pw1(s):
                first = isinstance(s.val(), int) and s.val() == 0
                slot(s, "pw1", (hl, hl), normed(N_FINAL) if first else None)
                if not first:
                    taps(s, 1)
            steps(pe, None, KC, 0, pw1, head=1)
            taps(Step(KC - 1), 0)
            mean(N_CONV)
            norm(N_CONV)
            gemm("pw2", (ylh, ylh), normed(N_CONV))

            def feed_forward(layer, n_mix, n_out):
                gate = f"gate{layer}"

                def ple(j):
                    if j >= 2:
                        pe.wait_ge(pg_used, KC // 2 * layer + j - 1)
                    for u in range(2):
                        m = 2 * j + u
                        for k in range(PC):
                            mm = product(PS[:, ple_bank(layer, j) + u, :], WPH[:, k, m * P:(m + 1) * P],
                                         WPL[:, k, m * P:(m + 1) * P], PPH[:, k, :], PPL[:, k, :], k == 0, k == PC - 1)
                    mm.then_inc(pg_ready, 1)

                pe.wait_ge(ple_lo, layer + 1)
                ple(0)
                mean(n_mix)
                norm(n_mix)
                for j in range(1, KC // 2):
                    ple(j)
                for j in range(COUNT[gate]):
                    if j == 1:
                        pe.wait_ge(pg_used, KC // 2 * (layer + 1))
                    slot(Step(j), gate, (hl, hl), normed(n_mix) if j == 0 else None)
                gemm(f"up{layer}", (hl, hl))
                down = f"down{layer}"

                def one(s):
                    for part in range(DOWN_S):
                        pe.wait_ge(ff_lo, FC * layer + min(KC * (part + 1), FC))
                        slot(s, down, ((FH, FL), (FH, FL)), last=part == DOWN_S - 1, mul=DOWN_S, part=part,
                             ks=min(KC, FC - part * KC))
                steps(pe, None, 4, 0, one)
                mean(n_out)
                norm(n_out)

            feed_forward(0, N_MIX0, N_OUT0)
            gemm("q1", (hl, hl), normed(N_OUT0))
            gemm("k1", (hl, hl))
            token_major("v1")

            def zs(h):
                pb, c = (h % 2) * 64, h // 2
                r = slice(pb, pb + 64)
                if h == 0:
                    pe.wait_ge(bank_free, GROUP0["v1"] + COUNT["v1"])
                if h >= 2:
                    pe.wait_ge(a_ready, h - 1)
                flat = PS[:, 4 * (h % 2):4 * (h % 2) + 3, :].rearrange("p b t -> p (b t)")
                for kc in (0, 1, 3, 2):
                    w = T - kc * P
                    reg = flat[:, SB_OFF[kc]:SB_OFF[kc] + w]
                    nc.tensor.matmul(reg, QK[r, KC + c, kc * P:(kc + 1) * P], QK[r, c, kc * P:T], start=kc != 3,
                                     stop=True, skip_group_check=True)
                    mm = nc.tensor.matmul(reg[:, 0:P], IDB[:], M_SB[:], start=False, stop=True, skip_group_check=True)
                mm.then_inc(sz_ps, 1)

            def tri(h):
                if h == 0:
                    pe.wait_ge(tri_ready, 1)
                flat = PS[:, 4 * (h % 2):4 * (h % 2) + 3, :].rearrange("p b t -> p (b t)")
                for ex, ready in ((EXH[h % 2], sp_hi), (EXL[h % 2], sp_lo)):
                    pe.wait_ge(ready, 2 * h + 1)
                    for kc in (1, 2, 3, 0):
                        if kc == 0:
                            pe.wait_ge(ready, 2 * h + 2)
                        for jc in range(kc, NT):
                            o = SB_OFF[kc] + (jc - kc) * P
                            w = T - jc * P
                            lhs = TRIR[:, 0:P] if kc == jc else TRIR[:, P:P + 1].to_broadcast([P, P])
                            mm = nc.tensor.matmul(flat[:, o:o + w], lhs, ex[:, SB_OFF[jc]:SB_OFF[jc] + w],
                                                  start=False, stop=True, skip_group_check=True)
                mm.then_inc(tri_done, 1)

            def sb_values(h):
                pb = (h % 2) * 64
                pe.wait_ge(a_ready, h + 1)
                if h >= 2:
                    pe.wait_ge(so_ready, h - 1)
                for kc in range(NT):
                    mm = nc.tensor.matmul(PS[pb:pb + 64, 4 * (h % 2) + 3, kc * P:T], VTOK[:, kc, h * 64:h * 64 + 64],
                                          AT[h % 2][:, SB_OFF[kc]:SB_OFF[kc] + T - kc * P], start=kc == 0,
                                          stop=True, skip_group_check=True)
                mm.then_inc(sb_pv, 1)

            for i in range(SB_HEADS + 2):
                if i < SB_HEADS:
                    zs(i)
                if 1 <= i <= SB_HEADS:
                    tri(i - 1)
                if i >= 2:
                    sb_values(i - 2)
            gemm("wo", (ylh, ylh), (so_lo, lambda k: k + 1))
            feed_forward(1, N_MIX1, N_OUT1)

        @block.scalar
        def _(act):
            own = Chain(act, act_own)
            a = nc.scalar.activation
            tables = nc.scalar.preload_act_table_set

            def split_hi(s, mul, g):
                if isinstance(s.val(), int) and s.val(mul, g) >= NSLOTS:
                    return
                p = s.odd(mul, g)
                act.wait_ge(raw_in[p], 16 * s.half(mul, g) + 16)
                if not (isinstance(s.val(), int) and s.val(mul, g) < 2):
                    act.wait_ge(slot_done, s.val(mul, g - 1))
                a(WH[:, p], RAW[:, p], ACT.Copy).then_inc(w_hi, 1)

            def slots(stage, body, per=0, tail=0, head=0):
                g0 = SLOT0[stage]

                def one(s):
                    split_hi(s, 1, g0 + 1)
                    body(s, s.odd(1, GROUP0[stage]))
                steps(act, own, COUNT[stage], per, one, tail=tail, head=head)

            def evacuated(s, stage):
                act.wait_ge(slot_done, s.val(1, SLOT0[stage] + 1))

            def squares(n, src, ready=None):
                tables("sqrt_and_others")
                for m in range(KC):
                    if ready:
                        act.wait_ge(ready[0], ready[1] + m + 1)
                    if KC * n + m >= 2:
                        act.wait_ge(sq_used, KC * n + m - 1)
                    a(TT[:, m % 2, :], src[:, m, :], ACT.Square).then_inc(sq_ready, 1)
                act.wait_ge(sq_used, KC * (n + 1))
                a(TT[:, 2, :], NB, ACT.Sqrt, bias=EPS_LN if n in LN_OF else EPS_RMS).then_inc(std_ready, 1)

            def norm_hi(n, dst, hi, bias=None, func=ACT.Identity, ms=range(KC)):
                for m in ms:
                    act.wait_ge(t_ready, KC * n + m + 1)
                    if bias is None:
                        a(hi[:, m, :], dst[:, m, :], ACT.Copy).then_inc(hi_ready, 1)
                    else:
                        a(hi[:, m, :], dst[:, m, :], func, bias=bias(m))
                        a(dst[:, m, :], dst[:, m, :], func, bias=bias(m)).then_inc(hi_ready, 1)

            for k in range(KC):
                act.dma_start(ADA[k][:], w_ada[k]).then_inc(ada_in[k], 16)
            act.wait_ge(par_in, 16)
            a(CSIL[:], col("c", 0, KC), ACT.Silu).then_inc(c_ready, 1)
            a(AEXP[0:SSM_HEADS], PAR[0:SSM_HEADS, PCOL["a_log"]:PCOL["a_log"] + 1], ACT.Exp).then_inc(c_ready, 1)
            act.wait_ge(sw_in, 16)
            a(SWH[:], SWR[:], ACT.Copy).then_inc(sw_hi, 1)
            act.wait_ge(x_in, 16)
            act.wait_ge(const_ready, 6)
            squares(N_X, X)
            split_hi(Step(0), 1, 0)
            act.wait_ge(ada_ready, 1)
            for m in range(KC):
                act.wait_ge(t_ready, m + 1)
                a(H[:, m, :], XN[:, m, :], ACT.Identity, bias=ADAV[:, m:m + 1], scale=GX[:, m:m + 1])
                a(XN[:, m, :], XN[:, m, :], ACT.Identity, bias=ADAV[:, m:m + 1],
                  scale=GX[:, m:m + 1]).then_inc(hi_ready, 1)

            def xbc(s, p):
                if s.first == COUNT["xbc"] - 1:
                    split_hi(Step(0), 1, SLOT0["q"] + 1)
                act.wait_ge(bank_free, s.val(1, GROUP0["xbc"] + 1))
                xc = rows(XC, s.val(2), 2)
                a(xc, xc, ACT.Silu).then_inc(xc_ready, 1)
            tables("silu_and_others")
            slots("xbc", xbc, head=2, tail=1)

            act.wait_ge(dt_u, 2)
            a(SM[0:SMALL, 1, :], SM[0:SMALL, 1, :], ACT.Exp).then_inc(dt_e, 1)
            act.wait_ge(dt_w, 1)
            a(SM[0:SMALL, 3, :], SM[0:SMALL, 2, :], ACT.Ln).then_inc(dt_l, 1)
            act.wait_ge(bt_ps, 1)
            a(BTOK[:].rearrange("p c n -> p (c n)"), PS[:, 4, :], ACT.Copy).then_inc(bt_ready, 1)
            act.wait_ge(cs_ready, 1)
            a(CSX[0:64], CS[0:64], ACT.Copy).then_inc(csx_hi, 1)
            act.wait_ge(dt_x, 1)
            a(SM[0:SSM_HEADS, 1, :], SM[0:SSM_HEADS, 1, :], ACT.Exp).then_inc(dt_d, 1)
            act.wait_ge(cb_ps, 2)
            for g in range(SSM_GROUPS):
                a(CBM[:, g, :], PS[:, 4 + g, :], ACT.Copy).then_inc(cb_ready, 1)
            for r in range(HPG):
                act.wait_ge(e_ps, r + 1)
                a(EL[:, r, :], PS[:, 6 + r % 2, P - 1::P], ACT.Exp)
                a(CE[:, r, :], PS[:, 6 + r % 2, :], ACT.Exp).then_inc(e_exp, 1)
            def copy(stage, dst, m0, scale):
                def body(s, p):
                    evacuated(s, stage)
                    act.wait_ge(bank_free, s.val(1, GROUP0[stage]))
                    a(rows(dst, s.val(2, m0), 2), PS[:, 2 * p:2 * p + 2, :], ACT.Copy,
                      scale=scale).then_inc(bank_free, 1)
                return body

            q_copy = copy("q", QK, 0, float(P ** -0.5))
            split_hi(Step(1), 1, SLOT0["q"] + 1)
            act.wait_ge(st_ps, NT - 1)
            for j in range(2):
                q_copy(Step(j), (GROUP0["q"] + j) % 2)
            for h in range(SSM_HEADS):
                if h % KC == 1:
                    split_hi(Step(2 + h // KC), 1, SLOT0["q"] + 1)
                if h == KC + 2:
                    q_copy(Step(2), (GROUP0["q"] + 2) % 2)
                act.wait_ge(seg_ready, h + 1)
                a(MT[:, h % 2, :], MT[:, h % 2, :], ACT.Exp).then_inc(seg_exp, 1)

            def z(s, p):
                evacuated(s, "z")
                act.wait_ge(bank_free, s.val(1, GROUP0["z"]))
                a(rows(ZS, s.val(2), 2), PS[:, 2 * p:2 * p + 2, :], ACT.Silu).then_inc(bank_free, 1)
            tables("silu_and_others")
            q_copy(Step(3), (GROUP0["q"] + 3) % 2)
            act.wait_ge(y_ps, SSM_HEADS)
            slots("z", z)

            def gates(stage, bias0, name):
                def body(s, p):
                    evacuated(s, stage)
                    a(TT[:, p, :], PS[:, 2 * p + 1, :], ACT.Sigmoid,
                      bias=dcol(name, s.val(1, bias0))).then_inc(sig_ready, 1)
                return body

            def v_copy(stage, vtok):
                def body(s, p):
                    evacuated(s, stage)
                    f = s.val(2 * P)
                    dst = vtok[:, :, f:f + 2 * P] if isinstance(f, int) else vtok[:, :, bass.ds(f, 2 * P)]
                    a(dst, PS[:, 2 * p:2 * p + 2, :].rearrange("p b (c f) -> p (b c) f", c=2),
                      ACT.Copy).then_inc(bank_free, 1)
                return body

            for j in range(COUNT["k"]):
                split_hi(Step(j), 1, SLOT0["k"] + 1)
                if j == 0:
                    squares(N_SSM, XC, (yz_ready, 0))
                else:
                    norm_hi(N_SSM, XC, YHS, ms=K_PART[j])
                copy("k", QK, KC, 1.0)(Step(j), (GROUP0["k"] + j) % 2)
            tables("sigmoid_and_others")
            slots("ssm_out", gates("ssm_out", 0, "b_gate"))
            slots("v", v_copy("v", VTOK_F))

            tables("exp_and_others")
            def p_turned(i):
                h, qb = divmod(i, NT)
                act.wait_ge(tr_ready, i + 1)
                if qb == 0 and h:
                    act.wait_ge(pv_done, h)
                a(PT[:, 0:qb + 1, qb * P:(qb + 1) * P],
                  PS[:, 6, 0:(qb + 1) * P].rearrange("p (k q) -> p k q", q=P), ACT.Copy).then_inc(pt_ready, 1)

            n = NT * FOX_HEADS
            def za(j):
                act.wait_ge(slot_done, SLOT0["za"] + j + 1)
                act.wait_ge(bank_free, GROUP0["za"] + j)
                b = (GROUP0["za"] + j) % 2
                a(ZA[:, 2 * j:2 * j + 2, :], PS[:, 2 * b:2 * b + 2, :], ACT.Silu).then_inc(bank_free, 1)

            def gated_hi(m):
                act.wait_ge(ya_ready, m + 1)
                a(YH[:, m, :], QK[:, m, :], ACT.Copy).then_inc(ya_hi, 1)

            for i in range(n + 1):
                j = i // KC
                if i % KC == 2:
                    split_hi(Step(j), 1, SLOT0["za"] + 1)
                if i % KC == 4 and j:
                    za(j - 1)
                if i < n:
                    w_ = (i % NT + 1) * P
                    act.wait_ge(nm_ready, i + 1)
                    if i >= 2:
                        act.wait_ge(tr_ready, i - 1)
                    a(TT[:, i % 2, 0:w_], PS[:, 4 + i % 2, 0:w_], ACT.Exp, bias=STAT[:, 0, i:i + 1],
                      accum_out=STAT[:, 1, i:i + 1]).then_inc(p_exp, 1)
                if i:
                    p_turned(i - 1)
                if i % NT == 1 and i // NT >= GATE_LAG:
                    gated_hi(i // NT - GATE_LAG)
            gated_hi(FOX_HEADS - GATE_LAG)
            za(COUNT["za"] - 1)
            for m in range(FOX_HEADS - GATE_LAG + 1, FOX_HEADS):
                gated_hi(m)

            tables("sigmoid_and_others")
            def att_out(s, p):
                gates("att_out", KC, "b_gate")(s, p)
                act.wait_ge(mg_ready, s.val(1, 1))
                a(rows(MH, s.val(), 1), rows(P1, s.val(), 1), ACT.Copy).then_inc(mg_hi, 1)
            slots("att_out", att_out)
            slots("w_out", lambda s, p: None)
            act.wait_ge(bank_free, GROUP0["w_out"] + COUNT["w_out"])
            squares(N_FINAL, X)
            norm_hi(N_FINAL, X, H)

            def load_ple(layer):
                act.dma_start(PWR[:], w_ple[layer]).then_inc(ple_in, 16)
                act.dma_start(PR[:], p_t[layer]).then_inc(ple_in, 16)

            def split_ple_hi(layer):
                act.wait_ge(ple_in, 32 * (layer + 1))
                a(WPH[:], PWR[:], ACT.Copy)
                a(PPH[:], PR[:], ACT.Copy).then_inc(ple_hi, 1)

            tables("sigmoid_and_others")
            a(DW[:, 0, :], col("dw_w", 0, PE_TAPS * KC), ACT.Copy).then_inc(dw_hi, 1)

            def pw1(s, p):
                gates("pw1", KC, "pw1_b")(s, p)
                act.wait_ge(bank_free, s.val(1, GROUP0["pw1"] + 1))
                q = s.odd()
                a(HCH[:, q:q + 1, :], rows(HC, s.val(), 1), ACT.Copy).then_inc(hc_hi, 1)
            slots("pw1", pw1)
            act.wait_ge(sum_ready, LN_OF[N_CONV] + 1)
            load_ple(0)
            squares(N_CONV, CV, (cen_ready, KC * LN_OF[N_CONV]))
            tables("silu_and_others")
            norm_hi(N_CONV, CV, YH, lambda m: col("ln_b", m), ACT.Silu)
            split_ple_hi(0)
            slots("pw2", lambda s, p: None)

            def feed_forward(layer, n_mix, n_out):
                def ple(j):
                    act.wait_ge(pg_ready, KC // 2 * layer + j + 1)
                    b = ple_bank(layer, j)
                    a(PO[:, 2 * j:2 * j + 2, :], PS[:, b:b + 2, :], ACT.Copy).then_inc(pg_used, 1)

                ple(0)
                squares(n_mix, X, (cen_ready, KC * LN_OF[n_mix]))
                ple(1)
                for j in range(4):
                    norm_hi(n_mix, X, H, lambda m: col("mix_b", KC * layer + m), ms=range(2 * j, 2 * j + 2))
                    if j in (0, 2):
                        ple(2 + j // 2)
                gate = f"gate{layer}"

                def gate_body(s, p):
                    evacuated(s, gate)
                    act.wait_ge(bank_free, s.val(1, GROUP0[gate]))
                    a(TT[:, 0:2, :], PS[:, 2 * p:2 * p + 2, :], ACT.Sigmoid).then_inc(sig_ready, 1)
                tables("sigmoid_and_others")
                slots(gate, gate_body)
                up = f"up{layer}"

                def up_body(s, p):
                    act.wait_ge(gc_ready, s.val(1, FC * layer + 1))
                    a(TT[:, p, :], TT[:, 3, :], ACT.Silu).then_inc(sl_ready, 1)
                    act.wait_ge(bank_free, s.val(1, GROUP0[up] + 1))
                    a(rows(FH, s.val(), 1), TT[:, 3:4, :], ACT.Copy).then_inc(ff_hi, 1)
                tables("silu_and_others")
                slots(up, up_body)
                down = f"down{layer}"

                def down_one(s):
                    for part in range(DOWN_S):
                        split_hi(s, DOWN_S, SLOT0[down] + part + 1)
                steps(act, own, 4, 0, down_one, tail=2 if layer else 0)
                squares(n_out, X, (cen_ready, KC * LN_OF[n_out]))

            feed_forward(0, N_MIX0, N_OUT0)
            norm_hi(N_OUT0, X, H, lambda m: col("out_b", m))
            slots("q1", copy("q1", QK, 0, float(SB_DIM ** -0.5)))
            slots("k1", copy("k1", QK, KC, 1.0))
            slots("v1", v_copy("v1", VTOK))

            tables("natural_log_exp_and_others")

            def weights(h):
                flat = PS[:, 4 * (h % 2):4 * (h % 2) + 3, :].rearrange("p b t -> p (b t)")[:, 0:SBC]
                act.wait_ge(tri_done, h + 1)
                if h >= 2:
                    act.wait_ge(sb_pv, h - 1)
                a(AT[h % 2][:], flat, ACT.Exp).then_inc(a_ready, 1)

            for i in range(SB_HEADS):
                ex = EX[i % 2]
                flat = PS[:, 4 * (i % 2):4 * (i % 2) + 3, :].rearrange("p b t -> p (b t)")[:, 0:SBC]
                act.wait_ge(sz_ps, i + 1)
                own.did(a(ex[:], flat, ACT.Abs))
                own.settle()
                own.did(a(ex[:], ex[:], ACT.Exp, scale=-1.0))
                if i:
                    weights(i - 1)
                own.settle()
                for cc in SB_PARTS:
                    a(ex[:, cc], ex[:, cc], ACT.Ln, bias=1.0).then_inc(sz_exp, 1)
                for n, cc in enumerate(SB_PARTS):
                    act.wait_ge(sp_ready, 2 * i + n + 1)
                    a(EXH[i % 2][:, cc], ex[:, cc], ACT.Copy).then_inc(sp_hi, 1)
            weights(SB_HEADS - 1)
            act.wait_ge(so_ready, SB_HEADS)
            for m in range(KC):
                a(YH[:, m, :], QK[:, m, :], ACT.Copy).then_inc(so_hi, 1)
            act.wait_ge(so_lo, KC)
            load_ple(1)
            slots("wo", lambda s, p: s.first == 2 and split_ple_hi(1), head=COUNT["wo"])
            feed_forward(1, N_MIX1, N_OUT1)
            for m in range(KC):
                act.wait_ge(t_ready, KC * N_OUT1 + m + 1)
                a(X[:, m, :], X[:, m, :], ACT.Identity, bias=col("out_b", KC + m)).then_inc(out_ready, 1)

        @block.vector
        def _(dve):
            own = Chain(dve, dve_own)
            v = nc.vector
            acc, tmp = TT[:, 2, :], TT[:, 3, :]

            def split_lo(s, mul, g):
                if isinstance(s.val(), int) and s.val(mul, g) >= NSLOTS:
                    return
                p = s.odd(mul, g)
                dve.wait_ge(w_hi, s.val(mul, g + 1))
                v.tensor_tensor(WL[:, p], RAW[:, p], WH[:, p].bitcast(F32), ALU.subtract).then_inc(w_lo, 1)

            def slots(stage, body, per=0, tail=0, head=0):
                g0 = SLOT0[stage]

                def one(s):
                    split_lo(s, 1, g0 + 1)
                    body(s, s.odd(1, GROUP0[stage]))
                steps(dve, own, COUNT[stage], per, one, tail=tail, head=head)

            def evacuated(s, stage, mul=1, more=0):
                dve.wait_ge(slot_done, s.val(mul, SLOT0[stage] + 1 + more))

            def free(s, stage, ins):
                ins.then_inc(bank_free, 1)

            def earlier_free(s, stage):
                dve.wait_ge(bank_free, s.val(1, GROUP0[stage]))

            def norm_out(n, src, dst, g, hi=None, lo=None, ms=range(KC)):
                if 0 in ms:
                    dve.wait_ge(std_ready, n + 1)
                    own.did(v.reciprocal(acc, acc))
                    own.settle()

                def low(m):
                    dve.wait_ge(hi_ready, KC * n + m + 1)
                    v.tensor_tensor(lo[:, m, :], dst[:, m, :], hi[:, m, :].bitcast(F32),
                                    ALU.subtract).then_inc(h_ready, 1)
                for m in ms:
                    v.scalar_tensor_tensor(dst[:, m, :], src[:, m, :], g(m), acc, ALU.mult,
                                           ALU.mult).then_inc(t_ready, 1)
                    if m > ms[0] and lo is not None:
                        low(m - 1)
                if lo is not None and ms:
                    low(ms[-1])

            def center(n, src):
                dve.wait_ge(mean_ready, LN_OF[n] + 1)
                for m in range(KC):
                    v.tensor_tensor(src[:, m, :], src[:, m, :], MB, ALU.subtract).then_inc(cen_ready, 1)

            dve.wait_ge(const_ready, 6)
            own.did(v.tensor_tensor(SEL[:], IDENT[:, 0:64], IDENT[:, 64:P], ALU.add))
            own.did(v.tensor_copy(TRIR[:, 0:P], TRI[:]))
            v.tensor_copy(TRIR[:, P:P + 1], NEGC).then_inc(tri_ready, 1)
            dve.wait_ge(c_ready, 2)
            dve.wait_ge(sw_hi, 1)
            v.tensor_tensor(SWL[:], SWR[:], SWH[:].bitcast(F32), ALU.subtract).then_inc(sw_lo, 1)
            for k in range(KC):
                if k == 4:
                    dve.wait_ge(std_ready, N_X + 1)
                    own.did(v.reciprocal(acc, acc))
                    own.settle()
                if k >= 4:
                    for m in range(2 * k - 8, 2 * k - 6):
                        v.tensor_tensor(XN[:, m, :], X[:, m, :], acc, ALU.mult).then_inc(t_ready, 1)
                dve.wait_ge(ada_in[k], 16)
                if k == 0:
                    own.did(v.tensor_scalar(ADAS[:], ADA[0][:], CSIL[:, 0:1], None, ALU.mult))
                    continue
                own.settle()
                for part in ADA_PARTS if k == KC - 1 else (0,):
                    cc = slice(part * D, (part + 1) * D) if k == KC - 1 else slice(0, 3 * D)
                    ins = v.scalar_tensor_tensor(ADAS[:, cc], ADA[k][:, cc], CSIL[:, k:k + 1], ADAS[:, cc], ALU.mult,
                                                 ALU.add)
                    if k == KC - 1:
                        ins.then_inc(ada_sum, 1)
                    else:
                        own.did(ins)
            split_lo(Step(0), 1, 0)

            def modulation(part):
                cc = slice(part * KC, (part + 1) * KC)
                own.did(v.tensor_tensor(ADAV[:, cc], PS[:, 5 + part // 2, cc], col("b_ada", part * KC, KC), ALU.add))

            dve.wait_ge(par_in, 16)
            dve.wait_ge(ada_ps, 2)
            modulation(1)
            own.settle()
            own.did(v.tensor_scalar(GX[:], ADAV[:, KC:2 * KC], 1.0, None, ALU.add))
            modulation(0)
            own.settle()
            v.tensor_tensor(GX[:], GX[:], col("norm_w", 0, KC), ALU.mult).then_inc(ada_ready, 1)
            for m in range(KC):
                dve.wait_ge(hi_ready, m + 1)
                v.tensor_tensor(L[:, m, :], XN[:, m, :], H[:, m, :].bitcast(F32), ALU.subtract).then_inc(h_ready, 1)
            dve.wait_ge(ada_ps, 3)
            modulation(2)
            sel = SEL[:, 0:SSM_HEADS].bitcast(F32).rearrange("p (g r) -> p g r", g=SSM_GROUPS)
            for g in range(SSM_GROUPS):
                ins = v.tensor_copy(SELE[:, :, g * 64:g * 64 + 64], sel[:, g, :].unsqueeze(2).to_broadcast([P, HPG, 64]))
            ins.then_inc(sele_ready, 1)

            def xbc(s, p):
                evacuated(s, "xbc")
                for tap in range(CONV_K):
                    d = tap
                    for u in range(2):
                        m = s.val(2, u)
                        w_ = dcol("conv_w", s.val(2, u + (CONV_K - 1 - tap) * XBC_C))
                        dst = rows(XC, m, 1)
                        ps = PS[:, 2 * p + u:2 * p + u + 1, :]
                        if tap == 0:
                            own.did(v.tensor_scalar(dst, ps, w_, dcol("conv_b", m), ALU.mult, ALU.add))
                        else:
                            ins = v.scalar_tensor_tensor(dst[:, :, d:T], ps[:, :, 0:T - d], w_, dst[:, :, d:T],
                                                         ALU.mult, ALU.add)
                            if tap == CONV_K - 1 and u == 1:
                                free(s, "xbc", ins)
                            else:
                                own.did(ins)
                    if tap < CONV_K - 1:
                        own.settle()
            slots("xbc", xbc, per=2 * CONV_K - 1)

            R = slice(0, SMALL)
            U, E, W1, LN1 = (SM[R, i, :] for i in range(4))
            T0, T1, T2, T3 = (TT[R, i, :] for i in range(4))
            dve.wait_ge(dt_ps, 1)
            v.tensor_scalar(U, PS[R, 4, :], PAR[R, PCOL["small_b"]:PCOL["small_b"] + 1], SGN[R], ALU.add,
                            ALU.mult).then_inc(dt_u, 1)
            dve.wait_ge(dt_u, 1)
            v.scalar_tensor_tensor(E, U, -1.0, U, ALU.mult, ALU.min).then_inc(dt_u, 1)
            split_lo(Step(0), 1, SLOT0["q"] + 1)
            dve.wait_ge(dt_e, 1)
            v.tensor_scalar(W1, E, 1.0, None, ALU.add).then_inc(dt_w, 1)
            dve.wait_ge(dt_w, 1)
            own.did(v.tensor_scalar(T0, W1, -1.0, HALF_ULP, ALU.add, ALU.max))
            own.did(v.tensor_scalar(T1, W1, 1.0, None, ALU.is_equal))
            own.settle()
            own.did(v.reciprocal(T0, T0))
            own.did(v.tensor_tensor(T1, T1, E, ALU.mult))
            own.settle()
            own.did(v.tensor_tensor(T0, T0, E, ALU.mult))
            dve.wait_ge(dt_l, 1)
            own.settle()
            own.did(v.tensor_tensor(T0, T0, LN1, ALU.mult))
            own.settle()
            own.did(v.tensor_tensor(T0, T0, T1, ALU.add))
            own.settle()
            own.did(v.scalar_tensor_tensor(LN1, U, 0.0, T0, ALU.max, ALU.add))
            own.settle()
            S = slice(0, SSM_HEADS)
            own.did(v.tensor_scalar(T2[S], LN1[S], AEXP[S], -1.0, ALU.mult, ALU.mult))
            own.settle()
            for c in range(NT):
                cc = slice(c * P, (c + 1) * P)
                own.did(v.tensor_tensor_scan(CS[S, cc], ONEC[S].to_broadcast([SSM_HEADS, P]), T2[S, cc], 0.0, ALU.mult,
                                             ALU.add))
            Fr = slice(32, 32 + FOX_HEADS)
            v.tensor_tensor_scan(CS[Fr, :], ONEC[Fr].to_broadcast([FOX_HEADS, T]), SM[Fr, 3, :], 0.0, ALU.mult,
                                 ALU.add).then_inc(cs_ready, 1)
            own.settle()
            cs = CS[S, :].rearrange("h (c t) -> h c t", c=NT)
            v.tensor_tensor(SM[S, 1, :].rearrange("h (c t) -> h c t", c=NT),
                            cs[:, :, P - 1:P].to_broadcast([SSM_HEADS, NT, P]), cs, ALU.subtract).then_inc(dt_x, 1)
            dve.wait_ge(csx_hi, 1)
            v.tensor_tensor(CSX[64:P], CS[0:64], CSX[0:64].bitcast(F32), ALU.subtract).then_inc(csx_lo, 1)
            dve.wait_ge(dt_d, 1)
            v.tensor_tensor(SM[S, 1, :], SM[S, 1, :], SM[S, 3, :], ALU.mult).then_inc(dt_rows, 1)
            dve.wait_ge(tok_ps, 1)
            v.tensor_copy(TOK[:].rearrange("p a c h -> p (a c h)"),
                          PS[:, 5, 0:3 * NT * SSM_HEADS]).then_inc(tok_ready, 1)
            dve.wait_ge(tok_ready, 1)

            for i in range(2 * NT):
                c, half = divmod(i, 2)
                dve.wait_ge(xt_ps, i + 1)
                ps = PS[:, 6 + i % 2, :].rearrange("p (h d) -> p h d", d=SSM_P)
                hs = slice(half * 8, half * 8 + 8)
                fs = slice(half * T, (half + 1) * T)

                def scaled(dst, which):
                    return v.tensor_tensor(dst[:, c, fs].rearrange("p (h d) -> p h d", d=SSM_P), ps,
                                           TOK[:, which, c, hs].unsqueeze(2).to_broadcast([P, 8, SSM_P]), ALU.mult)
                ins = scaled(XD, 1)
                if c < NT - 1:
                    own.did(ins)
                    ins = scaled(XDD, 2)
                ins.then_inc(xt_used, 1)
            for r in range(HPG):
                dve.wait_ge(e_exp, r + 1)
                v.tensor_tensor(CE[:, r, :], CE[:, r, :], XC[:, KC + 1, :], ALU.mult).then_inc(ce_ready, 1)
            for c in range(NT - 1):
                dve.wait_ge(st_ps, c + 1)
                if c == 0:
                    v.tensor_copy(ST[:, 0, :], PS[:, 5, :]).then_inc(st_ready, 1)
                else:
                    own.did(v.tensor_tensor(ST[:, c, :].rearrange("p (r d) -> p r d", d=SSM_P),
                                            ST[:, c - 1, :].rearrange("p (r d) -> p r d", d=SSM_P),
                                            EL[:, :, c:c + 1].to_broadcast([P, HPG, SSM_P]), ALU.mult))
                    own.settle()
                    v.tensor_tensor(ST[:, c, :], ST[:, c, :], PS[:, 5, :], ALU.add).then_inc(st_ready, 1)
                dve.wait_ge(st_ready, c + 1)

            def seg(h):
                dve.wait_ge(seg_ps, h + 1)
                if h >= 2:
                    dve.wait_ge(y_ps, h - 1)
                v.tensor_tensor(MT[:, h % 2, :].rearrange("p (c t) -> p c t", c=NT),
                                PS[:, 6 + h % 2, :].rearrange("p (c t) -> p c t", c=NT),
                                TOK[:, 0, :, h:h + 1].to_broadcast([P, NT, P]), ALU.subtract).then_inc(seg_ready, 1)

            dve.wait_ge(cb_ready, 2)
            split_lo(Step(1), 1, SLOT0["q"] + 1)
            seg(0)
            for h in range(SSM_HEADS):
                if h % KC == 1:
                    split_lo(Step(2 + h // KC), 1, SLOT0["q"] + 1)
                if h + 1 < SSM_HEADS:
                    seg(h + 1)
                dve.wait_ge(seg_exp, h + 1)
                v.tensor_tensor(MT[:, h % 2, :], MT[:, h % 2, :], CBM[:, h // HPG, :], ALU.mult).then_inc(mt_ready, 1)
                if h % 2 == 0 and h:
                    i = h // 2 - 1
                    dve.wait_ge(y_ps, 2 * i + 2)
                    v.scalar_tensor_tensor(XC[:, i, :], XC[:, i, :], col("d_skip", i), PS[:, 4 + i % 2, :], ALU.mult,
                                           ALU.add).then_inc(y_used, 1)
            i = KC - 1
            dve.wait_ge(y_ps, SSM_HEADS)
            v.scalar_tensor_tensor(XC[:, i, :], XC[:, i, :], col("d_skip", i), PS[:, 4 + i % 2, :], ALU.mult,
                                   ALU.add).then_inc(y_used, 1)
            dve.wait_ge(y_used, KC)
            slots("z", lambda s, p: None)
            for j in range(COUNT["k"]):
                split_lo(Step(j), 1, SLOT0["k"] + 1)
                if j == 0:
                    for m in range(KC):
                        dve.wait_ge(bank_free, GROUP0["z"] + m // 2 + 1)
                        v.tensor_tensor(XC[:, m, :], XC[:, m, :], ZS[:, m, :], ALU.mult).then_inc(yz_ready, 1)
                    dve.wait_ge(yz_ready, KC)
                else:
                    norm_out(N_SSM, XC, XC, lambda m: col("ssm_norm_w", m), YHS, YL, K_PART[j])

            def ssm_out(s, p):
                earlier_free(s, "ssm_out")
                dve.wait_ge(sig_ready, s.val(1, SIG0["ssm_out"] + 1))
                free(s, "ssm_out", v.tensor_tensor(rows(P1, s.val(), 1), PS[:, 2 * p:2 * p + 1, :], TT[:, p:p + 1, :],
                                                   ALU.mult))
            slots("ssm_out", ssm_out)
            slots("v", lambda s, p: None)

            n = NT * FOX_HEADS
            def gated(m):
                dve.wait_ge(bank_free, GROUP0["za"] + m // 2 + 1)
                v.tensor_tensor(QK[:, m, :], QK[:, m, :], ZA[:, m, :], ALU.mult).then_inc(ya_ready, 1)

            def gated_lo(m):
                dve.wait_ge(ya_hi, m + 1)
                v.tensor_tensor(YLA[:, m, :], QK[:, m, :], YH[:, m, :].bitcast(F32), ALU.subtract).then_inc(ya_lo, 1)

            def output(h):
                dve.wait_ge(pv_done, h + 1)
                v.tensor_copy(QK[:, h, :], PS[:, 7, :]).then_inc(ot_ready, 1)

            for i in range(n + 1):
                if i % KC == 2:
                    split_lo(Step(i // KC), 1, SLOT0["za"] + 1)
                if i < n:
                    w_ = (i % NT + 1) * P
                    dve.wait_ge(lg_ready, i + 1)
                    own.did(v.tensor_reduce(STAT[:, 2, i:i + 1], PS[:, 4 + i % 2, 0:w_], AX_X, ALU.max))
                    own.settle()
                    v.tensor_scalar(STAT[:, 0, i:i + 1], STAT[:, 2, i:i + 1], -1.0, None, ALU.mult).then_inc(nm_ready, 1)
                if i:
                    j = i - 1
                    h, qb = divmod(j, NT)
                    w_ = (qb + 1) * P
                    dve.wait_ge(p_exp, j + 1)
                    own.did(v.reciprocal(STAT[:, 2, j:j + 1], STAT[:, 1, j:j + 1]))
                    own.settle()
                    v.tensor_scalar(TT[:, j % 2, 0:w_], TT[:, j % 2, 0:w_], STAT[:, 2, j:j + 1], None,
                                    ALU.mult).then_inc(pn_ready, 1)
                    if qb == 1 and h:
                        output(h - 1)
                if i % NT == 0 and i // NT >= GATE_LAG and i < n:
                    dve.wait_ge(ot_ready, i // NT - GATE_LAG + 1)
                    gated(i // NT - GATE_LAG)
                if i % NT == 2 and i // NT >= GATE_LAG:
                    gated_lo(i // NT - GATE_LAG)
            dve.wait_ge(ot_ready, FOX_HEADS - 1)
            gated(FOX_HEADS - GATE_LAG)
            gated_lo(FOX_HEADS - GATE_LAG)
            for m in range(FOX_HEADS - GATE_LAG + 1, FOX_HEADS - 1):
                gated(m)
            output(FOX_HEADS - 1)
            dve.wait_ge(ot_ready, FOX_HEADS)
            gated(FOX_HEADS - 1)
            for m in range(FOX_HEADS - GATE_LAG + 1, FOX_HEADS):
                gated_lo(m)

            def att_out(s, p):
                earlier_free(s, "att_out")
                dve.wait_ge(sig_ready, s.val(1, SIG0["att_out"] + 1))
                ins = v.tensor_tensor(TT[:, p:p + 1, :], PS[:, 2 * p:2 * p + 1, :], TT[:, p:p + 1, :], ALU.mult)
                free(s, "att_out", ins)
                dve.wait_ge(bank_free, s.val(1, GROUP0["att_out"] + 1))
                p1 = rows(P1, s.val(), 1)
                v.tensor_tensor(p1, p1, TT[:, p:p + 1, :], ALU.add).then_inc(mg_ready, 1)
                dve.wait_ge(mg_hi, s.val(1, 1))
                v.tensor_tensor(rows(ML, s.val(), 1), p1, rows(MH, s.val(), 1).bitcast(F32),
                                ALU.subtract).then_inc(mg_lo, 1)
            slots("att_out", att_out)

            def w_out(s, p):
                evacuated(s, "w_out")
                for u in range(2):
                    x = rows(X, s.val(2, u), 1)
                    m = s.val(2, u + 2 * KC)
                    g = ADAV[:, m:m + 1] if isinstance(m, int) else ADAV[:, bass.ds(m, 1)]
                    ins = v.scalar_tensor_tensor(x, PS[:, 2 * p + u:2 * p + u + 1, :], g, x, ALU.mult, ALU.add)
                free(s, "w_out", ins)
            slots("w_out", w_out)
            norm_out(N_FINAL, X, X, lambda m: col("final_norm_w", m), H, L)

            own.did(v.memset(HC[:, :, 0:PAD], 0.0))

            dve.wait_ge(dw_hi, 1)
            own.did(v.tensor_tensor(DW[:, 1, :], col("dw_w", 0, PE_TAPS * KC), DW[:, 0, :].bitcast(F32), ALU.subtract))
            own.settle()
            own.did(v.memset(acc, 0.0))

            def taps_added(s, ahead, between=None):
                dve.wait_ge(cp_ps, s.val(1, 1 - ahead))
                cv = rows(CV, s.val(1, -ahead), 1)
                q = s.odd(1, -ahead)
                own.did(v.tensor_tensor(cv, cv, PS[:, 6 + q:7 + q, :], ALU.add))
                if between:
                    between()
                own.settle()
                own.did(v.tensor_tensor(TT[:, 2:3, :], TT[:, 2:3, :], cv, ALU.add))

            def pw1(s, p):
                dve.wait_ge(sig_ready, s.val(1, SIG0["pw1"] + 1))
                free(s, "pw1", v.scalar_tensor_tensor(rows(HC, s.val(), 1)[:, :, PAD:PAD + T],
                                                      PS[:, 2 * p:2 * p + 1, :], dcol("pw1_b", s.val()),
                                                      TT[:, p:p + 1, :], ALU.add, ALU.mult))
                dve.wait_ge(bank_free, s.val(1, GROUP0["pw1"] + 1))
                cv, hc = rows(CV, s.val(), 1), rows(HC, s.val(), 1)
                q, m = s.odd(), s.val()
                dw = DW[:].bitcast(F32).rearrange("p a (k m) -> p a k m", m=KC)
                v.tensor_copy(DWC[:, q].unsqueeze(3), dw[:, :, :, m:m + 1] if isinstance(m, int) else
                              dw[:, :, :, bass.ds(m, 1)]).then_inc(dwc_ready, 1)
                dsts = (cv, CVB[:])
                for n, k in enumerate(range(PE_TAPS, DW_K)):
                    w_ = dcol("dw_w", s.val(1, k * KC))
                    src, dst = hc[:, :, k:k + T], dsts[n % 2]
                    if n == 0:
                        own.did(v.tensor_scalar(dst, src, w_, dcol("dw_b", s.val()), ALU.mult, ALU.add))
                    elif n == 1:
                        own.did(v.tensor_scalar(dst, src, w_, None, ALU.mult))
                    else:
                        own.settle(1)
                        own.did(v.scalar_tensor_tensor(dst, src, w_, dst, ALU.mult, ALU.add))
                    if n == 2:
                        dve.wait_ge(hc_hi, s.val(1, 1))
                        v.tensor_tensor(HCL[:, q:q + 1, :], hc, HCH[:, q:q + 1, :].bitcast(F32),
                                        ALU.subtract).then_inc(hc_lo, 1)
                own.settle()
                both = lambda: own.did(v.tensor_tensor(cv, cv, CVB[:], ALU.add))
                if isinstance(s.val(), int) and s.val() == 0:
                    both()
                    own.settle()
                    own.did(v.memset(acc, 0.0))
                    own.settle()
                    own.did(v.memset(acc, 0.0))
                else:
                    taps_added(s, 1, both)
            slots("pw1", pw1, per=DW_K - PE_TAPS + 3, head=1)
            own.settle()
            taps_added(Step(KC - 1), 0)
            own.settle()
            v.tensor_copy(TT[:, 2, 0:1], TT[:, 2, 0:1]).then_inc(sum_ready, 1)
            center(N_CONV, CV)
            norm_out(N_CONV, CV, CV, lambda m: col("ln_g", m), YH, YL)
            for m in range(KC):
                own.did(v.tensor_scalar(X[:, m, :], X[:, m, :], ALPHA, col("pw2_b", m), ALU.mult, ALU.add))

            def split_ple_lo(layer):
                dve.wait_ge(ple_hi, layer + 1)
                own.did(v.tensor_tensor(WPL[:], PWR[:], WPH[:].bitcast(F32), ALU.subtract))
                v.tensor_tensor(PPL[:], PR[:], PPH[:].bitcast(F32), ALU.subtract).then_inc(ple_lo, 1)

            split_ple_lo(0)
            own.did(v.memset(acc, 0.0))
            own.settle()

            def sums(s, last=None):
                for u in range(2):
                    own.settle()
                    own.did(v.tensor_tensor(acc, acc, X[:, s.val(2, u), :] if isinstance(s.val(), int) else
                                            rows(X, s.val(2, u), 1).rearrange("p a t -> p (a t)"), ALU.add))

            def added(stage, mul=1, more=0, first=1.0):
                def body(s, p):
                    evacuated(s, stage, mul, more)
                    x = rows(X, s.val(2), 2)
                    ps = PS[:, 2 * p:2 * p + 2, :]
                    if first == 1.0:
                        ins = v.tensor_tensor(x, x, ps, ALU.add)
                    else:
                        ins = v.scalar_tensor_tensor(x, x, first, ps, ALU.mult, ALU.add)
                    free(s, stage, ins)
                    dve.wait_ge(bank_free, s.val(1, GROUP0[stage] + 1))
                    sums(s)
                return body
            slots("pw2", added("pw2"), per=2)

            def ln_front(n):
                own.settle()
                v.tensor_copy(X[:, 0, 0:1], X[:, 0, 0:1]).then_inc(sum_ready, 1)
                center(n, X)

            def feed_forward(layer, n_mix, n_out, g_out):
                ln_front(n_mix)
                norm_out(n_mix, X, X, lambda m: col("mix_g", KC * layer + m), H, L)
                gate = f"gate{layer}"

                def gate_body(s, p):
                    dve.wait_ge(sig_ready, s.val(1, SIG0[gate] + 1))
                    dve.wait_ge(pg_used, s.val(1, COUNT[gate] * layer + 1))
                    own.did(v.tensor_tensor(TT[:, 0:2, :], TT[:, 0:2, :], rows(PO, s.val(2), 2), ALU.mult))
                    own.settle()
                    x = rows(X, s.val(2), 2)
                    free(s, gate, v.scalar_tensor_tensor(x, x, ALPHA, TT[:, 0:2, :], ALU.mult, ALU.add))
                slots(gate, gate_body, per=1)
                up = f"up{layer}"

                def up_body(s, p):
                    evacuated(s, up)
                    gate_ps = PS[:, 2 * p + 1:2 * p + 2, :]
                    c = TT[:, 3:4, :]
                    if not (isinstance(s.val(), int) and s.val(1, layer) == 0):
                        dve.wait_ge(ff_lo, s.val(1, FC * layer))
                    for d in range(FCONV_K):
                        w_ = dcol("fconv_w", s.val(1, (layer * FCONV_K + FCONV_K - 1 - d) * FC))
                        if d == 0:
                            own.did(v.tensor_scalar(c, gate_ps, w_, dcol("fconv_b", s.val(1, layer * FC)), ALU.mult,
                                                    ALU.add))
                            own.settle()
                        else:
                            ins = v.scalar_tensor_tensor(c[:, :, d:T], gate_ps[:, :, 0:T - d], w_, c[:, :, d:T],
                                                         ALU.mult, ALU.add)
                            if d == FCONV_K - 1:
                                ins.then_inc(gc_ready, 1)
                            else:
                                own.did(ins)
                                own.settle()
                    dve.wait_ge(sl_ready, s.val(1, FC * layer + 1))
                    free(s, up, v.tensor_tensor(c, TT[:, p:p + 1, :], PS[:, 2 * p:2 * p + 1, :], ALU.mult))
                    dve.wait_ge(ff_hi, s.val(1, FC * layer + 1))
                    v.tensor_tensor(rows(FL, s.val(), 1), c, rows(FH, s.val(), 1).bitcast(F32),
                                    ALU.subtract).then_inc(ff_lo, 1)
                slots(up, up_body, per=FCONV_K - 1, head=1)
                own.did(v.memset(acc, 0.0))
                down = f"down{layer}"

                def down_one(s):
                    for part in range(DOWN_S):
                        split_lo(s, DOWN_S, SLOT0[down] + part + 1)
                    added(down, DOWN_S, DOWN_S - 1)(s, s.odd(1, GROUP0[down]))
                steps(dve, own, 4, 2, down_one, tail=2 if layer else 0)
                ln_front(n_out)
                if layer == 0:
                    norm_out(n_out, X, X, g_out, H, L)
                else:
                    norm_out(n_out, X, X, g_out)

            feed_forward(0, N_MIX0, N_OUT0, lambda m: col("out_g", m))
            for s_ in ("q1", "k1", "v1"):
                slots(s_, lambda s, p: None)

            for i in range(SB_HEADS + 2):
                flat = PS[:, 4 * (i % 2):4 * (i % 2) + 3, :].rearrange("p b t -> p (b t)")[:, 0:SBC]
                ex = EX[i % 2]
                if i < SB_HEADS:
                    for n, cc in enumerate(SB_PARTS):
                        dve.wait_ge(sz_exp, 2 * i + n + 1)
                        v.scalar_tensor_tensor(ex[:, cc], flat[:, cc], 0.0, ex[:, cc], ALU.max,
                                               ALU.add).then_inc(sp_ready, 1)
                    for n, cc in enumerate(SB_PARTS):
                        dve.wait_ge(sp_hi, 2 * i + n + 1)
                        v.tensor_tensor(EXL[i % 2][:, cc], ex[:, cc], EXH[i % 2][:, cc].bitcast(F32),
                                        ALU.subtract).then_inc(sp_lo, 1)
                if i >= 2:
                    h = i - 2
                    pb = (h % 2) * 64
                    dve.wait_ge(sb_pv, h + 1)
                    v.tensor_copy(QK[pb:pb + 64, h // 2, :], PS[pb:pb + 64, 4 * (h % 2) + 3, :]).then_inc(so_ready, 1)
            for m in range(KC):
                dve.wait_ge(so_hi, m + 1)
                v.tensor_tensor(YL[:, m, :], QK[:, m, :], YH[:, m, :].bitcast(F32), ALU.subtract).then_inc(so_lo, 1)
            own.did(v.memset(acc, 0.0))

            def wo(s, p):
                added("wo", first=ALPHA)(s, p)
                if s.first == 2:
                    split_ple_lo(1)
                else:
                    own.did(v.memset(STAT[:, 0, 0:1], 0.0))
            slots("wo", wo, per=3, head=COUNT["wo"])
            feed_forward(1, N_MIX1, N_OUT1, lambda m: col("out_g", KC + m))


def _unit(w, m, k0=0):
    blk = w[k0 * P:(k0 + KC) * P, m * P:(m + 1) * P]
    if blk.shape[0] < KC * P:
        blk = np.concatenate([blk, np.zeros((KC * P - blk.shape[0], P), w.dtype)])
    return blk.reshape(KC, P, P).transpose(1, 0, 2)


def _slots(i):
    w_in = i["w_in"]
    cut = lambda a, n: w_in[:, a:a + n]
    pairs = lambda a: [(_unit(a, 2 * j), _unit(a, 2 * j + 1)) for j in range(a.shape[1] // (2 * P))]
    both = lambda a, b: [(_unit(a, j), _unit(b, j)) for j in range(a.shape[1] // P)]
    down = lambda a: [(_unit(a, 2 * j, KC * s), _unit(a, 2 * j + 1, KC * s))
                      for j in range(KC // 2) for s in range(DOWN_S)]
    pw1 = i["a_pw1_w_2"][0]
    parts = [pairs(cut(XBC0, XBC)), pairs(cut(Q0, D)), pairs(cut(Z0, D)), pairs(cut(K0, D)),
             both(i["w_proj_ssm"], cut(G0, D)), pairs(cut(V0, D)), pairs(cut(ZA0, D)), both(i["w_proj_att"], cut(G0 + D, D)),
             pairs(i["w_out"]), both(pw1[:, 0:D], pw1[:, D:2 * D]), pairs(i["a_pw2_w_2"][0])]

    def ffn(layer):
        return [pairs(i["ple_w_gate_2"][layer]), both(i["ffn_w_up_2"][layer], i["ffn_w_gate_2"][layer]),
                down(i["ffn_w_down_2"][layer])]
    parts += ffn(0) + [pairs(i["b_wq_2"][0]), pairs(i["kv_wk_2"]), pairs(i["kv_wv_2"]), pairs(i["b_wo_2"][0])] + ffn(1)
    out = [np.stack(s, axis=1) for part in parts for s in part]
    return np.stack(out).reshape(NSLOTS, P, 2 * KC * P)


def _params(i):
    col = lambda a: np.asarray(a).reshape(-1, P).T
    rows = {
        "c": i["c"], "norm_w": i["norm_w"], "b_ada": i["b_ada"], "conv_w": i["conv_w"], "conv_b": i["conv_b"],
        "d_skip": np.repeat(i["d_skip"], SSM_P), "ssm_norm_w": i["ssm_norm_w"], "b_gate": i["b_gate"],
        "final_norm_w": i["final_norm_w"], "pw1_b": i["a_pw1_b_2"], "dw_w": i["a_dw_w_2"], "dw_b": i["a_dw_b_2"],
        "ln_g": i["a_ln_g_2"], "ln_b": i["a_ln_b_2"], "pw2_b": i["a_pw2_b_2"], "mix_g": i["ln_mix_g_2"],
        "mix_b": i["ln_mix_b_2"], "fconv_w": i["ffn_conv_w_2"], "fconv_b": i["ffn_conv_b_2"],
        "out_g": i["ln_ffn_g_2"], "out_b": i["ln_ffn_b_2"],
    }
    par = np.zeros((P, NPAR), np.float32)
    for name, a in rows.items():
        c = col(a)
        par[:, PCOL[name]:PCOL[name] + c.shape[1]] = c
    par[0:SSM_HEADS, PCOL["small_b"]] = i["dt_bias"]
    par[32:32 + FOX_HEADS, PCOL["small_b"]] = i["b_f"]
    par[0:SSM_HEADS, PCOL["a_log"]] = i["a_log"]
    return par


def kernel(**inputs):
    import concourse.bacc as bacc
    from concourse.bass_utils import run_bass_kernel_spmd

    i = {k: np.asarray(a) for k, a in inputs.items()}
    chunks = lambda a: a.reshape(-1, P, a.shape[-1]).transpose(1, 0, 2)
    w_small = np.zeros((D, SMALL), np.float32)
    w_small[:, 0:SSM_HEADS] = i["w_in"][:, DT0:DT0 + SSM_HEADS]
    w_small[:, 32:SMALL] = i["w_in"][:, FL0:FL0 + FOX_HEADS]
    arrays = {
        "w": _slots(i),
        "w_ada": i["w_ada"].reshape(KC, P, 3 * D),
        "w_small": chunks(w_small),
        "w_ple": np.stack([chunks(i["ple_w_proj_2"][n]) for n in range(2)]),
        "p_t": np.stack([chunks(i["p_2"][n, 0].T) for n in range(2)]),
        "x_t": chunks(i["x"][0].T),
        "par": _params(i),
    }
    arrays = {k: np.ascontiguousarray(a) for k, a in arrays.items()}
    nc = bacc.Bacc("TRN2", target_bir_lowering=False, num_devices=1)
    aps = [nc.dram_tensor(k, a.shape, F32, kind="ExternalInput").ap() for k, a in arrays.items()]
    out = nc.dram_tensor("out", (P, KC, T), F32, kind="ExternalOutput").ap()
    build(nc, *aps, out)
    r = run_bass_kernel_spmd(nc, [arrays], core_ids=[0])
    return np.asarray(r.results[0]["out"]).transpose(2, 1, 0).reshape(1, T, D)
```
